# Optimizing a Trainium2 kernel written in Bass

```python
import jax, jax.numpy as jnp
from jax import lax
import numpy as np

D_MODEL = 1024
BATCH = 1
SEQ = 1024
DEPTH = 2

CHUNK = 64
CONV_W = 4
EPS = 1e-6
F32 = jnp.float32

GDN_HEADS = 4
GDN_DK = 128
GDN_DV = 128
GDN_W = GDN_HEADS * GDN_DV
SSD_HEADS = 16
SSD_P = 64
SSD_N = 128
SSD_GROUPS = 2
SSD_W = SSD_HEADS * SSD_P
RET_HEADS = 4
RET_DK = 128
RET_DV = 128
RET_W = RET_HEADS * RET_DV
ROPE_BASE = 10000.0

MIX_W = GDN_W + SSD_W + RET_W

GDN_SIZES = [GDN_HEADS * GDN_DK, GDN_HEADS * GDN_DK, GDN_W, GDN_W, GDN_HEADS, GDN_HEADS]
SSD_SIZES = [SSD_W, SSD_GROUPS * SSD_N, SSD_GROUPS * SSD_N, SSD_W, SSD_HEADS]
RET_SIZES = [RET_HEADS * RET_DK, RET_HEADS * RET_DK, RET_W, RET_W]
IN_SIZES = GDN_SIZES + SSD_SIZES + RET_SIZES
N_IN = sum(IN_SIZES)
GDN_CONV_CH = 2 * GDN_HEADS * GDN_DK + GDN_W
SSD_CONV_CH = SSD_W + 2 * SSD_GROUPS * SSD_N

kernel_name = "hybrid_gdn_ssd_retention_parallel_groups"

def rmsnorm(x, w):
    xf = x.astype(F32)
    return xf * lax.rsqrt(jnp.mean(xf * xf, axis=-1, keepdims=True) + EPS) * w.astype(F32)

def split_cols(t, sizes):
    out, start = [], 0
    for s in sizes:
        out.append(t[..., start:start + s])
        start += s
    return out

def causal_conv(x, w):
    k = w.shape[0]
    seq = x.shape[1]
    xp = jnp.pad(x, ((0, 0), (k - 1, 0), (0, 0)))
    return sum(xp[:, i:i + seq] * w[i].astype(F32) for i in range(k))

def to_chunks(t):
    b, l = t.shape[:2]
    return jnp.moveaxis(t.reshape(b, l // CHUNK, CHUNK, *t.shape[2:]), 1, 0)

def from_chunks(t):
    n, b, c = t.shape[:3]
    return jnp.moveaxis(t, 0, 1).reshape(b, n * c, *t.shape[3:])

def l2norm(t):
    return t * lax.rsqrt(jnp.sum(t * t, axis=-1, keepdims=True) + EPS)

def rotary(t, pos):
    half = t.shape[-1] // 2
    inv = ROPE_BASE ** (-jnp.arange(half, dtype=F32) / half)
    ang = pos.astype(F32)[:, None] * inv[None, :]
    cos = jnp.cos(ang)[None, :, None, :]
    sin = jnp.sin(ang)[None, :, None, :]
    t1, t2 = t[..., :half], t[..., half:]
    return jnp.concatenate([t1 * cos - t2 * sin, t1 * sin + t2 * cos], axis=-1)

def gated_deltanet(q, k, v, b_raw, a_raw, A_log, dt_bias):
    bsz = q.shape[0]
    q = l2norm(q) * (GDN_DK ** -0.5)
    k = l2norm(k)
    beta = jax.nn.sigmoid(b_raw)
    g = -jnp.exp(A_log.astype(F32)) * jax.nn.softplus(a_raw + dt_bias.astype(F32))
    causal = jnp.tril(jnp.ones((CHUNK, CHUNK), bool))
    strict = jnp.tril(jnp.ones((CHUNK, CHUNK), F32), -1)
    eye = jnp.eye(CHUNK, dtype=F32)

    def step(S, inp):
        qi, ki, vi, bi, gi = inp
        gcum = jnp.cumsum(gi, axis=1)
        gh = jnp.swapaxes(gcum, 1, 2)
        diff = gh[..., :, None] - gh[..., None, :]
        decay = jnp.exp(jnp.where(causal, diff, -jnp.inf))
        kb = ki * bi[..., None]
        a_low = jnp.einsum('bihd,bjhd->bhij', kb, ki) * decay * strict
        rhs = jnp.concatenate([vi * bi[..., None], kb * jnp.exp(gcum)[..., None]], axis=-1)
        rhs = jnp.swapaxes(rhs, 1, 2)
        sol = lax.linalg.triangular_solve(a_low + eye, rhs, left_side=True, lower=True)
        u, w = sol[..., :GDN_DV], sol[..., GDN_DV:]
        v_new = u - jnp.einsum('bhcd,bhdv->bhcv', w, S)
        attn = jnp.einsum('bihd,bjhd->bhij', qi, ki) * decay
        o = (jnp.einsum('bihd,bhdv->bihv', qi * jnp.exp(gcum)[..., None], S)
             + jnp.einsum('bhij,bhjv->bihv', attn, v_new))
        glast = gcum[:, -1]
        kdec = ki * jnp.exp(glast[:, None, :] - gcum)[..., None]
        S = S * jnp.exp(glast)[:, :, None, None] + jnp.einsum('bjhd,bhjv->bhdv', kdec, v_new)
        return S, o

    s0 = jnp.zeros((bsz, GDN_HEADS, GDN_DK, GDN_DV), F32)
    _, o = lax.scan(step, s0, (to_chunks(q), to_chunks(k), to_chunks(v), to_chunks(beta), to_chunks(g)))
    return from_chunks(o)

def ssd(x, Bm, Cm, dt_raw, A_log, dt_bias, D):
    bsz, seq = x.shape[:2]
    hg = SSD_HEADS // SSD_GROUPS
    dt = jax.nn.softplus(dt_raw + dt_bias.astype(F32))
    a = (dt * -jnp.exp(A_log.astype(F32))).reshape(bsz, seq, SSD_GROUPS, hg)
    xdt = (x * dt[..., None]).reshape(bsz, seq, SSD_GROUPS, hg, SSD_P)
    causal = jnp.tril(jnp.ones((CHUNK, CHUNK), bool))

    def step(hs, inp):
        xi, bi, ci, ai = inp
        acum = jnp.cumsum(ai, axis=1)
        diff = acum[:, :, None] - acum[:, None]
        lmat = jnp.exp(jnp.where(causal[None, :, :, None, None], diff, -jnp.inf))
        cb = jnp.einsum('bign,bjgn->bijg', ci, bi)
        y = jnp.einsum('bijg,bijgh,bjghp->bighp', cb, lmat, xi)
        y = y + jnp.einsum('bign,bghpn->bighp', ci, hs) * jnp.exp(acum)[..., None]
        alast = acum[:, -1]
        wdec = jnp.exp(alast[:, None] - acum)
        hs = hs * jnp.exp(alast)[..., None, None] + jnp.einsum('bjgn,bjgh,bjghp->bghpn', bi, wdec, xi)
        return hs, y

    h0 = jnp.zeros((bsz, SSD_GROUPS, hg, SSD_P, SSD_N), F32)
    _, y = lax.scan(step, h0, (to_chunks(xdt), to_chunks(Bm), to_chunks(Cm), to_chunks(a)))
    y = from_chunks(y).reshape(bsz, seq, SSD_HEADS, SSD_P)
    return y + x * D.astype(F32)[:, None]

def retention(q, k, v):
    bsz = q.shape[0]
    lg = jnp.log(1.0 - 2.0 ** (-5.0 - jnp.arange(RET_HEADS, dtype=F32)))
    idx = jnp.arange(CHUNK, dtype=F32)
    rel = idx[:, None] - idx[None, :]
    dmat = jnp.where(rel[None] >= 0, jnp.exp(jnp.maximum(rel, 0.0)[None] * lg[:, None, None]), 0.0)
    qdec = jnp.exp((idx[:, None] + 1.0) * lg[None, :])
    kdec = jnp.exp((CHUNK - 1.0 - idx)[:, None] * lg[None, :])
    cdec = jnp.exp(CHUNK * lg)
    k = k * (RET_DK ** -0.5)

    def step(R, inp):
        qi, ki, vi = inp
        s = jnp.einsum('bihd,bjhd->bhij', qi, ki) * dmat
        o = (jnp.einsum('bhij,bjhv->bihv', s, vi)
             + jnp.einsum('bihd,bhdv->bihv', qi, R) * qdec[None, :, :, None])
        R = R * cdec[None, :, None, None] + jnp.einsum('bjhd,bjhv->bhdv', ki * kdec[None, :, :, None], vi)
        return R, o

    r0 = jnp.zeros((bsz, RET_HEADS, RET_DK, RET_DV), F32)
    _, o = lax.scan(step, r0, (to_chunks(q), to_chunks(k), to_chunks(v)))
    return from_chunks(o)

def hybrid_layer(x, pre_norm, post_norm, w_in, gdn_conv, gdn_A_log, gdn_dt_bias, gdn_norm,
                 ssd_conv, ssd_conv_b, ssd_A_log, ssd_dt_bias, ssd_D, ssd_norm, ret_norm, w_out, pos):
    bsz, seq, _ = x.shape
    h = rmsnorm(x, pre_norm)
    proj = jnp.einsum('bld,de->ble', h, w_in.astype(F32))
    (gq, gk, gv, gz, gb, ga, sx, sB, sC, sz, sdt, rq, rk, rv, rg) = split_cols(proj, IN_SIZES)

    qkv = jax.nn.silu(causal_conv(jnp.concatenate([gq, gk, gv], axis=-1), gdn_conv))
    gq, gk, gv = split_cols(qkv, [GDN_HEADS * GDN_DK, GDN_HEADS * GDN_DK, GDN_W])
    o_a = gated_deltanet(gq.reshape(bsz, seq, GDN_HEADS, GDN_DK), gk.reshape(bsz, seq, GDN_HEADS, GDN_DK),
                         gv.reshape(bsz, seq, GDN_HEADS, GDN_DV), gb, ga, gdn_A_log, gdn_dt_bias)
    o_a = rmsnorm(o_a, gdn_norm) * jax.nn.silu(gz.reshape(bsz, seq, GDN_HEADS, GDN_DV))

    xbc = jax.nn.silu(causal_conv(jnp.concatenate([sx, sB, sC], axis=-1), ssd_conv) + ssd_conv_b.astype(F32))
    sx, sB, sC = split_cols(xbc, [SSD_W, SSD_GROUPS * SSD_N, SSD_GROUPS * SSD_N])
    y_b = ssd(sx.reshape(bsz, seq, SSD_HEADS, SSD_P), sB.reshape(bsz, seq, SSD_GROUPS, SSD_N),
              sC.reshape(bsz, seq, SSD_GROUPS, SSD_N), sdt, ssd_A_log, ssd_dt_bias, ssd_D)
    y_b = y_b * jax.nn.silu(sz.reshape(bsz, seq, SSD_HEADS, SSD_P))
    o_b = rmsnorm(y_b.reshape(bsz, seq, SSD_GROUPS, SSD_W // SSD_GROUPS),
                  ssd_norm.reshape(SSD_GROUPS, SSD_W // SSD_GROUPS))

    q_c = rotary(rq.reshape(bsz, seq, RET_HEADS, RET_DK), pos)
    k_c = rotary(rk.reshape(bsz, seq, RET_HEADS, RET_DK), pos)
    o_c = retention(q_c, k_c, rv.reshape(bsz, seq, RET_HEADS, RET_DV))
    o_c = rmsnorm(o_c, ret_norm) * jax.nn.silu(rg.reshape(bsz, seq, RET_HEADS, RET_DV))

    mixed = jnp.concatenate([o_a.reshape(bsz, seq, GDN_W), o_b.reshape(bsz, seq, SSD_W),
                             o_c.reshape(bsz, seq, RET_W)], axis=-1)
    out = jnp.einsum('ble,ed->bld', mixed, w_out.astype(F32))
    return x + rmsnorm(out, post_norm).astype(x.dtype)

def setup_inputs(seed: int = 0) -> dict:
    key = jax.random.key(seed)
    ks = jax.random.split(key, 16)
    nrm = jax.random.normal

    def inv_softplus_dt(k, shape):
        dt = jnp.exp(jax.random.uniform(k, shape, F32, np.log(1e-3), np.log(1e-1)))
        return dt + jnp.log(-jnp.expm1(-dt))

    return {
        "x": nrm(ks[0], (BATCH, SEQ, D_MODEL), F32),
        "pre_norm": 1.0 + 0.05 * nrm(ks[1], (DEPTH, D_MODEL), F32),
        "post_norm": 1.0 + 0.05 * nrm(ks[2], (DEPTH, D_MODEL), F32),
        "w_in": nrm(ks[3], (DEPTH, D_MODEL, N_IN), F32) * D_MODEL ** -0.5,
        "gdn_conv": nrm(ks[4], (DEPTH, CONV_W, GDN_CONV_CH), F32) * CONV_W ** -0.5,
        "gdn_A_log": jnp.log(jax.random.uniform(ks[5], (DEPTH, GDN_HEADS), F32, 1.0, 16.0)),
        "gdn_dt_bias": inv_softplus_dt(ks[6], (DEPTH, GDN_HEADS)),
        "gdn_norm": 1.0 + 0.05 * nrm(ks[7], (DEPTH, GDN_DV), F32),
        "ssd_conv": nrm(ks[8], (DEPTH, CONV_W, SSD_CONV_CH), F32) * CONV_W ** -0.5,
        "ssd_conv_b": 0.02 * nrm(ks[9], (DEPTH, SSD_CONV_CH), F32),
        "ssd_A_log": jnp.log(jax.random.uniform(ks[10], (DEPTH, SSD_HEADS), F32, 1.0, 16.0)),
        "ssd_dt_bias": inv_softplus_dt(ks[11], (DEPTH, SSD_HEADS)),
        "ssd_D": 1.0 + 0.1 * nrm(ks[12], (DEPTH, SSD_HEADS), F32),
        "ssd_norm": 1.0 + 0.05 * nrm(ks[13], (DEPTH, SSD_W), F32),
        "ret_norm": 1.0 + 0.05 * nrm(ks[14], (DEPTH, RET_DV), F32),
        "w_out": nrm(ks[15], (DEPTH, MIX_W, D_MODEL), F32) * MIX_W ** -0.5,
    }

def reference(x, pre_norm, post_norm, w_in, gdn_conv, gdn_A_log, gdn_dt_bias, gdn_norm,
              ssd_conv, ssd_conv_b, ssd_A_log, ssd_dt_bias, ssd_D, ssd_norm, ret_norm, w_out):
    pos = jnp.arange(x.shape[1], dtype=jnp.int32)
    for l in range(DEPTH):
        x = hybrid_layer(x, pre_norm[l], post_norm[l], w_in[l], gdn_conv[l], gdn_A_log[l], gdn_dt_bias[l],
                         gdn_norm[l], ssd_conv[l], ssd_conv_b[l], ssd_A_log[l], ssd_dt_bias[l], ssd_D[l],
                         ssd_norm[l], ret_norm[l], w_out[l], pos)
    return x


_drawn_inputs = setup_inputs


def setup_inputs(seed=0):
    import zlib

    import numpy as np

    out = dict(_drawn_inputs(seed))
    spreads = {}
    factors = {'gdn_norm': 2.947, 'ret_norm': 3.054, 'ssd_conv_b': 3.076}
    for name, (base, spread) in spreads.items():
        noise = np.random.default_rng([zlib.crc32(name.encode()), seed]).standard_normal(out[name].shape)
        drawn = base * np.exp(spread * noise) if base else spread * noise
        out[name] = __import__('jax').numpy.asarray(drawn.astype(out[name].dtype))
    for name, factor in factors.items():
        out[name] = (out[name] * factor).astype(out[name].dtype)
    return out
```

```python
from contextlib import ExitStack

import numpy as np

import concourse.bass as bass
from concourse import mybir

ALU = mybir.AluOpType
ACT = mybir.ActivationFunctionType
F32 = mybir.dt.float32

P = 128
D, SEQ, DEPTH = 1024, 1024, 2
HALF = 512
NT = HALF // P
KD = D // P
PARTS = DEPTH * SEQ // HALF
EPS = 1e-6
GH, SH, RH = 4, 16, 4
SG, SP = 2, 64
HG = SH // SG
DK = 128
NDEC = GH + SH
NSM = GH + NDEC
LEVELS = 7
TAPS = 4
GROUPS = 4

PC = 256
N_GDN_PC, N_GZ, N_BC, N_SZ, N_SX, N_RET = 6, 2, 2, 2, 2, 8
PIECES = ([("gz", i) for i in range(N_GZ)] + [("gdn", i) for i in range(N_GDN_PC)] + [("bc", i) for i in range(N_BC)]
          + [(k, g, i) for g in range(SG) for k, n in (("sz", N_SZ), ("sx", N_SX)) for i in range(n)]
          + [("ret", i) for i in range(N_RET)])
AT = {piece: i for i, piece in enumerate(PIECES)}
W_RING = 3
SLOTS = 2
MIX_BANKS = (2, 3, 4, 5, 6)
LAM = [1.0 - 2.0 ** (-5.0 - h) for h in range(RH)]

C_ID, C_UP, C_LOW, C_ONE, C_LEV = 0, 128, 256, 384, 512
C_DM = C_LEV + LEVELS * 128
C_QD = C_DM + RH * 128
C_KD = C_QD + RH * 128
C_PW = C_KD + RH
C_ZERO = C_PW + 8
C_END = C_ZERO + 4
ROPE = NT * (DK // 2 + DK)

Q_CONV, Q_BIAS, Q_PRE, Q_MIX = 0, 96, 108, 116
Q_END = Q_MIX + 16
R_A, R_DT, R_D, R_END = 0, NDEC, 2 * NDEC, 2 * NDEC + SH


def constants():
    c = np.zeros((P, C_END), np.float32)
    r = np.arange(P)
    c[:, C_ID:C_ID + P] = np.eye(P)
    c[:, C_UP:C_UP + P] = r[:, None] <= r[None, :]
    c[:, C_LOW:C_LOW + P] = r[:, None] > r[None, :]
    c[:, C_ONE:C_ONE + P] = 1.0
    for k in range(LEVELS):
        b = 1 << k
        same = (r[:, None] // (2 * b)) == (r[None, :] // (2 * b))
        c[:, C_LEV + k * P:C_LEV + (k + 1) * P] = same & (r[:, None] // b % 2 == 0) & (r[None, :] // b % 2 == 1)
    for h, lam in enumerate(LAM):
        rel = (r[None, :] - r[:, None]).astype(np.float64)
        c[:, C_DM + h * P:C_DM + (h + 1) * P] = np.where(rel >= 0, lam ** np.maximum(rel, 0), 0.0) * DK ** -0.5
        c[:, C_QD + h * P:C_QD + (h + 1) * P] = (lam ** (r + 1.0))[None, :]
        c[:, C_KD + h] = lam ** (P - 1.0 - r) * DK ** -0.5
    c[:, C_PW:C_PW + 8] = -0.5
    half = DK // 2
    inv = (np.float32(10000.0) ** (-np.arange(half, dtype=np.float32) / half)).astype(np.float32)
    ang = (np.arange(SEQ, dtype=np.float32)[:, None] * inv[None, :]).astype(np.float32).astype(np.float64)
    ang = ang.reshape(SEQ // P, P, half).transpose(1, 0, 2)
    rope = np.zeros((SEQ // HALF, P, ROPE), np.float32)
    for i in range(SEQ // HALF):
        a = ang[:, i * NT:(i + 1) * NT]
        rope[i, :, :NT * half] = np.cos(a).reshape(P, -1)
        rope[i, :, NT * half:] = np.concatenate([-np.sin(a), np.sin(a)], axis=-1).reshape(P, -1)
    return c, rope


def mixing_steps(p):
    out = [("gdn_decay", p, h) for h in range(GH)]
    for h in range(GH):
        out += [("gdn_turn", p, h), ("gdn_back", p, h), ("gdn_gram", p, h), ("gdn_x0", p, h)]
        for k in range(1, LEVELS):
            out += [("gdn_p", p, h, k), ("gdn_xx", p, h, k)]
        out.append(("gdn_w", p, h))
        for c in range(NT):
            out += [("gdn_v", p, h, c), ("gdn_o", p, h, c)]
        out.append(("gdn_fin", p, h))
    out.append(("mix_turn", p, 0))
    out.append(("bc_turn", p))
    for g in range(SG):
        out.append(("x_turn", p, g))
        for c in range(NT):
            out += [("ssd_l", p, g, c), ("ssd_y", p, g, c)]
        out.append(("mix_turn", p, 1 + g))
    for h in range(RH):
        out += [("ret_turn", p, h), ("ret_s", p, h)] + [("ret_o", p, h, c) for c in range(NT)] + [("ret_fin", p, h)]
    out.append(("mix_turn", p, 3))
    return out


def make_plan():
    mix = [s for p in range(PARTS) for s in mixing_steps(p)]
    plan, done, at = [], set(), [0]
    outs = []

    def emit(s):
        plan.append(s)
        done.add(s)

    def ready(s):
        kind, p = s[0], s[1]
        need = {"gdn_turn": lambda: ("proj", p, AT["gdn", (3 * s[2] + 2) // 2], (3 * s[2] + 2) % 2, 3),
                "gdn_decay": lambda: ("small2", p), "gdn_fin": lambda: ("proj", p, AT["gz", N_GZ - 1], 1, 3),
                "bc_turn": lambda: ("proj", p, AT["bc", N_BC - 1], 1, 3),
                "x_turn": lambda: ("proj", p, AT["sx", s[2], N_SX - 1], 1, 3),
                "ret_turn": lambda: ("proj", p, AT["ret", 2 * s[2] + 1], 1, 3)}.get(kind)
        return need is None or need() in done

    def mix_one(between=True):
        s = mix[at[0]]
        if not ready(s):
            return False
        if s[0] == "mix_turn" and outs:
            if not between:
                return False
            flush_outs(len(outs))
        at[0] += 1
        emit(s)
        if s[0] == "mix_turn":
            outs.extend(("out", s[1], s[2], n, t) for n in range(2) for t in range(NT))
            if s[2] == GROUPS - 1:
                outs.extend(("final", s[1], t) for t in range(NT))
        return True

    def mix_until(s):
        while s not in done:
            assert mix_one(), (s, mix[at[0]])

    def flush_outs(n):
        while outs and n:
            emit(outs.pop(0))
            n -= 1

    for p in range(PARTS):
        if p >= 2:
            while ("final", p - 2, NT - 1) not in done:
                mix_until(("mix_turn", p - 2, 3))
                flush_outs(99)
        for t in range(NT):
            emit(("norm", p, t))
        emit(("small", p))
        emit(("small2", p))
        for i, piece in enumerate(PIECES):
            for half in range(2):
                for s in frees(p, i, half):
                    mix_until(s)
                flush_outs(2)
                for q in range(4):
                    emit(("proj", p, i, half, q))
                    mix_one(q == 3)
    while at[0] < len(mix):
        assert mix_one()
        flush_outs(2)
    flush_outs(99)
    return plan


def slot_of(p, i, half):
    kind = PIECES[i][0]
    if kind == "gdn":
        return 10 * p + (2 * PIECES[i][1] + half) // 3
    if kind == "sx":
        return 10 * p + 4 + PIECES[i][1]
    if kind == "ret":
        return 10 * p + 6 + PIECES[i][1] // 2
    return None


def slot_reader(n):
    p, j = divmod(n, 10)
    if j < 4:
        return ("gdn_turn", p, j)
    if j < 6:
        return ("x_turn", p, j - 4)
    return ("ret_o", p, j - 6, NT - 1)


def gate_of(p, i):
    kind = PIECES[i][0]
    return {"gz": 4 * p, "sz": 4 * p + 1 + (PIECES[i][1] if kind == "sz" else 0), "ret": 4 * p + 3}.get(kind)


def frees(p, i, half):
    need = []
    n = slot_of(p, i, half)
    if n is not None and n >= SLOTS:
        need.append(slot_reader(n - SLOTS))
    g = gate_of(p, i)
    if g is not None and g >= 2:
        need.append(("mix_turn", (g - 2) // 4, (g - 2) % 4))
    if PIECES[i][0] == "bc" and p:
        need.append(("ssd_y", p - 1, SG - 1, NT - 1))
    return need


def bank_uses(step):
    k = step[0]
    if k == "norm":
        return [("mix", (*step, j)) for j in range(2)]
    if k in ("small", "small2", "gdn_decay", "gdn_x0", "gdn_p", "gdn_w", "gdn_v"):
        return [("mix", step)]
    if k == "proj":
        return [("proj", step[:4])] if step[4] == 0 else []
    if k == "out":
        return [("proj", step)]
    if k == "gdn_turn":
        return [("mix", (*step, j)) for j in "qkv"]
    if k == "gdn_back":
        return [("mix", (*step, j)) for j in range(4)]
    if k == "gdn_gram":
        return [("mix", (*step, j)) for j in range(2)]
    if k == "gdn_xx":
        return [("mix", (*step, j)) for j in range(2 if step[3] < LEVELS - 1 else 1)]
    if k == "gdn_o":
        return ([("o", ("gdn_oo", *step[1:3]))] if step[3] == 0 else []) + [("mix", step)]
    if k == "mix_turn":
        return [("mix", (*step, t)) for t in range(NT)]
    if k == "bc_turn":
        return [("mix", (*step, j, g)) for g in range(SG) for j in range(2)]
    if k == "x_turn":
        return [("mix", (*step, c)) for c in range(NT)]
    if k == "ssd_l":
        return [("mix", (*step, j)) for j in range(2)]
    if k == "ssd_y":
        return [("mix", (*step, j)) for j in "yzw"]
    if k == "ret_turn":
        return [("mix", (*step, j)) for j in "qk"]
    if k == "ret_s":
        return [("mix", step)]
    if k == "ret_o":
        return ([("o", ("ret_oo", *step[1:3]))] if step[3] == 0 else []) + [("mix", step)]
    return []


def hybrid_kernel(nc, x, w_in, w_small, w_out, cons, rope, pars, rows, post_norm, out):
    plan = make_plan()
    pools = {"proj": (0, 1), "mix": MIX_BANKS, "o": (7,)}
    counts, bank_of, use_of = {k: 0 for k in pools}, {}, {}
    for s in plan:
        for pool, tag in bank_uses(s):
            banks = pools[pool]
            bank_of[tag] = banks[counts[pool] % len(banks)]
            use_of[tag] = counts[pool] // len(banks)
            counts[pool] += 1

    x1 = nc.dram_tensor("x_mid", (SEQ, D), F32, kind="Internal").ap()

    with ExitStack() as ctx:
        def sb(name, *shape):
            return ctx.enter_context(nc.sbuf_tensor(name, [P, *shape], F32))

        def sem(name):
            return ctx.enter_context(nc.semaphore(name))

        ps = ctx.enter_context(nc.psum_tensor("ps", [P, 8, 512], F32))
        con = sb("con", C_END)
        par = sb("par", DEPTH, Q_END)
        row = sb("row", DEPTH, R_END)
        nega = sb("nega", DEPTH, NDEC)
        xin = sb("xin", 2, D)
        post = sb("post", D)
        rp = sb("rp", ROPE)
        hT = sb("hT", KD, HALF)
        wr = sb("wr", W_RING, KD, PC)
        wsm = sb("wsm", KD, NSM)
        raw = sb("raw", 2, 3 + HALF)
        cv = sb("cv", 2, HALF)
        halo = sb("halo", 24, 3)
        slot = sb("slot", SLOTS, 4 * HALF)
        bc = sb("bc", 4, HALF)
        gate = sb("gate", 2, NT, 512)
        mixT = sb("mixT", 4, HALF)
        acc = sb("acc", NT, D)
        st_g = sb("st_g", GH, P)
        st_s = sb("st_s", SG, 512)
        st_r = sb("st_r", RH, P)
        small = sb("small", 2, NT, NSM)
        beta = sb("beta", 2, NT, GH)
        dt = sb("dt", 2, NT, NDEC)
        dg = sb("dg", 2, NT, NDEC)
        dec = sb("dec", 2, 3, NT, NDEC)
        sm_t = sb("sm_t", 6, NT * NDEC)
        ss = sb("ss", 16)
        rs = sb("rs", 16)
        sc = sb("sc", 6, NT)
        gss = sb("gss", 8)
        xss = sb("xss", 4)
        xrs, ssr, frs = sb("xrs", 2), sb("ssr", 2), sb("frs", 2)
        xf = sb("xf", 2, D)
        xfin, xsq2 = xf[:, 0, :], xf[:, 1, :]
        wk = sb("wk", 12, NT, P)
        et = sb("et", GH, NT, P)
        vnew = sb("vnew", 2, P)
        junk = sb("junk", 2, 512)
        kh, kb, qh, qe, kbe, kdc, vb, kT, kbT, qT, qeT = (wk[:, i] for i in range(11))
        X, XT, PP, wT, bT0, bT1, aT, att = kh, kb, qh, qh, qe, kT, kbT, qT
        flat = wk[:, :, :, :].rearrange("p a c n -> p (a c n)")
        bt = flat[:, 0:1024].rearrange("p (g c n) -> p g c n", g=SG, c=NT)
        gT = flat[:, 1024:2048].rearrange("p (g c n) -> p g c n", g=SG, c=NT)
        xt = flat[:, 2048:4096].rearrange("p (c n) -> p c n", c=NT)
        aU = flat[:, 4096:5120]
        LG = flat[:, 5120:6144]
        xdt, xw, xD, yy = (et[:, i].rearrange("p c n -> p (c n)") for i in range(4))
        rqT, rkT, rqd, rS, rkd, rtmp = (flat[:, i * 512:(i + 1) * 512].rearrange("p (c n) -> p c n", c=NT) for i in range(6))
        rot = sb("rot", 2, 512)

        filled = [sem(f"filled{b}") for b in range(8)]
        emptied = [sem(f"emptied{b}") for b in range(8)]
        loaded = sem("consts_loaded")
        w_in_sem = [sem(f"piece_loaded{i}") for i in range(W_RING)]
        w_used = sem("piece_used")
        wsm_in = sem("small_loaded")
        x_in = [sem(f"x_loaded{i}") for i in range(2)]
        xf_in = [sem(f"xf_loaded{i}") for i in range(2)]
        x_stored = sem("x_stored")
        rope_in, post_in = sem("rope_loaded"), sem("post_loaded")
        act_step, dve_step, pool_step = sem("act_step"), sem("dve_step"), sem("pool_step")
        names = ["nega_ready", "x_squares", "x_mean", "x_rstd", "x_normed", "sm_abs", "sm_exp", "sm_beta_exp", "sm_decays",
                 "conv_done", "silu_done", "gdn_squares", "gdn_sums", "gdn_rstd", "gdn_gu", "gdn_masks", "gdn_xt", "gdn_attn",
                 "gdn_used", "o_squares", "o_mean", "o_rstd", "o_mixed", "ssd_au", "ssd_lg", "ssd_xdt", "ssd_xw", "ssd_xd",
                 "ssd_state", "ssd_ygated", "ssd_squares", "ssd_mean", "ssd_rstd", "ssd_mixed", "ret_rot", "ret_sum", "ret_kd",
                 "gdn_state", "ret_state", "f_squares", "f_mean", "f_rstd", "f_scaled", "f_done", "mix_read", "gdn_done",
                 "states_clear", "bt_free"]
        S = {n: sem(n) for n in names}

        ident = con[:, C_ID:C_ID + P]
        upper = con[:, C_UP:C_UP + P]
        lower = con[:, C_LOW:C_LOW + P]
        ones = con[:, C_ONE:C_ONE + P]
        pw = con[:, C_PW:C_PW + 8]

        def bank(tag):
            return ps[:, bank_of[tag], :]

        def bank4(tag, n=NT):
            return bank(tag).rearrange("p (c n) -> p c n", c=n)

        def wait_filled(eng, tag):
            eng.wait_ge(filled[bank_of[tag]], use_of[tag] + 1)

        def wait_emptied(eng, tag):
            eng.wait_ge(emptied[bank_of[tag]], use_of[tag] + 1)

        def empty(ins, tag):
            ins.then_inc(emptied[bank_of[tag]], 1)

        def over_rows(a, n=NT):
            return a.unsqueeze(1).broadcast_to([P, n, a.shape[1]])

        def over_cols(a, m=P):
            return a.unsqueeze(2).broadcast_to([P, a.shape[1], m])

        def slot_view(n, h):
            return slot[:, n % SLOTS, :]

        def mtile(p, i, half):
            kind = PIECES[i][0]
            if kind == "gdn":
                m = 2 * PIECES[i][1] + half
                n = slot_of(p, i, half)
                return 24 * p + m, m, slot[:, n % SLOTS, (m % 3) * HALF:(m % 3 + 1) * HALF]
            if kind == "bc":
                j = 2 * PIECES[i][1] + half
                return 24 * p + 12 + j, 12 + j, bc[:, j, :]
            if kind == "sx":
                g, j = PIECES[i][1], 2 * PIECES[i][2] + half
                n = slot_of(p, i, half)
                return 24 * p + 16 + 4 * g + j, 16 + 4 * g + j, slot[:, n % SLOTS, j * HALF:(j + 1) * HALF]
            return None

        def piece_no(p, j):
            return order[("in", p, j)] if not isinstance(j, tuple) else order[("out", p, *j)]

        order, uses = {}, []
        for s in plan:
            if s[0] == "proj" and s[3] == 0 and s[4] == 0:
                order[("in", s[1], s[2])] = len(uses)
                uses.append(("in", s[1], s[2]))
            if s[0] == "out" and s[4] == 0:
                order[("out", s[1], s[2], s[3])] = len(uses)
                uses.append(("out", s[1], s[2], s[3]))
        finish, fin = {}, 0
        for s in plan:
            if s[0] == "proj" and s[3] == 1 and s[4] == 3:
                fin += 1
                finish[("in", s[1], s[2])] = fin
            if s[0] == "out" and s[4] == NT - 1:
                fin += 1
                finish[("out", s[1], s[2], s[3])] = fin
        block = ctx.enter_context(nc.Block())

        def ssd_before(s):
            m = NT * (SG * s[1] + s[2]) + s[3] - 1
            return ("ssd_y", m // (NT * SG), m // NT % SG, m % NT)

        def slot_wait(eng, n):
            if n < SLOTS:
                return
            r = slot_reader(n - SLOTS)
            if r[0] == "gdn_turn":
                wait_filled(eng, (*r, "v"))
            elif r[0] == "x_turn":
                wait_filled(eng, (*r, NT - 1))
            else:
                wait_filled(eng, r)

        def gate_wait(eng, G):
            if G >= 2:
                wait_filled(eng, ("mix_turn", (G - 2) // 4, (G - 2) % 4, NT - 1))

        def x_rows(p, t):
            r = (p % 2) * HALF + t * P
            return (x if p < 2 else x1)[r:r + P, :]

        @block.sync
        def _(sp):
            sp.dma_start(con[:], cons).then_inc(loaded, 16)
            for l in range(DEPTH):
                sp.dma_start(par[:, l, :], pars[l]).then_inc(loaded, 16)
                sp.dma_start(row[:, l, :], rows[l].partition_broadcast(P)).then_inc(loaded, 16)
            for s in plan:
                k, p = s[0], s[1]
                if k == "norm":
                    n = NT * p + s[2]
                    if n >= 2:
                        wait_filled(sp, ("norm", (n - 2) // NT, (n - 2) % NT, 1))
                    if p >= 2:
                        sp.wait_ge(x_stored, 16 * (NT * (p - 2) + s[2] + 1))
                    sp.dma_start(xin[:, n % 2, :], x_rows(p, s[2])).then_inc(x_in[n % 2], 16)
                    if s[2] == 0:
                        if p:
                            wait_filled(sp, ("small", p - 1))
                        sp.dma_start(wsm[:], w_small[p // 2]).then_inc(wsm_in, 16)
                key = None
                if k == "proj" and s[3] == 0 and s[4] == 0:
                    key, src = ("in", p, s[2]), w_in[p // 2, s[2]]
                if k == "out" and s[4] == 0:
                    key, src = ("out", p, s[2], s[3]), w_out[p // 2, s[2], s[3]]
                if key:
                    n = order[key]
                    if n >= W_RING:
                        sp.wait_ge(w_used, finish[uses[n - W_RING]])
                    sp.dma_start(wr[:, n % W_RING, :, :].rearrange("p k n -> p (k n)"), src).then_inc(w_in_sem[n % W_RING], 16)

        def loaded_piece(eng, n):
            eng.wait_ge(w_in_sem[n % W_RING], 16 * (n // W_RING + 1))

        @block.tensor
        def _(pe):
            last_use = {}

            def opened(tag):
                if use_of[tag]:
                    pe.wait_ge(emptied[bank_of[tag]], use_of[tag])
                return bank(tag)

            def close(ins, tag):
                ins.then_inc(filled[bank_of[tag]], 1)

            def mm(o, a, b, start=True, stop=True):
                return nc.tensor.matmul(o, a, b, start=start, stop=stop)

            def turn(o, a):
                return nc.tensor.transpose(o, a, ident)

            pe.wait_ge(loaded, 16 * (1 + 2 * DEPTH))
            for s in plan:
                k, p = s[0], s[1]
                if k == "norm":
                    t = s[2]
                    pe.wait_ge(S["x_normed"], NT * p + t + 1)
                    for j in range(2):
                        tag = (*s, j)
                        b = opened(tag)
                        for c in range(4):
                            i = turn(b[:, c * P:(c + 1) * P], xin[:, (NT * p + t) % 2, (4 * j + c) * P:(4 * j + c + 1) * P])
                        close(i, tag)
                elif k == "small":
                    pe.wait_ge(wsm_in, 16 * (p + 1))
                    wait_emptied(pe, ("norm", p, NT - 1, 1))
                    b = opened(s)
                    for t in range(NT):
                        for kk in range(KD):
                            i = mm(b[:, t * NSM:(t + 1) * NSM], hT[:, kk, t * P:(t + 1) * P], wsm[:, kk, :], kk == 0, kk == KD - 1)
                    close(i, s)
                elif k == "small2":
                    pe.wait_ge(S["sm_decays"], p + 1)
                    b = opened(s)
                    n = NT * NDEC
                    for j, m in enumerate((upper, lower, ones)):
                        i = mm(b[:, j * n:(j + 1) * n], m, dg[:, p % 2].rearrange("p t n -> p (t n)"))
                    close(i, s)
                elif k == "proj":
                    i_, half, q = s[2], s[3], s[4]
                    n = order[("in", p, i_)]
                    w = wr[:, n % W_RING]
                    tag = s[:4]
                    if q == 0:
                        opened(tag)
                        loaded_piece(pe, n)
                    b = bank(tag)
                    if PIECES[i_][0] in ("gdn", "bc", "sx"):
                        for kk in (2 * q, 2 * q + 1):
                            i = mm(b, w[:, kk, half * P:(half + 1) * P], hT[:, kk, :], kk == 0, kk == KD - 1)
                    else:
                        t, k0 = 2 * half + q // 2, 4 * (q % 2)
                        for kk in range(k0, k0 + 4):
                            i = mm(b[:, (q // 2) * PC:(q // 2 + 1) * PC], hT[:, kk, t * P:(t + 1) * P], w[:, kk, :],
                                   kk == 0, kk == KD - 1)
                    if q == 3:
                        close(i, tag)
                        if half == 1:
                            pe.wait_ge(filled[bank_of[tag]], use_of[tag] + 1)
                            pe.sem_inc(w_used, 1)
                elif k == "out":
                    G, nh, t = s[2:]
                    n = order[("out", p, G, nh)]
                    w = wr[:, n % W_RING].rearrange("p k n -> p (k n)").rearrange("p (k n) -> p k n", k=4)
                    b = opened(s)
                    if t == 0:
                        loaded_piece(pe, n)
                    wait_emptied(pe, ("mix_turn", p, G, t))
                    for kk in range(4):
                        i = mm(b, mixT[:, kk, t * P:(t + 1) * P], w[:, kk, :], kk == 0, kk == 3)
                    close(i, s)
                    if t == NT - 1:
                        pe.wait_ge(filled[bank_of[s]], use_of[s] + 1)
                        pe.sem_inc(w_used, 1)
                elif k == "gdn_decay":
                    h = s[2]
                    pe.wait_ge(S["gdn_gu"], GH * p + h + 1)
                    b = opened(s)
                    close(mm(b, lower, rot[:, h % 2, :]), s)
                elif k == "gdn_turn":
                    h = s[2]
                    n = 10 * p + h
                    pe.wait_ge(S["silu_done"], 24 * p + 3 * h + 3)
                    for j, name in enumerate("qkv"):
                        tag = (*s, name)
                        b = opened(tag)
                        for c in range(NT):
                            i = turn(b[:, c * P:(c + 1) * P], slot[:, n % SLOTS, j * HALF + c * P:j * HALF + (c + 1) * P])
                        close(i, tag)
                elif k == "gdn_back":
                    h = s[2]
                    wait_emptied(pe, ("gdn_turn", p, h, "k"))
                    for j, src in enumerate((kh, kb, qh, qe)):
                        if j == 2:
                            wait_emptied(pe, ("gdn_turn", p, h, "q"))
                        tag = (*s, j)
                        b = opened(tag)
                        for c in range(NT):
                            i = turn(b[:, c * P:(c + 1) * P], src[:, c, :])
                        close(i, tag)
                elif k == "gdn_gram":
                    h = s[2]
                    for j, src in enumerate((kbT, qT)):
                        wait_emptied(pe, ("gdn_back", p, h, j + 1))
                        tag = (*s, j)
                        b = opened(tag)
                        for c in range(NT):
                            i = mm(b[:, c * P:(c + 1) * P], kT[:, c, :], src[:, c, :])
                        close(i, tag)
                elif k == "gdn_x0":
                    h = s[2]
                    pe.wait_ge(S["gdn_xt"], GH * p + h + 1)
                    b = opened(s)
                    for c in range(NT):
                        i = turn(b[:, c * P:(c + 1) * P], XT[:, c, :])
                    close(i, s)
                elif k == "gdn_p":
                    h, lv = s[2], s[3]
                    wait_emptied(pe, ("gdn_x0", p, h) if lv == 1 else ("gdn_xx", p, h, lv - 1, 1))
                    pe.wait_ge(S["gdn_masks"], LEVELS * (GH * p + h) + lv + 1)
                    b = opened(s)
                    for c in range(NT):
                        i = mm(b[:, c * P:(c + 1) * P], (bT0, bT1)[lv % 2][:, c, :], X[:, c, :])
                    close(i, s)
                elif k == "gdn_xx":
                    h, lv = s[2], s[3]
                    wait_emptied(pe, ("gdn_p", p, h, lv))
                    if lv < LEVELS - 1:
                        tag = (*s, 0)
                        b = opened(tag)
                        for c in range(NT):
                            i = mm(b[:, c * P:(c + 1) * P], XT[:, c, :], PP[:, c, :])
                        close(i, tag)
                    tag = (*s, 1 if lv < LEVELS - 1 else 0)
                    b = opened(tag)
                    for c in range(NT):
                        i = mm(b[:, c * P:(c + 1) * P], PP[:, c, :], XT[:, c, :])
                    close(i, tag)
                elif k == "gdn_w":
                    h = s[2]
                    wait_emptied(pe, ("gdn_xx", p, h, LEVELS - 1, 0))
                    b = opened(s)
                    for c in range(NT):
                        i = mm(b[:, c * P:(c + 1) * P], kbe[:, c, :], XT[:, c, :])
                    close(i, s)
                elif k == "gdn_v":
                    h, c = s[2:]
                    first = p % 2 == 0 and c == 0
                    if c == 0:
                        wait_emptied(pe, ("gdn_w", p, h))
                    else:
                        wait_emptied(pe, ("gdn_o", p, h, c - 1))
                    b = opened(s)[:, 0:P]
                    i = mm(b, XT[:, c, :], vb[:, c, :], True, first)
                    if not first:
                        i = mm(b, wT[:, c, :], st_g[:, h, :], False, True)
                    close(i, s)
                elif k == "gdn_o":
                    h, c = s[2:]
                    first = p % 2 == 0 and c == 0
                    oo = ("gdn_oo", p, h)
                    if c == 0:
                        opened(oo)
                        wait_emptied(pe, ("gdn_back", p, h, 3))
                        pe.wait_ge(S["gdn_attn"], GH * p + h + 1)
                    o = bank(oo)[:, c * P:(c + 1) * P]
                    if not first:
                        mm(o, qeT[:, c, :], st_g[:, h, :], True, False)
                    wait_emptied(pe, ("gdn_v", p, h, c))
                    i = mm(o, att[:, c, :], vnew[:, c % 2, :], first, True)
                    if c == NT - 1:
                        close(i, oo)
                    b = opened(s)[:, 0:P]
                    close(mm(b, kdc[:, c, :], vnew[:, c % 2, :]), s)
                elif k == "mix_turn":
                    G = 4 * p + s[2]
                    if s[2] in (0, 3):
                        pe.wait_ge(S["o_mixed"], 8 * p + (4 if s[2] == 0 else 8))
                    else:
                        pe.wait_ge(S["ssd_mixed"], NT * (SG * p + s[2]))
                    for t in range(NT):
                        tag = (*s, t)
                        b = opened(tag)
                        for j in range(4):
                            i = turn(b[:, j * P:(j + 1) * P], gate[:, G % 2, t, j * P:(j + 1) * P])
                        close(i, tag)
                elif k == "bc_turn":
                    pe.wait_ge(S["silu_done"], 24 * p + 16)
                    for g in range(SG):
                        tag = (*s, 0, g)
                        b = opened(tag)
                        for c in range(NT):
                            i = turn(b[:, c * P:(c + 1) * P], bc[:, g, c * P:(c + 1) * P])
                        close(i, tag)
                        tag = (*s, 1, g)
                        b = opened(tag)
                        for c in range(NT):
                            i = mm(b[:, c * P:(c + 1) * P], bc[:, g, c * P:(c + 1) * P], bc[:, 2 + g, c * P:(c + 1) * P])
                        close(i, tag)
                elif k == "x_turn":
                    g = s[2]
                    n = 10 * p + 4 + g
                    pe.wait_ge(S["silu_done"], 24 * p + 20 + 4 * g)
                    for c in range(NT):
                        tag = (*s, c)
                        b = opened(tag)
                        for j in range(4):
                            i = turn(b[:, j * P:(j + 1) * P], slot[:, n % SLOTS, j * HALF + c * P:j * HALF + (c + 1) * P])
                        close(i, tag)
                elif k == "ssd_l":
                    g, c = s[2:]
                    m = NT * (SG * p + g) + c
                    pe.wait_ge(S["ssd_au"], m + 1)
                    for j in range(2):
                        tag = (*s, j)
                        close(mm(opened(tag), lower, aU[:, j * 512:(j + 1) * 512]), tag)
                elif k == "ssd_y":
                    g, c = s[2:]
                    m = NT * (SG * p + g) + c
                    first = p % 2 == 0 and c == 0
                    pe.wait_ge(S["ssd_lg"], m + 1)
                    tag = (*s, "y")
                    b = opened(tag)
                    for j in range(HG):
                        i = mm(b[:, j * SP:(j + 1) * SP], LG[:, j * P:(j + 1) * P], xdt[:, j * SP:(j + 1) * SP])
                    close(i, tag)
                    tag = (*s, "z")
                    b = opened(tag)
                    if first:
                        pe.wait_ge(S["states_clear"], p // 2 + 1)
                    elif c or p % 2:
                        pe.wait_ge(S["ssd_state"], m if c else m - NT + 0)
                    close(mm(b, bc[:, 2 + g, c * P:(c + 1) * P], st_s[:, g, :]), tag)
                    tag = (*s, "w")
                    b = opened(tag)
                    pe.wait_ge(S["ssd_xw"], m + 1)
                    close(mm(b, bt[:, g, c, :], xw), tag)
                elif k == "ret_turn":
                    h = s[2]
                    pe.wait_ge(S["ret_rot"], 2 * (RH * p + h) + 2)
                    v = slot[:, (10 * p + 6 + h) % SLOTS, 0:1024].rearrange("p (t q n) -> p t q n", t=NT, q=2)
                    for j, name in enumerate("qk"):
                        tag = (*s, name)
                        b = opened(tag)
                        for c in range(NT):
                            i = turn(b[:, c * P:(c + 1) * P], v[:, c, j, :])
                        close(i, tag)
                elif k == "ret_s":
                    h = s[2]
                    wait_emptied(pe, ("ret_turn", p, h, "q"))
                    wait_emptied(pe, ("ret_turn", p, h, "k"))
                    b = opened(s)
                    for c in range(NT):
                        i = mm(b[:, c * P:(c + 1) * P], rkT[:, c, :], rqT[:, c, :])
                    close(i, s)
                elif k == "ret_o":
                    h, c = s[2:]
                    first = p % 2 == 0 and c == 0
                    oo = ("ret_oo", p, h)
                    vv = slot[:, (10 * p + 6 + h) % SLOTS, 1024:1536].rearrange("p (t n) -> p t n", t=NT)
                    if c == 0:
                        opened(oo)
                        wait_emptied(pe, ("ret_s", p, h))
                        wait_emptied(pe, ("proj", p, AT["ret", 2 * h + 1], 1))
                    else:
                        wait_emptied(pe, ("ret_o", p, h, c - 1))
                    o = bank(oo)[:, c * P:(c + 1) * P]
                    if not first:
                        mm(o, rqd[:, c, :], st_r[:, h, :], True, False)
                    i = mm(o, rS[:, c, :], vv[:, c, :], first, True)
                    if c == NT - 1:
                        close(i, oo)
                    if c == 0:
                        pe.wait_ge(S["ret_kd"], RH * p + h + 1)
                    b = opened(s)[:, 0:P]
                    close(mm(b, rkd[:, c, :], vv[:, c, :]), s)

        @block.vector
        def _(dve):
            n_step = [0]

            def chain(ins):
                n_step[0] += 1
                ins.then_inc(dve_step, 1)
                dve.wait_ge(dve_step, n_step[0])

            tt, ts, stt = nc.vector.tensor_tensor, nc.vector.tensor_scalar, nc.vector.scalar_tensor_tensor

            def clear_states():
                nc.vector.memset(st_s[:].rearrange("p a b -> p (a b)"), 0.0).then_inc(S["states_clear"], 1)

            def mean_eps(src, dst, width, name):
                ts(dst, src, 1.0 / width, EPS, ALU.mult, ALU.add).then_inc(S[name], 1)

            dve.wait_ge(loaded, 16 * (1 + 2 * DEPTH))
            chain(nc.vector.memset(sm_t[:].rearrange("p a b -> p (a b)"), 0.0))
            clear_states()
            dve.wait_ge(S["nega_ready"], 1)
            chain(ts(nega[:], nega[:], -1.0, None, ALU.mult))
            for s in plan:
                k, p = s[0], s[1]
                l, first_half = p // 2, p % 2 == 0
                if k == "norm":
                    t = s[2]
                    n = NT * p + t
                    dve.wait_ge(S["x_squares"], n + 1)
                    chain(tt(xss[:, 0:1], xss[:, 0:1], xss[:, 1:2], ALU.add))
                    mean_eps(xss[:, 0:1], xss[:, 2:3], D, "x_mean")
                    for j in range(2):
                        tag = (*s, j)
                        wait_filled(dve, tag)
                        empty(tt(hT[:, 4 * j:4 * j + 4, t * P:(t + 1) * P], bank4(tag),
                                 over_cols(par[:, l, Q_PRE + 4 * j:Q_PRE + 4 * j + 4]), ALU.mult), tag)
                elif k == "small":
                    wait_filled(dve, s)
                    sm = small[:, p % 2]
                    empty(nc.vector.tensor_copy(sm, bank(s)[:, 0:NT * NSM].rearrange("p (t n) -> p t n", t=NT)), s)
                    wait_emptied(dve, s)
                    v = [sm_t[:, i, :].rearrange("p (t n) -> p t n", t=NT) for i in range(6)]
                    a, e, z, q, r, m = v
                    chain(tt(a, sm[:, :, GH:NSM], over_rows(row[:, l, R_DT:R_DT + NDEC]), ALU.add))
                    chain(ts(m, a, -1.0, None, ALU.mult))
                    tt(m, m, a, ALU.max).then_inc(S["sm_abs"], 1)
                    dve.wait_ge(S["sm_exp"], p + 1)
                    chain(ts(q, e, 2.0, None, ALU.add))
                    chain(nc.vector.reciprocal(q, q))
                    chain(tt(q, q, e, ALU.mult))
                    chain(tt(z, q, q, ALU.mult))
                    chain(ts(r, z, 1.0 / 17, None, ALU.mult))
                    for o in (15, 13, 11, 9, 7, 5, 3):
                        chain(stt(r, r, 1.0 / o, z, ALU.add, ALU.mult))
                    chain(stt(r, r, 1.0, q, ALU.add, ALU.mult))
                    chain(ts(a, a, 0.0, None, ALU.max))
                    chain(stt(dt[:, p % 2], r, 2.0, a, ALU.mult, ALU.add))
                    dve.wait_ge(S["sm_beta_exp"], p + 1)
                    chain(ts(beta[:, p % 2], beta[:, p % 2], 1.0, None, ALU.add))
                    chain(nc.vector.reciprocal(beta[:, p % 2], beta[:, p % 2]))
                    tt(dg[:, p % 2], dt[:, p % 2], over_rows(nega[:, l, :]), ALU.mult).then_inc(S["sm_decays"], 1)
                elif k == "proj" and s[4] == 3:
                    i, half = s[2], s[3]
                    tag = s[:4]
                    mt = mtile(p, i, half)
                    if mt:
                        n, m, dst = mt
                        wait_emptied(dve, tag)
                        if n >= 2:
                            dve.wait_ge(S["silu_done"], n - 1)
                        w = par[:, l, Q_CONV + TAPS * m:Q_CONV + TAPS * (m + 1)]
                        r, o = raw[:, n % 2, :], cv[:, n % 2, :]
                        if m >= 12:
                            b = par[:, l, Q_BIAS + m - 12:Q_BIAS + m - 11]
                            chain(ts(o, r[:, 0:HALF], w[:, 0:1], b, ALU.mult, ALU.add))
                        else:
                            chain(ts(o, r[:, 0:HALF], w[:, 0:1], None, ALU.mult))
                        for j in range(1, TAPS):
                            ins = stt(o, r[:, j:j + HALF], w[:, j:j + 1], o, ALU.mult, ALU.add)
                            if j < TAPS - 1:
                                chain(ins)
                            else:
                                ins.then_inc(S["conv_done"], 1)
                    elif PIECES[i][0] == "ret" and PIECES[i][1] % 2 == 0:
                        h = PIECES[i][1] // 2
                        m = 2 * (RH * p + h) + half
                        wait_filled(dve, tag)
                        dve.wait_ge(rope_in, 16 * (p + 1))
                        slot_wait(dve, 10 * p + 6 + h)
                        if m >= 1:
                            dve.wait_ge(S["ret_sum"], m)
                        b = bank(tag).rearrange("p (t q e n) -> p t q e n", t=2, q=2, e=2)
                        ns = slot[:, (10 * p + 6 + h) % SLOTS, 0:1024].rearrange("p (t q e n) -> p t q e n", t=NT, q=2, e=2)
                        r0 = rot[:, 0, :].rearrange("p (t q e n) -> p t q e n", t=2, q=2, e=2)
                        r1 = rot[:, 1, :].rearrange("p (t q e n) -> p t q e n", t=2, q=2, e=2)
                        for u in range(2):
                            tile = 2 * half + u
                            co = rp[:, tile * 64:(tile + 1) * 64]
                            si = rp[:, NT * 64 + tile * 128:NT * 64 + (tile + 1) * 128].rearrange("p (e n) -> p e n", e=2)
                            tt(r0[:, u].rearrange("p q e n -> p (q e) n"), b[:, u].rearrange("p q e n -> p (q e) n"),
                               over_rows(co), ALU.mult)
                            ins = tt(r1[:, u], b[:, u, :, ::-1, :],
                                     si.unsqueeze(1).broadcast_to([P, 2, 2, 64]), ALU.mult)
                        empty(ins, tag)
                        wait_emptied(dve, tag)
                        tt(slot[:, (10 * p + 6 + h) % SLOTS, half * 512:half * 512 + 512], rot[:, 0, :], rot[:, 1, :],
                           ALU.add).then_inc(S["ret_sum"], 1)
                        dve.wait_ge(S["ret_sum"], m + 1)
                        dve.sem_inc(S["ret_rot"], 1)
                elif k == "gdn_turn":
                    h = s[2]
                    n = GH * p + h
                    be = beta[:, p % 2, :, h]
                    de = dec[:, p % 2]
                    dve.wait_ge(S["gdn_squares"], n + 1)
                    if n:
                        dve.wait_ge(S["gdn_rstd"], n)
                    nc.vector.tensor_reduce(gss[:], junk[:].rearrange("p q (c n) -> p (q c) n", c=NT), mybir.AxisListType.X,
                                            ALU.add).then_inc(S["gdn_sums"], 1)
                    dve.wait_ge(S["gdn_rstd"], n + 1)
                    wait_emptied(dve, ("small2", p))
                    rq, rk = rs[:, 0:4], rs[:, 4:8]
                    nc.vector.tensor_copy(sc[:, 0, :], rk)
                    tt(sc[:, 1, :], rk, be, ALU.mult)
                    tt(sc[:, 3, :], rk, de[:, 1, :, h], ALU.mult)
                    chain(ts(sc[:, 4, :], rq, DK ** -0.5, None, ALU.mult))
                    tt(sc[:, 2, :], sc[:, 1, :], de[:, 0, :, h], ALU.mult)
                    chain(tt(sc[:, 5, :], sc[:, 4, :], de[:, 0, :, h], ALU.mult))
                    for name, outs in (("k", ((kh, 0), (kb, 1), (kbe, 2), (kdc, 3))), ("q", ((qh, 4), (qe, 5)))):
                        tag = (*s, name)
                        wait_filled(dve, tag)
                        for o, j in outs:
                            ins = tt(o, bank4(tag), over_cols(sc[:, j, :]), ALU.mult)
                        empty(ins, tag)
                    tag = (*s, "v")
                    wait_filled(dve, tag)
                    empty(tt(vb, bank4(tag), over_cols(be), ALU.mult), tag)
                elif k == "gdn_gram":
                    h = s[2]
                    n = GH * p + h
                    wait_emptied(dve, ("gdn_decay", p, h))
                    tag = (*s, 0)
                    wait_filled(dve, tag)
                    if n:
                        dve.wait_ge(S["gdn_masks"], LEVELS * n)
                    empty(tt(aT, bank4(tag), et[:, h], ALU.mult), tag)
                    tag = (*s, 1)
                    wait_filled(dve, tag)
                    empty(tt(att, bank4(tag), et[:, h], ALU.mult), tag)
                    dve.wait_ge(S["gdn_masks"], LEVELS * n + 1)
                    stt(XT, bT0, -1.0, over_rows(ident), ALU.mult, ALU.add).then_inc(S["gdn_xt"], 1)
                elif k == "gdn_xx":
                    h, lv = s[2], s[3]
                    if lv < LEVELS - 1:
                        tag = (*s, 0)
                        wait_filled(dve, tag)
                        wait_emptied(dve, ("gdn_x0", p, h) if lv == 1 else ("gdn_xx", p, h, lv - 1, 1))
                        empty(tt(X, X, bank4(tag), ALU.subtract), tag)
                    tag = (*s, 1 if lv < LEVELS - 1 else 0)
                    wait_filled(dve, tag)
                    if lv == 1:
                        dve.wait_ge(S["gdn_xt"], GH * p + h + 1)
                    empty(tt(XT, XT, bank4(tag), ALU.subtract), tag)
                elif k == "gdn_v":
                    wait_filled(dve, s)
                    empty(nc.vector.tensor_copy(vnew[:, s[3] % 2, :], bank(s)[:, 0:P]), s)
                elif k == "gdn_o":
                    h, c = s[2:]
                    wait_filled(dve, s)
                    if first_half and c == 0:
                        empty(nc.vector.tensor_copy(st_g[:, h, :], bank(s)[:, 0:P]), s)
                    else:
                        if c:
                            wait_emptied(dve, ("gdn_o", p, h, c - 1))
                        empty(stt(st_g[:, h, :], st_g[:, h, :], dec[:, p % 2, 2, c, h:h + 1], bank(s)[:, 0:P],
                                  ALU.mult, ALU.add), s)
                elif k in ("gdn_fin", "ret_fin"):
                    h = s[2]
                    r = k == "ret_fin"
                    n = 8 * p + 4 * r + h
                    G = 4 * p + 3 * r
                    oo = ("ret_oo" if r else "gdn_oo", p, h)
                    dve.wait_ge(S["o_squares"], n + 1)
                    chain(nc.vector.tensor_reduce(ss[:, 2:6], junk[:, 0, :].rearrange("p (c n) -> p c n", c=NT),
                                                  mybir.AxisListType.X, ALU.add))
                    mean_eps(ss[:, 2:6], rs[:, 8:12], P, "o_mean")
                    dve.wait_ge(S["o_rstd"], n + 1)
                    g = gate[:, G % 2, :, h * P:(h + 1) * P]
                    if r:
                        wait_emptied(dve, ("proj", p, AT["ret", 2 * h + 1], 1))
                    else:
                        wait_emptied(dve, ("proj", p, AT["gz", h // 2], 1))
                    chain(tt(g, g, over_cols(rs[:, 12:16]), ALU.mult))
                    empty(tt(g, g, bank4(oo), ALU.mult), oo)
                    wait_emptied(dve, oo)
                    dve.sem_inc(S["o_mixed"], 1)
                elif k == "mix_turn":
                    for t in range(NT):
                        tag = (*s, t)
                        wait_filled(dve, tag)
                        empty(tt(mixT[:, :, t * P:(t + 1) * P], bank4(tag), over_cols(par[:, l, Q_MIX + 4 * s[2]:Q_MIX + 4 * s[2] + 4]),
                                 ALU.mult), tag)
                elif k == "out":
                    G, nh, t = s[2:]
                    wait_filled(dve, s)
                    o = acc[:, t, nh * 512:(nh + 1) * 512]
                    if G == 0:
                        if p:
                            dve.wait_ge(S["f_scaled"], NT * (p - 1) + t + 1)
                        empty(nc.vector.tensor_copy(o, bank(s)), s)
                    else:
                        wait_emptied(dve, ("out", p, G - 1, nh, t))
                        empty(tt(o, o, bank(s), ALU.add), s)
                elif k == "bc_turn":
                    for g in range(SG):
                        tag = (*s, 1, g)
                        wait_filled(dve, tag)
                        empty(tt(gT[:, g], bank4(tag), over_rows(upper), ALU.mult), tag)
                elif k == "ssd_y":
                    g, c = s[2:]
                    m = NT * (SG * p + g) + c
                    G = 4 * p + 1 + g
                    heads = slice(GH + HG * g, GH + HG * (g + 1))
                    per_head = lambda a: a.unsqueeze(2).broadcast_to([P, HG, SP])
                    v8 = lambda a: a.rearrange("p (h n) -> p h n", h=HG)
                    wait_emptied(dve, ("x_turn", p, g, c))
                    if m:
                        dve.wait_ge(S["ssd_xw"], m)
                        wait_filled(dve, (*ssd_before(s), "y"))
                    tt(v8(xdt), v8(xt[:, c, :]), per_head(dt[:, p % 2, c, heads]), ALU.mult).then_inc(S["ssd_xdt"], 1)
                    wait_emptied(dve, ("ssd_l", p, g, c, 1))
                    L3 = LG.rearrange("p (h n) -> p h n", h=HG)
                    if c == 0:
                        wait_emptied(dve, ("bc_turn", p, 1, g))
                    tt(L3, L3, over_rows(gT[:, g, c, :], HG), ALU.mult).then_inc(S["ssd_lg"], 1)
                    tag = (*s, "z")
                    wait_filled(dve, tag)
                    if m:
                        dve.wait_ge(S["ssd_mixed"], m)
                    empty(tt(v8(yy), v8(bank(tag)), per_head(dec[:, p % 2, 0, c, heads]), ALU.mult), tag)
                    wait_emptied(dve, tag)
                    tag = (*s, "y")
                    empty(tt(yy, yy, bank(tag), ALU.add), tag)
                    tag = (*s, "w")
                    st = st_s[:, g, :]
                    wait_filled(dve, tag)
                    chain(tt(v8(st), v8(st), per_head(dec[:, p % 2, 2, c, heads]), ALU.mult))
                    empty(tt(st, st, bank(tag), ALU.add), tag)
                    wait_emptied(dve, tag)
                    if first_half is False and c == NT - 1 and g == SG - 1 and l + 1 < DEPTH:
                        clear_states()
                    dve.sem_inc(S["ssd_state"], 1)
                    dve.wait_ge(S["ssd_xd"], m + 1)
                    chain(tt(yy, yy, xD, ALU.add))
                    wait_emptied(dve, ("proj", p, AT["sz", g, N_SZ - 1], 1))
                    tt(yy, yy, gate[:, G % 2, c, :], ALU.mult).then_inc(S["ssd_ygated"], 1)
                    dve.wait_ge(S["ssd_squares"], m + 1)
                    mean_eps(ss[:, 6:7], ss[:, 7:8], 512, "ssd_mean")
                elif k == "ret_turn":
                    h = s[2]
                    tag = (*s, "q")
                    wait_filled(dve, tag)
                    nc.vector.tensor_copy(rqT, bank4(tag))
                    empty(tt(rqd, bank4(tag), over_rows(con[:, C_QD + h * P:C_QD + (h + 1) * P]), ALU.mult), tag)
                elif k == "ret_s":
                    h = s[2]
                    wait_filled(dve, s)
                    empty(tt(rS, bank4(s), over_rows(con[:, C_DM + h * P:C_DM + (h + 1) * P]), ALU.mult), s)
                elif k == "ret_o":
                    h, c = s[2:]
                    wait_filled(dve, s)
                    if first_half and c == 0:
                        empty(nc.vector.tensor_copy(st_r[:, h, :], bank(s)[:, 0:P]), s)
                    else:
                        if c:
                            wait_emptied(dve, ("ret_o", p, h, c - 1))
                        empty(stt(st_r[:, h, :], st_r[:, h, :], LAM[h] ** P, bank(s)[:, 0:P], ALU.mult, ALU.add), s)
                elif k == "final":
                    t = s[2]
                    n = NT * p + t
                    dve.wait_ge(S["f_squares"], n + 1)
                    mean_eps(ss[:, 8:9], ss[:, 9:10], D, "f_mean")
                    dve.wait_ge(S["f_scaled"], n + 1)
                    dve.wait_ge(post_in, 16 * (l + 1))
                    chain(tt(xsq2, xsq2, post[:], ALU.mult))
                    dve.wait_ge(xf_in[0], 16 * (n + 1))
                    tt(xsq2, xsq2, xfin, ALU.add).then_inc(S["f_done"], 1)

        @block.scalar
        def _(act):
            A = nc.scalar.activation
            n_step = [0]

            def chain(ins):
                n_step[0] += 1
                ins.then_inc(act_step, 1)
                act.wait_ge(act_step, n_step[0])

            junk_read = []

            def square_into_junk(read_by):
                if junk_read:
                    act.wait_ge(*junk_read.pop())
                junk_read.append(read_by)

            act.wait_ge(loaded, 16 * (1 + 2 * DEPTH))
            A(nega[:], row[:, :, R_A:R_A + NDEC], ACT.Exp).then_inc(S["nega_ready"], 1)
            for s in plan:
                k, p = s[0], s[1]
                l, first_half = p // 2, p % 2 == 0
                if k == "norm":
                    t = s[2]
                    n = NT * p + t
                    act.wait_ge(x_in[n % 2], 16 * (n // 2 + 1))
                    square_into_junk((S["x_mean"], n + 1))
                    for j in range(2):
                        ins = A(junk[:, j, :], xin[:, n % 2, j * 512:(j + 1) * 512], ACT.Square, accum_out=xss[:, j:j + 1])
                    ins.then_inc(S["x_squares"], 1)
                    act.wait_ge(S["x_rstd"], n + 1)
                    A(xin[:, n % 2, :], xin[:, n % 2, :], ACT.Copy, scale=xrs[:, 0:1]).then_inc(S["x_normed"], 1)
                elif k == "small":
                    act.wait_ge(S["sm_abs"], p + 1)
                    A(sm_t[:, 1, :], sm_t[:, 5, :], ACT.Exp, scale=-1.0).then_inc(S["sm_exp"], 1)
                    A(beta[:, p % 2], small[:, p % 2, :, 0:GH], ACT.Exp, scale=-1.0).then_inc(S["sm_beta_exp"], 1)
                elif k == "small2":
                    wait_filled(act, s)
                    empty(A(dec[:, p % 2].rearrange("p j t n -> p (j t n)"), bank(s)[:, 0:3 * NT * NDEC], ACT.Exp), s)
                elif k == "proj" and s[4] == 3:
                    i, half = s[2], s[3]
                    tag = s[:4]
                    mt = mtile(p, i, half)
                    kind = PIECES[i][0]
                    wait_filled(act, tag) if kind != "ret" or PIECES[i][1] % 2 else None
                    if mt:
                        n, m, dst = mt
                        if n >= 2:
                            act.wait_ge(S["conv_done"], n - 1)
                        A(raw[:, n % 2, 0:3], halo[:, m, :] if not first_half else con[:, C_ZERO:C_ZERO + 3], ACT.Copy)
                        if first_half:
                            act.wait_ge(act_step, n_step[0]) if n_step[0] else None
                            A(halo[:, m, :], bank(tag)[:, HALF - 3:HALF], ACT.Copy)
                        empty(A(raw[:, n % 2, 3:3 + HALF], bank(tag), ACT.Copy), tag)
                        act.wait_ge(S["conv_done"], n + 1)
                        sl = slot_of(p, i, half)
                        if sl is not None and sl >= SLOTS:
                            slot_wait(act, sl)
                        A(dst, cv[:, n % 2, :], ACT.Silu).then_inc(S["silu_done"], 1)
                    elif kind in ("gz", "sz"):
                        j = PIECES[i][-1]
                        G = gate_of(p, i)
                        gate_wait(act, G)
                        empty(A(gate[:, G % 2, 2 * half:2 * half + 2, j * PC:(j + 1) * PC],
                                bank(tag).rearrange("p (t n) -> p t n", t=2), ACT.Silu), tag)
                    elif PIECES[i][1] % 2:
                        h = PIECES[i][1] // 2
                        G = gate_of(p, i)
                        gate_wait(act, G)
                        b = bank(tag).rearrange("p (t n) -> p t n", t=2)
                        v = slot[:, (10 * p + 6 + h) % SLOTS, 1024:1536].rearrange("p (t n) -> p t n", t=NT)
                        slot_wait(act, 10 * p + 6 + h)
                        A(v[:, 2 * half:2 * half + 2, :], b[:, :, 0:P], ACT.Copy)
                        empty(A(gate[:, G % 2, 2 * half:2 * half + 2, h * P:(h + 1) * P], b[:, :, P:2 * P], ACT.Silu), tag)
                elif k == "gdn_decay":
                    wait_filled(act, s)
                    empty(A(et[:, s[2]].rearrange("p c n -> p (c n)"), bank(s), ACT.Exp), s)
                elif k == "gdn_turn":
                    h = s[2]
                    n = GH * p + h
                    square_into_junk((S["gdn_sums"], n + 1))
                    for j, name in enumerate("qk"):
                        tag = (*s, name)
                        wait_filled(act, tag)
                        ins = A(junk[:, j, :], bank(tag), ACT.Square)
                    ins.then_inc(S["gdn_squares"], 1)
                elif k == "gdn_back":
                    for j, o in enumerate((kT, kbT, qT, qeT)):
                        tag = (*s, j)
                        wait_filled(act, tag)
                        empty(A(o, bank4(tag), ACT.Copy), tag)
                elif k == "gdn_x0":
                    wait_filled(act, s)
                    empty(A(X, bank4(s), ACT.Copy), s)
                elif k == "gdn_p":
                    wait_filled(act, s)
                    empty(A(PP, bank4(s), ACT.Copy), s)
                elif k == "gdn_w":
                    wait_filled(act, s)
                    empty(A(wT, bank4(s), ACT.Copy, scale=-1.0), s)
                elif k in ("gdn_fin", "ret_fin"):
                    r = k == "ret_fin"
                    n = 8 * p + 4 * r + s[2]
                    oo = ("ret_oo" if r else "gdn_oo", p, s[2])
                    wait_filled(act, oo)
                    square_into_junk((S["o_mean"], n + 1))
                    A(junk[:, 0, :], bank(oo), ACT.Square).then_inc(S["o_squares"], 1)
                elif k == "bc_turn":
                    if p:
                        pass
                    for g in range(SG):
                        tag = (*s, 0, g)
                        wait_filled(act, tag)
                        if g == 0:
                            act.wait_ge(S["o_mixed"], 8 * p + 4)
                        empty(A(bt[:, g], bank4(tag), ACT.Copy), tag)
                elif k == "x_turn":
                    g = s[2]
                    if SG * p + g:
                        act.wait_ge(S["ssd_xd"], NT * (SG * p + g))
                        act.wait_ge(S["ssd_xdt"], NT * (SG * p + g))
                    for c in range(NT):
                        tag = (*s, c)
                        wait_filled(act, tag)
                        empty(A(xt[:, c, :], bank(tag), ACT.Copy), tag)
                elif k == "ssd_l":
                    g, c = s[2:]
                    m = NT * (SG * p + g) + c
                    if m:
                        wait_filled(act, (*ssd_before(s), "y"))
                    for j in range(2):
                        tag = (*s, j)
                        wait_filled(act, tag)
                        empty(A(LG[:, j * 512:(j + 1) * 512], bank(tag), ACT.Exp), tag)
                elif k == "ssd_y":
                    g, c = s[2:]
                    m = NT * (SG * p + g) + c
                    G = 4 * p + 1 + g
                    act.wait_ge(S["ssd_ygated"], m + 1)
                    square_into_junk((S["ssd_mean"], m + 1))
                    A(junk[:, 0, :], yy, ACT.Square, accum_out=ss[:, 6:7]).then_inc(S["ssd_squares"], 1)
                    act.wait_ge(S["ssd_rstd"], m + 1)
                    A(gate[:, G % 2, c, :], yy, ACT.Copy, scale=ssr[:, 0:1]).then_inc(S["ssd_mixed"], 1)
                elif k == "ret_turn":
                    h = s[2]
                    tag = (*s, "k")
                    wait_filled(act, tag)
                    empty(A(rkT, bank4(tag), ACT.Copy), tag)
                    v = slot[:, (10 * p + 6 + h) % SLOTS, 0:1024].rearrange("p (t q n) -> p t q n", t=NT, q=2)
                    if h:
                        wait_filled(act, ("ret_o", p, h - 1, NT - 1))
                    else:
                        act.wait_ge(S["ssd_mixed"], NT * SG * (p + 1))
                    A(rkd, v[:, :, 1, :], ACT.Copy, scale=con[:, C_KD + h:C_KD + h + 1]).then_inc(S["ret_kd"], 1)
                elif k == "final":
                    t = s[2]
                    n = NT * p + t
                    wait_emptied(act, ("out", p, GROUPS - 1, 1, t))
                    if n:
                        act.wait_ge(S["f_mean"], n)
                        act.wait_ge(x_stored, 16 * n)
                    A(xsq2, acc[:, t, :], ACT.Square, accum_out=ss[:, 8:9]).then_inc(S["f_squares"], 1)
                    act.wait_ge(S["f_rstd"], n + 1)
                    A(xsq2, acc[:, t, :], ACT.Copy, scale=frs[:, 0:1]).then_inc(S["f_scaled"], 1)

        @block.gpsimd
        def _(pool):
            tt, ts = nc.gpsimd.tensor_tensor, nc.gpsimd.tensor_scalar
            n_step = [0]

            def chain(ins):
                n_step[0] += 1
                ins.then_inc(pool_step, 1)
                pool.wait_ge(pool_step, n_step[0])

            pool.wait_ge(loaded, 16 * (1 + 2 * DEPTH))
            for s in plan:
                k, p = s[0], s[1]
                if k == "norm":
                    n = NT * p + s[2]
                    pool.wait_ge(S["x_mean"], n + 1)
                    if n:
                        pool.wait_ge(S["x_normed"], n)
                    tt(xrs[:, 0:1], xss[:, 2:3], pw[:, 0:1], ALU.pow).then_inc(S["x_rstd"], 1)
                elif k == "gdn_decay":
                    h = s[2]
                    if h == 0:
                        pool.wait_ge(S["sm_decays"], p + 1)
                        if p:
                            pool.wait_ge(S["ret_sum"], 2 * RH * p)
                        pool.dma_start(rp[:], rope[p % 2]).then_inc(rope_in, 16)
                    if h >= 2:
                        wait_filled(pool, ("gdn_decay", p, h - 2))
                    tt(rot[:, h % 2, :].rearrange("p (c n) -> p c n", c=NT), over_rows(upper), over_cols(dg[:, p % 2, :, h]),
                       ALU.mult).then_inc(S["gdn_gu"], 1)
                elif k == "gdn_turn":
                    n = GH * p + s[2]
                    pool.wait_ge(S["gdn_sums"], n + 1)
                    if n:
                        wait_emptied(pool, ("gdn_turn", (n - 1) // GH, (n - 1) % GH, "q"))
                    chain(ts(gss[:, :], gss[:, :], EPS, None, ALU.add))
                    tt(rs[:, 0:8], gss[:, :], pw, ALU.pow).then_inc(S["gdn_rstd"], 1)
                elif k == "gdn_gram":
                    h = s[2]
                    wait_emptied(pool, (*s, 0))
                    for lv in range(LEVELS):
                        if lv == 2:
                            pool.wait_ge(S["gdn_xt"], GH * p + h + 1)
                        if lv == 1:
                            wait_emptied(pool, (*s, 1))
                            tt(att, att, over_rows(upper), ALU.mult).then_inc(S["gdn_attn"], 1)
                        if lv >= 3:
                            wait_filled(pool, ("gdn_p", p, h, lv - 2))
                        m = con[:, C_LEV + lv * P:C_LEV + (lv + 1) * P]
                        tt((bT0, bT1)[lv % 2], aT, over_rows(m), ALU.mult).then_inc(S["gdn_masks"], 1)
                elif k in ("gdn_fin", "ret_fin"):
                    n = 8 * p + 4 * (k == "ret_fin") + s[2]
                    pool.wait_ge(S["o_mean"], n + 1)
                    if n:
                        pool.wait_ge(S["o_mixed"], n)
                    tt(rs[:, 12:16], rs[:, 8:12], pw[:, 0:4], ALU.pow).then_inc(S["o_rstd"], 1)
                elif k == "ssd_l":
                    g, c = s[2:]
                    m = NT * (SG * p + g) + c
                    heads = slice(GH + HG * g, GH + HG * (g + 1))
                    if m:
                        wait_filled(pool, ("ssd_l", *ssd_before(s)[1:], 1))
                    if g == 0 and c == 0:
                        pool.wait_ge(S["o_mixed"], 8 * p + 4)
                    tt(aU.rearrange("p (h n) -> p h n", h=HG), over_rows(upper, HG), over_cols(dg[:, p % 2, c, heads]),
                       ALU.mult).then_inc(S["ssd_au"], 1)
                elif k == "ssd_y":
                    g, c = s[2:]
                    m = NT * (SG * p + g) + c
                    heads = slice(GH + HG * g, GH + HG * (g + 1))
                    per_head = lambda a: a.unsqueeze(2).broadcast_to([P, HG, SP])
                    v8 = lambda a: a.rearrange("p (h n) -> p h n", h=HG)
                    pool.wait_ge(S["ssd_xdt"], m + 1)
                    if m:
                        wait_filled(pool, (*ssd_before(s), "w"))
                    tt(v8(xw), v8(xdt), per_head(dec[:, p % 2, 1, c, heads]), ALU.mult).then_inc(S["ssd_xw"], 1)
                    if m:
                        pool.wait_ge(S["ssd_ygated"], m)
                    tt(v8(xD), v8(xt[:, c, :]), per_head(row[:, p // 2, R_D + HG * g:R_D + HG * (g + 1)]), ALU.mult)\
                        .then_inc(S["ssd_xd"], 1)
                    pool.wait_ge(S["ssd_mean"], m + 1)
                    if m:
                        pool.wait_ge(S["ssd_mixed"], m)
                    tt(ssr[:, 0:1], ss[:, 7:8], pw[:, 0:1], ALU.pow).then_inc(S["ssd_rstd"], 1)
                elif k == "final":
                    t = s[2]
                    n = NT * p + t
                    if n:
                        pool.wait_ge(S["f_done"], n)
                    if n % (2 * NT) == 0:
                        pool.dma_start(post[:], post_norm[p // 2].partition_broadcast(P)).then_inc(post_in, 16)
                    pool.dma_start(xfin, x_rows(p, t)).then_inc(xf_in[0], 16)
                    pool.wait_ge(S["f_mean"], n + 1)
                    tt(frs[:, 0:1], ss[:, 9:10], pw[:, 0:1], ALU.pow).then_inc(S["f_rstd"], 1)
                    pool.wait_ge(S["f_done"], n + 1)
                    r = (p % 2) * HALF + t * P
                    pool.dma_start((x1 if p < 2 else out)[r:r + P, :], xsq2).then_inc(x_stored, 16)
            pool.wait_ge(x_stored, 16 * NT * PARTS)


def kernel(**inputs):
    import concourse.bacc as bacc
    from concourse.bass_utils import run_bass_kernel_spmd

    f = {k: np.asarray(v) for k, v in inputs.items()}
    w, wo = f["w_in"], f["w_out"]
    at = np.cumsum([0, 512, 512, 512, 512, 4, 4, 1024, 256, 256, 1024, 16, 512, 512, 512, 512])
    gq, gk, gv, gz, gb, ga, sx, sB, sC, sz, sdt, rq, rk, rv, rg = [w[:, :, a:b] for a, b in zip(at[:-1], at[1:])]
    h128 = lambda a, h: a[:, :, h * P:(h + 1) * P]
    cols = [gz] + [t for h in range(GH) for t in (h128(gq, h), h128(gk, h), h128(gv, h))] + [sB, sC]
    for g in range(SG):
        cols += [sz[:, :, g * 512:(g + 1) * 512], sx[:, :, g * 512:(g + 1) * 512]]
    cols += [t for h in range(RH) for t in (h128(rq, h), h128(rk, h), h128(rv, h), h128(rg, h))]
    wl = np.concatenate(cols, axis=2)
    n_pc = len(PIECES)
    wl = wl.reshape(DEPTH, KD, P, n_pc, PC).transpose(0, 3, 2, 1, 4).reshape(DEPTH, n_pc, P, KD * PC)
    ws = np.concatenate([gb, ga, sdt], axis=2).reshape(DEPTH, KD, P, NSM).transpose(0, 2, 1, 3)
    wol = wo.reshape(DEPTH, GROUPS, 4, P, 2, 512).transpose(0, 1, 4, 3, 2, 5).reshape(DEPTH, GROUPS, 2, P, 2048)
    pars = np.zeros((DEPTH, P, Q_END), np.float32)
    gc, scv = f["gdn_conv"], f["ssd_conv"]
    tiles = [gc[:, :, j * 512 + h * P:j * 512 + (h + 1) * P] for h in range(GH) for j in range(3)]
    tiles += [scv[:, :, 1024 + j * P:1024 + (j + 1) * P] for j in range(4)] + [scv[:, :, j * P:(j + 1) * P] for j in range(8)]
    bias = f["ssd_conv_b"]
    bts = [bias[:, 1024 + j * P:1024 + (j + 1) * P] for j in range(4)] + [bias[:, j * P:(j + 1) * P] for j in range(8)]
    for m, t in enumerate(tiles):
        pars[:, :, Q_CONV + TAPS * m:Q_CONV + TAPS * (m + 1)] = t.transpose(0, 2, 1)
    for m, t in enumerate(bts):
        pars[:, :, Q_BIAS + m] = t
    pars[:, :, Q_PRE:Q_PRE + KD] = f["pre_norm"].reshape(DEPTH, KD, P).transpose(0, 2, 1)
    pars[:, :, Q_MIX:Q_MIX + 4] = f["gdn_norm"][:, :, None]
    pars[:, :, Q_MIX + 4:Q_MIX + 12] = f["ssd_norm"].reshape(DEPTH, 8, P).transpose(0, 2, 1)
    pars[:, :, Q_MIX + 12:Q_MIX + 16] = f["ret_norm"][:, :, None]
    rows = np.concatenate([f["gdn_A_log"], f["ssd_A_log"], f["gdn_dt_bias"], f["ssd_dt_bias"], f["ssd_D"]], axis=1)
    cons, rope = constants()

    nc = bacc.Bacc("TRN2", target_bir_lowering=False, num_devices=1)
    arrays = {"x": f["x"].reshape(SEQ, D), "w_in": wl, "w_small": ws, "w_out": wol, "cons": cons, "rope": rope, "pars": pars, "rows": rows,
              "post": f["post_norm"]}
    arrays = {f"in_{k}": np.ascontiguousarray(v) for k, v in arrays.items()}
    args = [nc.dram_tensor(k, v.shape, mybir.dt.from_np(v.dtype), kind="ExternalInput").ap() for k, v in arrays.items()]
    out = nc.dram_tensor("out_0", (SEQ, D), F32, kind="ExternalOutput").ap()
    hybrid_kernel(nc, *args, out)
    r = run_bass_kernel_spmd(nc, [arrays], core_ids=[0])
    return r.results[0]["out_0"].reshape(1, SEQ, D)
```

```python
from contextlib import ExitStack

import numpy as np

import concourse.bass as bass
from concourse import mybir

ALU = mybir.AluOpType
ACT = mybir.ActivationFunctionType
F32 = mybir.dt.float32

P = 128
D, SEQ, DEPTH = 1024, 1024, 2
HALF = 512
NT = HALF // P
KD = D // P
PARTS = DEPTH * SEQ // HALF
EPS = 1e-6
GH, SH, RH = 4, 16, 4
SG, SP = 2, 64
HG = SH // SG
DK = 128
NDEC = GH + SH
NSM = GH + NDEC
LEVELS = 7
TAPS = 4
GROUPS = 4

PC = 256
N_GDN_PC, N_GZ, N_BC, N_SZ, N_SX, N_RET = 6, 2, 2, 2, 2, 8
PIECES = ([("gz", 0)] + [("gdn", i) for i in range(4)] + [("gz", 1)] + [("gdn", i) for i in range(4, N_GDN_PC)]
          + [("bc", i) for i in range(N_BC)]
          + [(k, g, i) for g in range(SG) for k, n in (("sx", N_SX), ("sz", N_SZ)) for i in range(n)]
          + [("ret", i) for i in range(N_RET)])
AT = {piece: i for i, piece in enumerate(PIECES)}
W_RING = 3
SLOTS = 2
MIX_BANKS = (2, 3, 4, 5, 6)
LAM = [1.0 - 2.0 ** (-5.0 - h) for h in range(RH)]

C_ID, C_UP, C_LOW, C_ONE, C_LEV = 0, 128, 256, 384, 512
C_DM = C_LEV + LEVELS * 128
C_QD = C_DM + RH * 128
C_KD = C_QD + RH * 128
C_PW = C_KD + RH
C_ZERO = C_PW + 8
C_END = C_ZERO + 4
ROPE = NT * (DK // 2 + DK)

Q_CONV, Q_BIAS, Q_PRE, Q_MIX = 0, 96, 108, 116
Q_END = Q_MIX + 16
R_A, R_DT, R_D, R_END = 0, NDEC, 2 * NDEC, 2 * NDEC + SH


def constants():
    c = np.zeros((P, C_END), np.float32)
    r = np.arange(P)
    c[:, C_ID:C_ID + P] = np.eye(P)
    c[:, C_UP:C_UP + P] = r[:, None] <= r[None, :]
    c[:, C_LOW:C_LOW + P] = r[:, None] > r[None, :]
    c[:, C_ONE:C_ONE + P] = 1.0
    for k in range(LEVELS):
        b = 1 << k
        same = (r[:, None] // (2 * b)) == (r[None, :] // (2 * b))
        c[:, C_LEV + k * P:C_LEV + (k + 1) * P] = same & (r[:, None] // b % 2 == 0) & (r[None, :] // b % 2 == 1)
    for h, lam in enumerate(LAM):
        rel = (r[None, :] - r[:, None]).astype(np.float64)
        c[:, C_DM + h * P:C_DM + (h + 1) * P] = np.where(rel >= 0, lam ** np.maximum(rel, 0), 0.0) * DK ** -0.5
        c[:, C_QD + h * P:C_QD + (h + 1) * P] = (lam ** (r + 1.0))[None, :]
        c[:, C_KD + h] = lam ** (P - 1.0 - r) * DK ** -0.5
    c[:, C_PW:C_PW + 8] = -0.5
    half = DK // 2
    inv = (np.float32(10000.0) ** (-np.arange(half, dtype=np.float32) / half)).astype(np.float32)
    ang = (np.arange(SEQ, dtype=np.float32)[:, None] * inv[None, :]).astype(np.float32).astype(np.float64)
    ang = ang.reshape(SEQ // P, P, half).transpose(1, 0, 2)
    rope = np.zeros((SEQ // HALF, P, ROPE), np.float32)
    for i in range(SEQ // HALF):
        a = ang[:, i * NT:(i + 1) * NT]
        rope[i, :, :NT * half] = np.cos(a).reshape(P, -1)
        rope[i, :, NT * half:] = np.concatenate([-np.sin(a), np.sin(a)], axis=-1).reshape(P, -1)
    return c, rope


def mixing_steps(p):
    out = [("gdn_decay", p, h) for h in range(GH)]
    for h in range(GH):
        out += [("gdn_turn", p, h), ("gdn_back", p, h), ("gdn_gram", p, h), ("gdn_x0", p, h)]
        for k in range(1, LEVELS):
            out += [("gdn_p", p, h, k), ("gdn_xx", p, h, k)]
        out.append(("gdn_w", p, h))
        for c in range(NT):
            out += [("gdn_v", p, h, c), ("gdn_o", p, h, c)]
        out.append(("gdn_fin", p, h))
    out.append(("bc_turn", p))
    out.append(("mix_turn", p, 0))
    for g in range(SG):
        out.append(("x_turn", p, g))
        out.append(("ssd_l", p, g, 0))
        for c in range(NT):
            out += [("ssd_l", p, g, c + 1)] * (c + 1 < NT) + [("ssd_y", p, g, c)]
        out.append(("ssd_norm", p, g))
        out.append(("mix_turn", p, 1 + g))
    for h in range(RH):
        out += [("ret_turn", p, h), ("ret_s", p, h)] + [("ret_o", p, h, c) for c in range(NT)] + [("ret_fin", p, h)]
    out.append(("mix_turn", p, 3))
    return out


def make_plan():
    mix = [s for p in range(PARTS) for s in mixing_steps(p)]
    plan, done, at, rest = [], set(), [0], [0]
    pause = {"gdn_turn": 4, "gdn_back": 2, "ssd_y": 1, "gdn_gram": 2, "gdn_fin": 1, "ret_turn": 1, "ret_fin": 1, "ssd_norm": 2, "x_turn": 1}
    outs = []

    def emit(s):
        plan.append(s)
        done.add(s)

    def ready(s):
        kind, p = s[0], s[1]
        after = lambda i, half: ("proj", p, i + half, 1 - half, 3)
        need = {"gdn_turn": lambda: after(AT["gdn", (3 * s[2] + 2) // 2], (3 * s[2] + 2) % 2),
                "gdn_decay": lambda: ("small2", p), "gdn_fin": lambda: ("proj", p, AT["gz", s[2] // 2], 1, 3),
                "bc_turn": lambda: after(AT["bc", N_BC - 1], 1),
                "x_turn": lambda: ("proj", p, AT["sz", s[2], N_SZ - 1], 1, 3),
                "ret_turn": lambda: ("proj", p, AT["ret", 2 * s[2] + 1], 1, 3)}.get(kind)
        return need is None or need() in done

    def mix_one(between=True, forced=False):
        s = mix[at[0]]
        if not ready(s):
            return False
        if rest[0] > 0 and not forced:
            rest[0] -= 1
            return False
        if s[0] == "mix_turn" and outs:
            if not between:
                return False
            flush_outs(len(outs))
        at[0] += 1
        emit(s)
        rest[0] = pause.get(s[0], 0)
        if s[0] == "mix_turn":
            outs.extend(("out", s[1], s[2], n, t) for n in range(2) for t in range(NT))
            if s[2] == GROUPS - 1:
                rows = []
                for t in range(NT):
                    rows += [("out", s[1], s[2], 1, t), ("squares", s[1], t)] + [("final", s[1], t - 1)] * (t > 0)
                outs[-NT:] = rows + [("final", s[1], NT - 1)]
        return True

    def mix_until(s):
        while s not in done:
            assert mix_one(True, True), (s, mix[at[0]])
            if rest[0]:
                flush_outs(1)

    def flush_outs(n):
        while outs and n:
            emit(outs.pop(0))
            n -= 1

    for p in range(PARTS):
        if p >= 2:
            while ("final", p - 2, NT - 1) not in done:
                mix_until(("mix_turn", p - 2, 3))
                flush_outs(99)
        for t in range(2):
            if ("scale", p, t) not in done:
                emit(("scale", p, t))
        def norms(t0):
            for t in (t0, t0 + 1):
                emit(("norm", p, t))
                mix_one()

        norms(0)
        for i, piece in enumerate(PIECES):
            for half in range(2):
                if (i, half) == (0, 1):
                    norms(2)
                for s in frees(p, i, half):
                    mix_until(s)
                flush_outs(2)
                if i == len(PIECES) - 1 and p + 1 < PARTS:
                    if p >= 1:
                        while ("final", p - 1, NT - 1) not in done:
                            mix_until(("mix_turn", p - 1, 3))
                            flush_outs(99)
                    emit(("scale", p + 1, half))
                for q in range(4):
                    emit(("proj", p, i, half, q))
                    if i == 0 and half == 0 and q % 2:
                        emit(("scale", p, 2 + q // 2))
                    if mix_one(q == 3) and rest[0] > 1 and outs:
                        flush_outs(1)
                        rest[0] -= 2
                if (i, half) == (0, 1):
                    emit(("small", p))
                if (i, half) == (1, 1):
                    emit(("small2", p))
    while at[0] < len(mix):
        assert mix_one(True, True)
        flush_outs(2)
    flush_outs(99)
    return plan


def slot_of(p, i, half):
    kind = PIECES[i][0]
    if kind == "gdn":
        return 10 * p + (2 * PIECES[i][1] + half) // 3
    if kind == "sx":
        return 10 * p + 4 + PIECES[i][1]
    if kind == "ret":
        return 10 * p + 6 + PIECES[i][1] // 2
    return None


def slot_reader(n):
    p, j = divmod(n, 10)
    if j < 4:
        return ("gdn_turn", p, j)
    if j < 6:
        return ("x_turn", p, j - 4)
    return ("ret_o", p, j - 6, NT - 1)


def gate_of(p, i):
    kind = PIECES[i][0]
    return {"gz": 4 * p, "sz": 4 * p + 1 + (PIECES[i][1] if kind == "sz" else 0), "ret": 4 * p + 3}.get(kind)


def frees(p, i, half):
    need = []
    n = slot_of(p, i, half)
    if n is not None and n >= SLOTS:
        need.append(slot_reader(n - SLOTS))
    g = gate_of(p, i)
    if g is not None and g >= 2:
        need.append(("mix_turn", (g - 2) // 4, (g - 2) % 4))
    if PIECES[i][0] == "bc" and p:
        need.append(("ssd_y", p - 1, SG - 1, NT - 1))
    return need


def bank_uses(step):
    k = step[0]
    if k == "norm":
        return [("mix", (*step, j)) for j in range(2)]
    if k in ("small", "small2", "gdn_decay", "gdn_x0", "gdn_p", "gdn_w", "gdn_v"):
        return [("mix", step)]
    if k == "proj":
        return [("proj", step[:4])] if step[4] == 0 else []
    if k == "out":
        return [("mix", step)]
    if k == "gdn_turn":
        return [("mix", (*step, j)) for j in "qkv"]
    if k == "gdn_back":
        return [("mix", (*step, j)) for j in range(4)]
    if k == "gdn_gram":
        return [("mix", (*step, j)) for j in range(2)]
    if k == "gdn_xx":
        return [("mix", (*step, j)) for j in range(2 if step[3] < LEVELS - 1 else 1)]
    if k == "gdn_o":
        return ([("o", ("gdn_oo", *step[1:3]))] if step[3] == 0 else []) + [("mix", step)]
    if k == "mix_turn":
        return [("mix", (*step, t)) for t in range(NT)]
    if k == "bc_turn":
        return [("mix", (*step, j, g)) for g in range(SG) for j in range(2)]
    if k == "x_turn":
        return [("mix", (*step, c)) for c in range(NT)]
    if k == "ssd_l":
        return [("mix", (*step, j)) for j in range(2)]
    if k == "ssd_y":
        return [("mix", (*step, j)) for j in "zyw"]
    if k == "ret_turn":
        return [("mix", (*step, j)) for j in "qk"]
    if k == "ret_s":
        return [("mix", step)]
    if k == "ret_o":
        return ([("o", ("ret_oo", *step[1:3]))] if step[3] == 0 else []) + [("mix", step)]
    return []


def hybrid_kernel(nc, x, w_in, w_small, w_out, cons, rope, pars, rows, post_norm, out):
    plan = make_plan()
    pools = {"proj": (0, 1), "mix": MIX_BANKS, "o": (7,)}
    counts, bank_of, use_of = {k: 0 for k in pools}, {}, {}
    for s in plan:
        for pool, tag in bank_uses(s):
            banks = pools[pool]
            bank_of[tag] = banks[counts[pool] % len(banks)]
            use_of[tag] = counts[pool] // len(banks)
            counts[pool] += 1

    x1 = nc.dram_tensor("x_mid", (SEQ, D), F32, kind="Internal").ap()

    with ExitStack() as ctx:
        def sb(name, *shape):
            return ctx.enter_context(nc.sbuf_tensor(name, [P, *shape], F32))

        def sem(name):
            return ctx.enter_context(nc.semaphore(name))

        ps = ctx.enter_context(nc.psum_tensor("ps", [P, 8, 512], F32))
        con = sb("con", C_END)
        par = sb("par", DEPTH, Q_END)
        row = sb("row", DEPTH, R_END)
        nega = sb("nega", DEPTH, NDEC)
        xin = sb("xin", 2, D)
        post = sb("post", D)
        rp = sb("rp", ROPE)
        hT = sb("hT", KD, HALF)
        wr = sb("wr", W_RING, KD, PC)
        wsm = sb("wsm", KD, NSM)
        raw = sb("raw", 2, 3 + HALF)
        halo = sb("halo", 24, 3)
        slot = sb("slot", SLOTS, 4 * HALF)
        bc = sb("bc", 4, HALF)
        gate = sb("gate", 2, NT, 512)
        mixT = sb("mixT", 4, HALF)
        acc = sb("acc", NT, D)
        st_g = sb("st_g", GH, P)
        st_s = sb("st_s", SG, 512)
        st_r = sb("st_r", RH, P)
        small = sb("small", 2, NT, NSM)
        beta = sb("beta", 2, NT, GH)
        dt = sb("dt", 2, NT, NDEC)
        dg = sb("dg", 2, NT, NDEC)
        dec = sb("dec", 2, 3, NT, NDEC)
        sm_t = sb("sm_t", 6, NT * NDEC)
        ss = sb("ss", 16)
        fss = sb("fss", NT)
        rs = sb("rs", 16)
        sc = sb("sc", 6, NT)
        gss = sb("gss", 8)
        xss = sb("xss", 4)
        xrs, ssr, frs, sss = sb("xrs", 2), sb("ssr", NT), sb("frs", NT), sb("sss", 2 * NT)
        xf = sb("xf", D)
        xfin = xf[:]
        wk = sb("wk", 12, NT, P)
        et = sb("et", GH, NT, P)
        vnew = sb("vnew", 2, P)
        junk = sb("junk", 2, 512)
        kh, kb, qh, qe, kbe, kdc, vb, kT, kbT, qT, qeT = (wk[:, i] for i in range(11))
        X, XT, PP, wT, bT0, bT1, aT, att = kh, kb, qh, qh, qe, kT, kbT, qT
        lg2 = sb("lg2", 1024)
        xdt1, xw1 = sb("xdt1", 512), sb("xw1", 512)
        flat = wk[:, :, :, :].rearrange("p a c n -> p (a c n)")
        bt = flat[:, 0:1024].rearrange("p (g c n) -> p g c n", g=SG, c=NT)
        gT = flat[:, 1024:2048].rearrange("p (g c n) -> p g c n", g=SG, c=NT)
        xt = flat[:, 2048:4096].rearrange("p (c n) -> p c n", c=NT)
        aU = flat[:, 4096:5120]
        LGs = (flat[:, 5120:6144], lg2[:])
        xdt0, xw0, xD, yy = (et[:, i].rearrange("p c n -> p (c n)") for i in range(4))
        xdt, xw = (xdt0, xdt1[:]), (xw0, xw1[:])
        rqT, rkT, rqd, rS, rkd, rtmp = (flat[:, i * 512:(i + 1) * 512].rearrange("p (c n) -> p c n", c=NT) for i in range(6))
        rot = sb("rot", 2, 512)

        filled = [sem(f"filled{b}") for b in range(8)]
        emptied = [sem(f"emptied{b}") for b in range(8)]
        loaded = sem("consts_loaded")
        w_in_sem = [sem(f"piece_loaded{i}") for i in range(W_RING)]
        wsm_in = sem("small_loaded")
        x_in = [sem(f"x_loaded{i}") for i in range(2)]
        xf_in = [sem(f"xf_loaded{i}") for i in range(2)]
        x_stored = [sem(f"x_stored{t}") for t in range(NT)]
        rope_in, post_in = sem("rope_loaded"), sem("post_loaded")
        act_step, dve_step, pool_step = sem("act_step"), sem("dve_step"), sem("pool_step")
        names = ["nega_ready", "x_squares", "x_mean", "x_rstd", "x_normed", "sm_abs", "sm_exp", "sm_beta_exp", "sm_decays",
                 "conv_done", "silu_done", "gdn_squares", "gdn_sums", "gdn_rstd", "gdn_gu", "gdn_masks", "gdn_xt", "gdn_attn",
                 "gdn_used", "o_squares", "o_mean", "o_rstd", "o_mixed", "ssd_au", "ssd_lg", "ssd_xdt", "ssd_xw", "ssd_xd",
                 "ssd_state", "ssd_ygated", "ssd_squares", "ssd_chunk_squares", "ssd_mean", "ssd_rstd", "ssd_mixed", "ret_rot", "ret_sum", "ret_kd",
                 "gdn_state", "ret_state", "f_squares", "f_rstd", "f_done",
                
                 "states_clear", "bt_free"]
        S = {n: sem(n) for n in names}

        ident = con[:, C_ID:C_ID + P]
        upper = con[:, C_UP:C_UP + P]
        lower = con[:, C_LOW:C_LOW + P]
        ones = con[:, C_ONE:C_ONE + P]
        pw = con[:, C_PW:C_PW + 8]

        def bank(tag):
            return ps[:, bank_of[tag], :]

        def bank4(tag, n=NT):
            return bank(tag).rearrange("p (c n) -> p c n", c=n)

        def wait_filled(eng, tag):
            eng.wait_ge(filled[bank_of[tag]], use_of[tag] + 1)

        def wait_emptied(eng, tag):
            eng.wait_ge(emptied[bank_of[tag]], use_of[tag] + 1)

        def empty(ins, tag):
            ins.then_inc(emptied[bank_of[tag]], 1)

        def over_rows(a, n=NT):
            return a.unsqueeze(1).broadcast_to([P, n, a.shape[1]])

        def over_cols(a, m=P):
            return a.unsqueeze(2).broadcast_to([P, a.shape[1], m])

        def mtile(p, i, half):
            kind = PIECES[i][0]
            if kind == "gdn":
                m = 2 * PIECES[i][1] + half
                n = slot_of(p, i, half)
                return 24 * p + m, m, slot[:, n % SLOTS, (m % 3) * HALF:(m % 3 + 1) * HALF]
            if kind == "bc":
                j = 2 * PIECES[i][1] + half
                return 24 * p + 12 + j, 12 + j, bc[:, j, :]
            if kind == "sx":
                g, j = PIECES[i][1], 2 * PIECES[i][2] + half
                n = slot_of(p, i, half)
                return 24 * p + 16 + 4 * g + j, 16 + 4 * g + j, slot[:, n % SLOTS, j * HALF:(j + 1) * HALF]
            return None

        key_of = lambda s: ("in", s[1], s[2]) if s[0] == "proj" else s[:4]
        pieces, last = [], {}
        for i, s in enumerate(plan):
            if s[0] in ("proj", "out"):
                if key_of(s) not in last:
                    pieces.append(key_of(s))
                last[key_of(s)] = i
        place, held = {}, [None] * W_RING
        turns = [0] * W_RING
        for key in pieces:
            r = min(range(W_RING), key=lambda j: last[held[j]] if held[j] else -1)
            place[key] = (r, turns[r], held[r])
            held[r], turns[r] = key, turns[r] + 1
        block = ctx.enter_context(nc.Block())

        def ssd_before(s):
            m = NT * (SG * s[1] + s[2]) + s[3] - 1
            return ("ssd_y", m // (NT * SG), m // NT % SG, m % NT)

        def slot_wait(eng, n):
            if n is None or n < SLOTS:
                return
            r = slot_reader(n - SLOTS)
            if r[0] == "gdn_turn":
                wait_filled(eng, (*r, "v"))
            elif r[0] == "x_turn":
                wait_filled(eng, (*r, NT - 1))
            else:
                wait_filled(eng, r)

        def gate_wait(eng, G):
            if G >= 2:
                wait_filled(eng, ("mix_turn", (G - 2) // 4, (G - 2) % 4, NT - 1))

        def x_rows(p, t):
            r = (p % 2) * HALF + t * P
            return (x if p < 2 else x1)[r:r + P, :]

        @block.sync
        def _(sp):
            for s in plan:
                k, p = s[0], s[1]
                if k == "scale" and s[2] == 1:
                    if p:
                        wait_filled(sp, ("small", p - 1))
                    sp.dma_start(wsm[:], w_small[p // 2]).then_inc(wsm_in, 16)
                if k == "scale":
                    n = NT * p + s[2]
                    if n >= 2:
                        wait_filled(sp, ("norm", (n - 2) // NT, (n - 2) % NT, 1))
                    if p >= 2:
                        sp.wait_ge(x_stored[s[2]], 16 * (p - 1))
                    sp.dma_start(xin[:, n % 2, :], x_rows(p, s[2])).then_inc(x_in[n % 2], 16)
                key = None
                if k == "proj" and s[3] == 0 and s[4] == 0:
                    key, src = ("in", p, s[2]), w_in[p // 2, s[2]]
                if k == "out" and s[4] == 0:
                    key, src = ("out", p, s[2], s[3]), w_out[p // 2, s[2], s[3]]
                if key:
                    r, _, before = place[key]
                    if before:
                        wait_filled(sp, ("proj", *before[1:], 1) if before[0] == "in" else (*before, NT - 1))
                    sp.dma_start(wr[:, r, :, :].rearrange("p k n -> p (k n)"), src).then_inc(w_in_sem[r], 16)

        def loaded_piece(eng, key):
            r, turn, _ = place[key]
            eng.wait_ge(w_in_sem[r], 16 * (turn + 1))

        @block.tensor
        def _(pe):
            last_use = {}

            def opened(tag):
                if use_of[tag]:
                    pe.wait_ge(emptied[bank_of[tag]], use_of[tag])
                return bank(tag)

            def close(ins, tag):
                ins.then_inc(filled[bank_of[tag]], 1)

            def mm(o, a, b, start=True, stop=True):
                return nc.tensor.matmul(o, a, b, start=start, stop=stop)

            def turn(o, a):
                return nc.tensor.transpose(o, a, ident)

            pe.wait_ge(loaded, 16 * (1 + 2 * DEPTH))
            for s in plan:
                k, p = s[0], s[1]
                if k == "norm":
                    t = s[2]
                    pe.wait_ge(S["x_normed"], NT * p + t + 1)
                    for j in range(2):
                        tag = (*s, j)
                        b = opened(tag)
                        for c in range(4):
                            i = turn(b[:, c * P:(c + 1) * P], xin[:, (NT * p + t) % 2, (4 * j + c) * P:(4 * j + c + 1) * P])
                        close(i, tag)
                elif k == "small":
                    pe.wait_ge(wsm_in, 16 * (p + 1))
                    wait_emptied(pe, ("norm", p, NT - 1, 1))
                    b = opened(s)
                    for t in range(NT):
                        for kk in range(KD):
                            i = mm(b[:, t * NSM:(t + 1) * NSM], hT[:, kk, t * P:(t + 1) * P], wsm[:, kk, :], kk == 0, kk == KD - 1)
                    close(i, s)
                elif k == "small2":
                    pe.wait_ge(S["sm_decays"], p + 1)
                    b = opened(s)
                    n = NT * NDEC
                    for j, m in enumerate((upper, lower, ones)):
                        i = mm(b[:, j * n:(j + 1) * n], m, dg[:, p % 2].rearrange("p t n -> p (t n)"))
                    close(i, s)
                elif k == "proj":
                    i_, half, q = s[2], s[3], s[4]
                    w = wr[:, place["in", p, i_][0]]
                    tag = s[:4]
                    if q == 0:
                        opened(tag)
                        loaded_piece(pe, ("in", p, i_))
                        if i_ == 0:
                            wait_emptied(pe, ("norm", p, 2 * half + 1, 1))
                    b = bank(tag)
                    if PIECES[i_][0] in ("gdn", "bc", "sx"):
                        for kk in (2 * q, 2 * q + 1):
                            i = mm(b, w[:, kk, half * P:(half + 1) * P], hT[:, kk, :], kk == 0, kk == KD - 1)
                    else:
                        t, k0 = 2 * half + q // 2, 4 * (q % 2)
                        for kk in range(k0, k0 + 4):
                            i = mm(b[:, (q // 2) * PC:(q // 2 + 1) * PC], hT[:, kk, t * P:(t + 1) * P], w[:, kk, :],
                                   kk == 0, kk == KD - 1)
                    if q == 3:
                        close(i, tag)
                elif k == "out":
                    G, nh, t = s[2:]
                    w = wr[:, place["out", p, G, nh][0]].rearrange("p k n -> p (k n)").rearrange("p (k n) -> p k n", k=4)
                    b = opened(s)
                    if t == 0:
                        loaded_piece(pe, ("out", p, G, nh))
                    wait_emptied(pe, ("mix_turn", p, G, t))
                    for kk in range(4):
                        i = mm(b, mixT[:, kk, t * P:(t + 1) * P], w[:, kk, :], kk == 0, kk == 3)
                    close(i, s)
                elif k == "gdn_decay":
                    h = s[2]
                    pe.wait_ge(S["gdn_gu"], GH * p + h + 1)
                    b = opened(s)
                    close(mm(b, lower, rot[:, h % 2, :]), s)
                elif k == "gdn_turn":
                    h = s[2]
                    n = 10 * p + h
                    pe.wait_ge(S["silu_done"], 24 * p + 3 * h + 3)
                    for j, name in enumerate("qkv"):
                        tag = (*s, name)
                        b = opened(tag)
                        for c in range(NT):
                            i = turn(b[:, c * P:(c + 1) * P], slot[:, n % SLOTS, j * HALF + c * P:j * HALF + (c + 1) * P])
                        close(i, tag)
                elif k == "gdn_back":
                    h = s[2]
                    wait_emptied(pe, ("gdn_turn", p, h, "k"))
                    for j, src in enumerate((kh, kb, qh, qe)):
                        if j == 2:
                            wait_emptied(pe, ("gdn_turn", p, h, "q"))
                        tag = (*s, j)
                        b = opened(tag)
                        for c in range(NT):
                            i = turn(b[:, c * P:(c + 1) * P], src[:, c, :])
                        close(i, tag)
                elif k == "gdn_gram":
                    h = s[2]
                    for j, src in enumerate((kbT, qT)):
                        wait_emptied(pe, ("gdn_back", p, h, j + 1))
                        tag = (*s, j)
                        b = opened(tag)
                        for c in range(NT):
                            i = mm(b[:, c * P:(c + 1) * P], kT[:, c, :], src[:, c, :])
                        close(i, tag)
                elif k == "gdn_x0":
                    h = s[2]
                    pe.wait_ge(S["gdn_xt"], GH * p + h + 1)
                    b = opened(s)
                    for c in range(NT):
                        i = turn(b[:, c * P:(c + 1) * P], XT[:, c, :])
                    close(i, s)
                elif k == "gdn_p":
                    h, lv = s[2], s[3]
                    wait_emptied(pe, ("gdn_x0", p, h) if lv == 1 else ("gdn_xx", p, h, lv - 1, 1))
                    pe.wait_ge(S["gdn_masks"], (LEVELS - 1) * (GH * p + h) + lv)
                    b = opened(s)
                    for c in range(NT):
                        i = mm(b[:, c * P:(c + 1) * P], (bT0, bT1)[lv % 2][:, c, :], X[:, c, :])
                    close(i, s)
                elif k == "gdn_xx":
                    h, lv = s[2], s[3]
                    wait_emptied(pe, ("gdn_p", p, h, lv))
                    if lv < LEVELS - 1:
                        tag = (*s, 0)
                        b = opened(tag)
                        for c in range(NT):
                            i = mm(b[:, c * P:(c + 1) * P], XT[:, c, :], PP[:, c, :])
                        close(i, tag)
                    tag = (*s, 1 if lv < LEVELS - 1 else 0)
                    b = opened(tag)
                    for c in range(NT):
                        i = mm(b[:, c * P:(c + 1) * P], PP[:, c, :], XT[:, c, :])
                    close(i, tag)
                elif k == "gdn_w":
                    h = s[2]
                    wait_emptied(pe, ("gdn_xx", p, h, LEVELS - 1, 0))
                    b = opened(s)
                    for c in range(NT):
                        i = mm(b[:, c * P:(c + 1) * P], kbe[:, c, :], XT[:, c, :])
                    close(i, s)
                elif k == "gdn_v":
                    h, c = s[2:]
                    first = p % 2 == 0 and c == 0
                    if c == 0:
                        wait_emptied(pe, ("gdn_w", p, h))
                    else:
                        wait_emptied(pe, ("gdn_o", p, h, c - 1))
                    b = opened(s)[:, 0:P]
                    i = mm(b, XT[:, c, :], vb[:, c, :], True, first)
                    if not first:
                        i = mm(b, wT[:, c, :], st_g[:, h, :], False, True)
                    close(i, s)
                elif k == "gdn_o":
                    h, c = s[2:]
                    first = p % 2 == 0 and c == 0
                    oo = ("gdn_oo", p, h)
                    if c == 0:
                        opened(oo)
                        wait_emptied(pe, ("gdn_back", p, h, 3))
                        pe.wait_ge(S["gdn_attn"], GH * p + h + 1)
                    o = bank(oo)[:, c * P:(c + 1) * P]
                    if not first:
                        mm(o, qeT[:, c, :], st_g[:, h, :], True, False)
                    wait_emptied(pe, ("gdn_v", p, h, c))
                    i = mm(o, att[:, c, :], vnew[:, c % 2, :], first, True)
                    if c == NT - 1:
                        close(i, oo)
                    b = opened(s)[:, 0:P]
                    close(mm(b, kdc[:, c, :], vnew[:, c % 2, :]), s)
                elif k == "mix_turn":
                    G = 4 * p + s[2]
                    if s[2] in (0, 3):
                        pe.wait_ge(S["o_mixed"], 8 * p + (4 if s[2] == 0 else 8))
                    else:
                        pe.wait_ge(S["ssd_mixed"], SG * p + s[2])
                    for t in range(NT):
                        tag = (*s, t)
                        b = opened(tag)
                        for j in range(4):
                            i = turn(b[:, j * P:(j + 1) * P], gate[:, G % 2, t, j * P:(j + 1) * P])
                        close(i, tag)
                elif k == "bc_turn":
                    pe.wait_ge(S["silu_done"], 24 * p + 16)
                    for g in range(SG):
                        tag = (*s, 0, g)
                        b = opened(tag)
                        for c in range(NT):
                            i = turn(b[:, c * P:(c + 1) * P], bc[:, g, c * P:(c + 1) * P])
                        close(i, tag)
                        tag = (*s, 1, g)
                        b = opened(tag)
                        for c in range(NT):
                            i = mm(b[:, c * P:(c + 1) * P], bc[:, g, c * P:(c + 1) * P], bc[:, 2 + g, c * P:(c + 1) * P])
                        close(i, tag)
                elif k == "x_turn":
                    g = s[2]
                    n = 10 * p + 4 + g
                    pe.wait_ge(S["silu_done"], 24 * p + 20 + 4 * g)
                    for c in range(NT):
                        tag = (*s, c)
                        b = opened(tag)
                        for j in range(4):
                            i = turn(b[:, j * P:(j + 1) * P], slot[:, n % SLOTS, j * HALF + c * P:j * HALF + (c + 1) * P])
                        close(i, tag)
                elif k == "ssd_l":
                    g, c = s[2:]
                    m = NT * (SG * p + g) + c
                    pe.wait_ge(S["ssd_au"], m + 1)
                    for j in range(2):
                        tag = (*s, j)
                        close(mm(opened(tag), lower, aU[:, j * 512:(j + 1) * 512]), tag)
                elif k == "ssd_y":
                    g, c = s[2:]
                    m = NT * (SG * p + g) + c
                    first = p % 2 == 0 and c == 0
                    tag = (*s, "z")
                    b = opened(tag)
                    if first:
                        pe.wait_ge(S["states_clear"], p // 2 + 1)
                    elif c or p % 2:
                        pe.wait_ge(S["ssd_state"], m if c else m - NT)
                    close(mm(b, bc[:, 2 + g, c * P:(c + 1) * P], st_s[:, g, :]), tag)
                    pe.wait_ge(S["ssd_lg"], m + 1)
                    pe.wait_ge(S["ssd_xdt"], m + 1)
                    LG = LGs[m % 2]
                    tag = (*s, "y")
                    b = opened(tag)
                    for j in range(HG):
                        i = mm(b[:, j * SP:(j + 1) * SP], LG[:, j * P:(j + 1) * P], xdt[m % 2][:, j * SP:(j + 1) * SP])
                    close(i, tag)
                    tag = (*s, "w")
                    b = opened(tag)
                    pe.wait_ge(S["ssd_xw"], m + 1)
                    close(mm(b, bt[:, g, c, :], xw[m % 2]), tag)
                elif k == "ret_turn":
                    h = s[2]
                    pe.wait_ge(S["ret_rot"], 2 * (RH * p + h) + 2)
                    v = slot[:, (10 * p + 6 + h) % SLOTS, 0:1024].rearrange("p (t q n) -> p t q n", t=NT, q=2)
                    for j, name in enumerate("qk"):
                        tag = (*s, name)
                        b = opened(tag)
                        for c in range(NT):
                            i = turn(b[:, c * P:(c + 1) * P], v[:, c, j, :])
                        close(i, tag)
                elif k == "ret_s":
                    h = s[2]
                    wait_emptied(pe, ("ret_turn", p, h, "q"))
                    wait_emptied(pe, ("ret_turn", p, h, "k"))
                    b = opened(s)
                    for c in range(NT):
                        i = mm(b[:, c * P:(c + 1) * P], rkT[:, c, :], rqT[:, c, :])
                    close(i, s)
                elif k == "ret_o":
                    h, c = s[2:]
                    first = p % 2 == 0 and c == 0
                    oo = ("ret_oo", p, h)
                    vv = slot[:, (10 * p + 6 + h) % SLOTS, 1024:1536].rearrange("p (t n) -> p t n", t=NT)
                    if c == 0:
                        opened(oo)
                        wait_emptied(pe, ("ret_s", p, h))
                        wait_emptied(pe, ("proj", p, AT["ret", 2 * h + 1], 1))
                    else:
                        wait_emptied(pe, ("ret_o", p, h, c - 1))
                    o = bank(oo)[:, c * P:(c + 1) * P]
                    if not first:
                        mm(o, rqd[:, c, :], st_r[:, h, :], True, False)
                    i = mm(o, rS[:, c, :], vv[:, c, :], first, True)
                    if c == NT - 1:
                        close(i, oo)
                    if c == 0:
                        pe.wait_ge(S["ret_kd"], RH * p + h + 1)
                    b = opened(s)[:, 0:P]
                    close(mm(b, rkd[:, c, :], vv[:, c, :]), s)

        @block.vector
        def _(dve):
            n_step = [0]

            def chain(ins):
                n_step[0] += 1
                ins.then_inc(dve_step, 1)
                dve.wait_ge(dve_step, n_step[0])

            tt, ts, stt = nc.vector.tensor_tensor, nc.vector.tensor_scalar, nc.vector.scalar_tensor_tensor

            def clear_states():
                nc.vector.memset(st_s[:].rearrange("p a b -> p (a b)"), 0.0).then_inc(S["states_clear"], 1)

            def mean_eps(src, dst, width, name):
                ts(dst, src, 1.0 / width, EPS, ALU.mult, ALU.add).then_inc(S[name], 1)

            conv_at = None
            dve.wait_ge(loaded, 16 * (1 + 2 * DEPTH))
            chain(nc.vector.memset(sm_t[:].rearrange("p a b -> p (a b)"), 0.0))
            clear_states()
            dve.wait_ge(S["nega_ready"], 1)
            chain(ts(nega[:], nega[:], -1.0, None, ALU.mult))
            for s in plan:
                k, p = s[0], s[1]
                l, first_half = p // 2, p % 2 == 0
                if k == "scale":
                    n = NT * p + s[2]
                    dve.wait_ge(S["x_squares"], n + 1)
                    chain(tt(xss[:, 0:1], xss[:, 0:1], xss[:, 1:2], ALU.add))
                    mean_eps(xss[:, 0:1], xss[:, 2:3], D, "x_mean")
                elif k == "norm":
                    t = s[2]
                    for j in range(2):
                        tag = (*s, j)
                        wait_filled(dve, tag)
                        empty(tt(hT[:, 4 * j:4 * j + 4, t * P:(t + 1) * P], bank4(tag),
                                 over_cols(par[:, l, Q_PRE + 4 * j:Q_PRE + 4 * j + 4]), ALU.mult), tag)
                elif k == "small":
                    wait_filled(dve, s)
                    sm = small[:, p % 2]
                    empty(nc.vector.tensor_copy(sm, bank(s)[:, 0:NT * NSM].rearrange("p (t n) -> p t n", t=NT)), s)
                    wait_emptied(dve, s)
                    v = [sm_t[:, i, :].rearrange("p (t n) -> p t n", t=NT) for i in range(6)]
                    a, e, z, q, r, m = v
                    chain(tt(a, sm[:, :, GH:NSM], over_rows(row[:, l, R_DT:R_DT + NDEC]), ALU.add))
                    chain(ts(m, a, -1.0, None, ALU.mult))
                    tt(m, m, a, ALU.max).then_inc(S["sm_abs"], 1)
                    dve.wait_ge(S["sm_exp"], p + 1)
                    chain(ts(q, e, 2.0, None, ALU.add))
                    chain(nc.vector.reciprocal(q, q))
                    chain(tt(q, q, e, ALU.mult))
                    chain(tt(z, q, q, ALU.mult))
                    chain(ts(r, z, 1.0 / 17, None, ALU.mult))
                    for o in (15, 13, 11, 9, 7, 5, 3):
                        chain(stt(r, r, 1.0 / o, z, ALU.add, ALU.mult))
                    chain(stt(r, r, 1.0, q, ALU.add, ALU.mult))
                    chain(ts(a, a, 0.0, None, ALU.max))
                    chain(stt(dt[:, p % 2], r, 2.0, a, ALU.mult, ALU.add))
                    dve.wait_ge(S["sm_beta_exp"], p + 1)
                    chain(ts(beta[:, p % 2], beta[:, p % 2], 1.0, None, ALU.add))
                    chain(nc.vector.reciprocal(beta[:, p % 2], beta[:, p % 2]))
                    tt(dg[:, p % 2], dt[:, p % 2], over_rows(nega[:, l, :]), ALU.mult).then_inc(S["sm_decays"], 1)
                elif k == "proj":
                    i, half, q = s[2], s[3], s[4]
                    tag = s[:4]
                    if conv_at is not None:
                        cp, ci, ch = conv_at
                        n, m, dst = mtile(cp, ci, ch)
                        w = par[:, cp // 2, Q_CONV + TAPS * m:Q_CONV + TAPS * (m + 1)]
                        r, o = raw[:, n % 2, :], dst
                        if q == 0:
                            wait_emptied(dve, ("proj", cp, ci, ch))
                            slot_wait(dve, slot_of(cp, ci, ch))
                            b = par[:, cp // 2, Q_BIAS + m - 12:Q_BIAS + m - 11]
                            ins = (ts(o, r[:, 0:HALF], w[:, 0:1], b, ALU.mult, ALU.add) if m >= 12 else
                                   ts(o, r[:, 0:HALF], w[:, 0:1], None, ALU.mult))
                        else:
                            dve.wait_ge(S["conv_done"], TAPS * n + q)
                            ins = stt(o, r[:, q:q + HALF], w[:, q:q + 1], o, ALU.mult, ALU.add)
                        ins.then_inc(S["conv_done"], 1)
                        if q == TAPS - 1:
                            conv_at = None
                    if q < 3:
                        continue
                    if mtile(p, i, half):
                        conv_at = (p, i, half)
                    elif PIECES[i][0] == "ret" and PIECES[i][1] % 2 == 0:
                        h = PIECES[i][1] // 2
                        m = 2 * (RH * p + h) + half
                        wait_filled(dve, tag)
                        dve.wait_ge(rope_in, 16 * (p + 1))
                        slot_wait(dve, 10 * p + 6 + h)
                        if m >= 1:
                            dve.wait_ge(S["ret_sum"], m)
                        b = bank(tag).rearrange("p (t q e n) -> p t q e n", t=2, q=2, e=2)
                        ns = slot[:, (10 * p + 6 + h) % SLOTS, 0:1024].rearrange("p (t q e n) -> p t q e n", t=NT, q=2, e=2)
                        r0 = rot[:, 0, :].rearrange("p (t q e n) -> p t q e n", t=2, q=2, e=2)
                        r1 = rot[:, 1, :].rearrange("p (t q e n) -> p t q e n", t=2, q=2, e=2)
                        for u in range(2):
                            tile = 2 * half + u
                            co = rp[:, tile * 64:(tile + 1) * 64]
                            si = rp[:, NT * 64 + tile * 128:NT * 64 + (tile + 1) * 128].rearrange("p (e n) -> p e n", e=2)
                            tt(r0[:, u].rearrange("p q e n -> p (q e) n"), b[:, u].rearrange("p q e n -> p (q e) n"),
                               over_rows(co), ALU.mult)
                            ins = tt(r1[:, u], b[:, u, :, ::-1, :],
                                     si.unsqueeze(1).broadcast_to([P, 2, 2, 64]), ALU.mult)
                        empty(ins, tag)
                        wait_emptied(dve, tag)
                        tt(slot[:, (10 * p + 6 + h) % SLOTS, half * 512:half * 512 + 512], rot[:, 0, :], rot[:, 1, :],
                           ALU.add).then_inc(S["ret_sum"], 1)
                        dve.wait_ge(S["ret_sum"], m + 1)
                        dve.sem_inc(S["ret_rot"], 1)
                elif k == "gdn_turn":
                    h = s[2]
                    n = GH * p + h
                    be = beta[:, p % 2, :, h]
                    de = dec[:, p % 2]
                    dve.wait_ge(S["gdn_squares"], n + 1)
                    if n:
                        dve.wait_ge(S["gdn_rstd"], n)
                    nc.vector.tensor_reduce(gss[:], junk[:].rearrange("p q (c n) -> p (q c) n", c=NT), mybir.AxisListType.X,
                                            ALU.add).then_inc(S["gdn_sums"], 1)
                    dve.wait_ge(S["gdn_rstd"], n + 1)
                    wait_emptied(dve, ("small2", p))
                    rq, rk = rs[:, 0:4], rs[:, 4:8]
                    nc.vector.tensor_copy(sc[:, 0, :], rk)
                    tt(sc[:, 1, :], rk, be, ALU.mult)
                    tt(sc[:, 3, :], rk, de[:, 1, :, h], ALU.mult)
                    chain(ts(sc[:, 4, :], rq, DK ** -0.5, None, ALU.mult))
                    tt(sc[:, 2, :], sc[:, 1, :], de[:, 0, :, h], ALU.mult)
                    chain(tt(sc[:, 5, :], sc[:, 4, :], de[:, 0, :, h], ALU.mult))
                    for name, outs in (("k", ((kh, 0), (kb, 1), (kbe, 2), (kdc, 3))), ("q", ((qh, 4), (qe, 5)))):
                        tag = (*s, name)
                        wait_filled(dve, tag)
                        for o, j in outs:
                            ins = tt(o, bank4(tag), over_cols(sc[:, j, :]), ALU.mult)
                        empty(ins, tag)
                    tag = (*s, "v")
                    wait_filled(dve, tag)
                    empty(tt(vb, bank4(tag), over_cols(be), ALU.mult), tag)
                elif k == "gdn_gram":
                    h = s[2]
                    n = GH * p + h
                    wait_emptied(dve, ("gdn_decay", p, h))
                    tag = (*s, 0)
                    wait_filled(dve, tag)
                    if n:
                        dve.wait_ge(S["gdn_masks"], (LEVELS - 1) * n)
                    empty(tt(aT, bank4(tag), et[:, h], ALU.mult), tag)
                    tag = (*s, 1)
                    wait_filled(dve, tag)
                    empty(tt(att, bank4(tag), et[:, h], ALU.mult), tag)
                    wait_emptied(dve, (*s, 0))
                    chain(tt(bT0, aT, over_rows(con[:, C_LEV:C_LEV + P]), ALU.mult))
                    stt(XT, bT0, -1.0, over_rows(ident), ALU.mult, ALU.add).then_inc(S["gdn_xt"], 1)
                elif k == "gdn_xx":
                    h, lv = s[2], s[3]
                    if lv < LEVELS - 1:
                        tag = (*s, 0)
                        wait_filled(dve, tag)
                        wait_emptied(dve, ("gdn_x0", p, h) if lv == 1 else ("gdn_xx", p, h, lv - 1, 1))
                        empty(tt(X, X, bank4(tag), ALU.subtract), tag)
                    tag = (*s, 1 if lv < LEVELS - 1 else 0)
                    wait_filled(dve, tag)
                    if lv == 1:
                        dve.wait_ge(S["gdn_xt"], GH * p + h + 1)
                    empty(tt(XT, XT, bank4(tag), ALU.subtract), tag)
                elif k == "gdn_v":
                    wait_filled(dve, s)
                    empty(nc.vector.tensor_copy(vnew[:, s[3] % 2, :], bank(s)[:, 0:P]), s)
                elif k == "gdn_o":
                    h, c = s[2:]
                    wait_filled(dve, s)
                    if first_half and c == 0:
                        empty(nc.vector.tensor_copy(st_g[:, h, :], bank(s)[:, 0:P]), s)
                    else:
                        if c:
                            wait_emptied(dve, ("gdn_o", p, h, c - 1))
                        empty(stt(st_g[:, h, :], st_g[:, h, :], dec[:, p % 2, 2, c, h:h + 1], bank(s)[:, 0:P],
                                  ALU.mult, ALU.add), s)
                elif k in ("gdn_fin", "ret_fin"):
                    h = s[2]
                    r = k == "ret_fin"
                    n = 8 * p + 4 * r + h
                    G = 4 * p + 3 * r
                    oo = ("ret_oo" if r else "gdn_oo", p, h)
                    dve.wait_ge(S["o_squares"], n + 1)
                    chain(nc.vector.tensor_reduce(ss[:, 2:6], junk[:, 0, :].rearrange("p (c n) -> p c n", c=NT),
                                                  mybir.AxisListType.X, ALU.add))
                    mean_eps(ss[:, 2:6], rs[:, 8:12], P, "o_mean")
                    dve.wait_ge(S["o_rstd"], n + 1)
                    g = gate[:, G % 2, :, h * P:(h + 1) * P]
                    if r:
                        wait_emptied(dve, ("proj", p, AT["ret", 2 * h + 1], 1))
                    else:
                        wait_emptied(dve, ("proj", p, AT["gz", h // 2], 1))
                    chain(tt(g, g, over_cols(rs[:, 12:16]), ALU.mult))
                    empty(tt(g, g, bank4(oo), ALU.mult), oo)
                    wait_emptied(dve, oo)
                    dve.sem_inc(S["o_mixed"], 1)
                elif k == "mix_turn":
                    for t in range(NT):
                        tag = (*s, t)
                        wait_filled(dve, tag)
                        empty(tt(mixT[:, :, t * P:(t + 1) * P], bank4(tag), over_cols(par[:, l, Q_MIX + 4 * s[2]:Q_MIX + 4 * s[2] + 4]),
                                 ALU.mult), tag)
                elif k == "out":
                    G, nh, t = s[2:]
                    wait_filled(dve, s)
                    o = acc[:, t, nh * 512:(nh + 1) * 512]
                    if G == 0:
                        if p:
                            dve.wait_ge(x_stored[t], 16 * p)
                        empty(nc.vector.tensor_copy(o, bank(s)), s)
                    else:
                        wait_emptied(dve, ("out", p, G - 1, nh, t))
                        empty(tt(o, o, bank(s), ALU.add), s)
                elif k == "bc_turn":
                    for g in range(SG):
                        tag = (*s, 1, g)
                        wait_filled(dve, tag)
                        empty(tt(gT[:, g], bank4(tag), over_rows(upper), ALU.mult), tag)
                elif k == "ssd_y":
                    g, c = s[2:]
                    m = NT * (SG * p + g) + c
                    G = 4 * p + 1 + g
                    heads = slice(GH + HG * g, GH + HG * (g + 1))
                    per_head = lambda a: a.unsqueeze(2).broadcast_to([P, HG, SP])
                    v8 = lambda a: a.rearrange("p (h n) -> p h n", h=HG)
                    tag = (*s, "z")
                    wait_filled(dve, tag)
                    if m:
                        dve.wait_ge(S["ssd_ygated"], m)
                    empty(tt(v8(yy), v8(bank(tag)), per_head(dec[:, p % 2, 0, c, heads]), ALU.mult), tag)
                    st = st_s[:, g, :]
                    chain(tt(v8(st), v8(st), per_head(dec[:, p % 2, 2, c, heads]), ALU.mult))
                    wait_emptied(dve, tag)
                    tag = (*s, "y")
                    wait_filled(dve, tag)
                    empty(tt(yy, yy, bank(tag), ALU.add), tag)
                    tag = (*s, "w")
                    wait_filled(dve, tag)
                    empty(tt(st, st, bank(tag), ALU.add), tag)
                    wait_emptied(dve, tag)
                    if first_half is False and c == NT - 1 and g == SG - 1 and l + 1 < DEPTH:
                        clear_states()
                    dve.sem_inc(S["ssd_state"], 1)
                    dve.wait_ge(S["ssd_xd"], m + 1)
                    chain(tt(yy, yy, xD, ALU.add))
                    wait_emptied(dve, ("proj", p, AT["sz", g, N_SZ - 1], 1))
                    tt(gate[:, G % 2, c, :], yy, gate[:, G % 2, c, :], ALU.mult).then_inc(S["ssd_ygated"], 1)
                elif k == "ssd_norm":
                    dve.wait_ge(S["ssd_squares"], SG * p + s[2] + 1)
                    mean_eps(sss[:, 0:NT], sss[:, NT:2 * NT], 512, "ssd_mean")
                elif k == "ssd_l":
                    g, c = s[2:]
                    m = NT * (SG * p + g) + c
                    heads = slice(GH + HG * g, GH + HG * (g + 1))
                    per_head = lambda a: a.unsqueeze(2).broadcast_to([P, HG, SP])
                    v8 = lambda a: a.rearrange("p (h n) -> p h n", h=HG)
                    wait_emptied(dve, ("x_turn", p, g, c))
                    if m >= 2:
                        dve.wait_ge(S["ssd_xw"], m - 1)
                        wait_filled(dve, (*ssd_before(ssd_before(s)), "y"))
                    tt(v8(xdt[m % 2]), v8(xt[:, c, :]), per_head(dt[:, p % 2, c, heads]), ALU.mult).then_inc(S["ssd_xdt"], 1)
                    wait_emptied(dve, ("ssd_l", p, g, c, 1))
                    if c == 0:
                        wait_emptied(dve, ("bc_turn", p, 1, g))
                    L3 = LGs[m % 2].rearrange("p (h n) -> p h n", h=HG)
                    tt(L3, L3, over_rows(gT[:, g, c, :], HG), ALU.mult).then_inc(S["ssd_lg"], 1)
                elif k == "ret_turn":
                    h = s[2]
                    tag = (*s, "q")
                    wait_filled(dve, tag)
                    nc.vector.tensor_copy(rqT, bank4(tag))
                    empty(tt(rqd, bank4(tag), over_rows(con[:, C_QD + h * P:C_QD + (h + 1) * P]), ALU.mult), tag)
                elif k == "ret_s":
                    h = s[2]
                    wait_filled(dve, s)
                    empty(tt(rS, bank4(s), over_rows(con[:, C_DM + h * P:C_DM + (h + 1) * P]), ALU.mult), s)
                elif k == "ret_o":
                    h, c = s[2:]
                    wait_filled(dve, s)
                    if first_half and c == 0:
                        empty(nc.vector.tensor_copy(st_r[:, h, :], bank(s)[:, 0:P]), s)
                    else:
                        if c:
                            wait_emptied(dve, ("ret_o", p, h, c - 1))
                        empty(stt(st_r[:, h, :], st_r[:, h, :], LAM[h] ** P, bank(s)[:, 0:P], ALU.mult, ALU.add), s)
                elif k == "final":
                    t = s[2]
                    n = NT * p + t
                    dve.wait_ge(S["f_rstd"], n + 1)
                    dve.wait_ge(post_in, 16 * (l + 1))
                    chain(stt(acc[:, t, :], acc[:, t, :], frs[:, t:t + 1], post[:], ALU.mult, ALU.mult))
                    dve.wait_ge(xf_in[0], 16 * (n + 1))
                    tt(acc[:, t, :], acc[:, t, :], xfin, ALU.add).then_inc(S["f_done"], 1)

        @block.scalar
        def _(act):
            A = nc.scalar.activation
            n_step = [0]

            def chain(ins):
                n_step[0] += 1
                ins.then_inc(act_step, 1)
                act.wait_ge(act_step, n_step[0])

            silu_at = None
            junk_read = []

            def square_into_junk(read_by):
                if junk_read:
                    act.wait_ge(*junk_read.pop())
                junk_read.append(read_by)

            act.wait_ge(loaded, 16 * (1 + 2 * DEPTH))
            A(nega[:], row[:, :, R_A:R_A + NDEC], ACT.Exp).then_inc(S["nega_ready"], 1)
            for s in plan:
                k, p = s[0], s[1]
                l, first_half = p // 2, p % 2 == 0
                if k == "scale":
                    t = s[2]
                    n = NT * p + t
                    act.wait_ge(x_in[n % 2], 16 * (n // 2 + 1))
                    square_into_junk((S["x_mean"], n + 1))
                    for j in range(2):
                        ins = A(junk[:, j, :], xin[:, n % 2, j * 512:(j + 1) * 512], ACT.Square, accum_out=xss[:, j:j + 1])
                    ins.then_inc(S["x_squares"], 1)
                    act.wait_ge(S["x_rstd"], n + 1)
                    A(xin[:, n % 2, :], xin[:, n % 2, :], ACT.Copy, scale=xrs[:, 0:1]).then_inc(S["x_normed"], 1)
                elif k == "small":
                    act.wait_ge(S["sm_abs"], p + 1)
                    A(sm_t[:, 1, :], sm_t[:, 5, :], ACT.Exp, scale=-1.0).then_inc(S["sm_exp"], 1)
                    A(beta[:, p % 2], small[:, p % 2, :, 0:GH], ACT.Exp, scale=-1.0).then_inc(S["sm_beta_exp"], 1)
                elif k == "small2":
                    wait_filled(act, s)
                    empty(A(dec[:, p % 2].rearrange("p j t n -> p (j t n)"), bank(s)[:, 0:3 * NT * NDEC], ACT.Exp), s)
                elif k == "proj" and s[4] == 3:
                    i, half = s[2], s[3]
                    tag = s[:4]
                    mt = mtile(p, i, half)
                    kind = PIECES[i][0]
                    if silu_at is not None:
                        n, m, dst, sl = silu_at
                        act.wait_ge(S["conv_done"], TAPS * (n + 1))
                        A(dst, dst, ACT.Silu).then_inc(S["silu_done"], 1)
                        silu_at = None
                    if kind != "ret" or PIECES[i][1] % 2:
                        wait_filled(act, tag)
                    if mt:
                        n, m, dst = mt
                        if n >= 2:
                            act.wait_ge(S["conv_done"], TAPS * (n - 1))
                        A(raw[:, n % 2, 0:3], halo[:, m, :] if not first_half else con[:, C_ZERO:C_ZERO + 3], ACT.Copy)
                        if first_half:
                            act.wait_ge(act_step, n_step[0]) if n_step[0] else None
                            A(halo[:, m, :], bank(tag)[:, HALF - 3:HALF], ACT.Copy)
                        empty(A(raw[:, n % 2, 3:3 + HALF], bank(tag), ACT.Copy), tag)
                        silu_at = (n, m, dst, slot_of(p, i, half))
                    elif kind in ("gz", "sz"):
                        j = PIECES[i][-1]
                        G = gate_of(p, i)
                        gate_wait(act, G)
                        empty(A(gate[:, G % 2, 2 * half:2 * half + 2, j * PC:(j + 1) * PC],
                                bank(tag).rearrange("p (t n) -> p t n", t=2), ACT.Silu), tag)
                    elif PIECES[i][1] % 2:
                        h = PIECES[i][1] // 2
                        G = gate_of(p, i)
                        gate_wait(act, G)
                        b = bank(tag).rearrange("p (t n) -> p t n", t=2)
                        v = slot[:, (10 * p + 6 + h) % SLOTS, 1024:1536].rearrange("p (t n) -> p t n", t=NT)
                        slot_wait(act, 10 * p + 6 + h)
                        A(v[:, 2 * half:2 * half + 2, :], b[:, :, 0:P], ACT.Copy)
                        empty(A(gate[:, G % 2, 2 * half:2 * half + 2, h * P:(h + 1) * P], b[:, :, P:2 * P], ACT.Silu), tag)
                elif k == "gdn_decay":
                    wait_filled(act, s)
                    empty(A(et[:, s[2]].rearrange("p c n -> p (c n)"), bank(s), ACT.Exp), s)
                elif k == "gdn_turn":
                    h = s[2]
                    n = GH * p + h
                    square_into_junk((S["gdn_sums"], n + 1))
                    for j, name in enumerate("qk"):
                        tag = (*s, name)
                        wait_filled(act, tag)
                        ins = A(junk[:, j, :], bank(tag), ACT.Square)
                    ins.then_inc(S["gdn_squares"], 1)
                elif k == "gdn_back":
                    for j, o in enumerate((kT, kbT, qT, qeT)):
                        tag = (*s, j)
                        wait_filled(act, tag)
                        empty(A(o, bank4(tag), ACT.Copy), tag)
                elif k == "gdn_x0":
                    wait_filled(act, s)
                    empty(A(X, bank4(s), ACT.Copy), s)
                elif k == "gdn_p":
                    wait_filled(act, s)
                    empty(A(PP, bank4(s), ACT.Copy), s)
                elif k == "gdn_w":
                    wait_filled(act, s)
                    empty(A(wT, bank4(s), ACT.Copy, scale=-1.0), s)
                elif k in ("gdn_fin", "ret_fin"):
                    r = k == "ret_fin"
                    n = 8 * p + 4 * r + s[2]
                    oo = ("ret_oo" if r else "gdn_oo", p, s[2])
                    wait_filled(act, oo)
                    square_into_junk((S["o_mean"], n + 1))
                    A(junk[:, 0, :], bank(oo), ACT.Square).then_inc(S["o_squares"], 1)
                elif k == "bc_turn":
                    if p:
                        pass
                    for g in range(SG):
                        tag = (*s, 0, g)
                        wait_filled(act, tag)
                        if g == 0:
                            wait_filled(act, ("gdn_o", p, GH - 1, NT - 1))
                        empty(A(bt[:, g], bank4(tag), ACT.Copy), tag)
                elif k == "x_turn":
                    g = s[2]
                    if SG * p + g:
                        act.wait_ge(S["ssd_xd"], NT * (SG * p + g))
                        act.wait_ge(S["ssd_xdt"], NT * (SG * p + g))
                    for c in range(NT):
                        tag = (*s, c)
                        wait_filled(act, tag)
                        empty(A(xt[:, c, :], bank(tag), ACT.Copy), tag)
                elif k == "ssd_l":
                    g, c = s[2:]
                    m = NT * (SG * p + g) + c
                    LG = LGs[m % 2]
                    if m >= 2:
                        wait_filled(act, (*ssd_before(ssd_before(s)), "y"))
                    for j in range(2):
                        tag = (*s, j)
                        wait_filled(act, tag)
                        empty(A(LG[:, j * 512:(j + 1) * 512], bank(tag), ACT.Exp), tag)
                elif k == "ssd_norm":
                    n = SG * p + s[2]
                    G = 4 * p + 1 + s[2]
                    if n:
                        act.wait_ge(S["ssd_mean"], n)
                    for c in range(NT):
                        act.wait_ge(S["ssd_ygated"], NT * n + c + 1)
                        square_into_junk((S["ssd_chunk_squares"], (NT - 1) * n + c + 1) if c < NT - 1 else (S["ssd_squares"], n + 1))
                        A(junk[:, 0, :], gate[:, G % 2, c, :], ACT.Square, accum_out=sss[:, c:c + 1])\
                            .then_inc(S["ssd_chunk_squares" if c < NT - 1 else "ssd_squares"], 1)
                    act.wait_ge(S["ssd_rstd"], n + 1)
                    for c in range(NT):
                        ins = A(gate[:, G % 2, c, :], gate[:, G % 2, c, :], ACT.Copy, scale=ssr[:, c:c + 1])
                    ins.then_inc(S["ssd_mixed"], 1)
                elif k == "ret_turn":
                    h = s[2]
                    tag = (*s, "k")
                    wait_filled(act, tag)
                    empty(A(rkT, bank4(tag), ACT.Copy), tag)
                    v = slot[:, (10 * p + 6 + h) % SLOTS, 0:1024].rearrange("p (t q n) -> p t q n", t=NT, q=2)
                    if h:
                        wait_filled(act, ("ret_o", p, h - 1, NT - 1))
                    else:
                        act.wait_ge(S["ssd_mixed"], SG * (p + 1))
                    A(rkd, v[:, :, 1, :], ACT.Copy, scale=con[:, C_KD + h:C_KD + h + 1]).then_inc(S["ret_kd"], 1)
                elif k == "squares":
                    t = s[2]
                    n = NT * p + t
                    wait_emptied(act, ("out", p, GROUPS - 1, 1, t))
                    if p:
                        act.wait_ge(S["f_rstd"], n - NT + 1)
                    square_into_junk((S["f_squares"], n + 1))
                    A(junk[:].rearrange("p a b -> p (a b)"), acc[:, t, :], ACT.Square, accum_out=fss[:, t:t + 1]).then_inc(S["f_squares"], 1)

        @block.gpsimd
        def _(pool):
            tt, ts = nc.gpsimd.tensor_tensor, nc.gpsimd.tensor_scalar
            n_step = [0]

            def chain(ins):
                n_step[0] += 1
                ins.then_inc(pool_step, 1)
                pool.wait_ge(pool_step, n_step[0])

            def mask_level(lv):
                m = con[:, C_LEV + lv * P:C_LEV + (lv + 1) * P]
                tt((bT0, bT1)[lv % 2], aT, over_rows(m), ALU.mult).then_inc(S["gdn_masks"], 1)

            pool.dma_start(con[:], cons).then_inc(loaded, 16)
            for l in range(DEPTH):
                pool.dma_start(par[:, l, :], pars[l]).then_inc(loaded, 16)
                pool.dma_start(row[:, l, :], rows[l].partition_broadcast(P)).then_inc(loaded, 16)
            pool.wait_ge(loaded, 16 * (1 + 2 * DEPTH))
            for s in plan:
                k, p = s[0], s[1]
                if k == "scale":
                    n = NT * p + s[2]
                    pool.wait_ge(S["x_mean"], n + 1)
                    if n:
                        pool.wait_ge(S["x_normed"], n)
                    tt(xrs[:, 0:1], xss[:, 2:3], pw[:, 0:1], ALU.pow).then_inc(S["x_rstd"], 1)
                elif k == "gdn_decay":
                    h = s[2]
                    if h == 0:
                        pool.wait_ge(S["sm_decays"], p + 1)
                        if p:
                            pool.wait_ge(S["ret_sum"], 2 * RH * p)
                        pool.dma_start(rp[:], rope[p % 2]).then_inc(rope_in, 16)
                    if h >= 2:
                        wait_filled(pool, ("gdn_decay", p, h - 2))
                    tt(rot[:, h % 2, :].rearrange("p (c n) -> p c n", c=NT), over_rows(upper), over_cols(dg[:, p % 2, :, h]),
                       ALU.mult).then_inc(S["gdn_gu"], 1)
                elif k == "gdn_turn":
                    n = GH * p + s[2]
                    pool.wait_ge(S["gdn_sums"], n + 1)
                    if n:
                        wait_emptied(pool, ("gdn_turn", (n - 1) // GH, (n - 1) % GH, "q"))
                    chain(ts(gss[:, :], gss[:, :], EPS, None, ALU.add))
                    tt(rs[:, 0:8], gss[:, :], pw, ALU.pow).then_inc(S["gdn_rstd"], 1)
                elif k == "gdn_gram":
                    h = s[2]
                    for lv in (1, 2):
                        if lv == 2:
                            pool.wait_ge(S["gdn_xt"], GH * p + h + 1)
                        if lv == 1:
                            wait_emptied(pool, (*s, 1))
                            tt(att, att, over_rows(upper), ALU.mult).then_inc(S["gdn_attn"], 1)
                        mask_level(lv)
                elif k == "gdn_p" and s[3] + 2 < LEVELS:
                    wait_filled(pool, s)
                    mask_level(s[3] + 2)
                elif k in ("gdn_fin", "ret_fin"):
                    n = 8 * p + 4 * (k == "ret_fin") + s[2]
                    pool.wait_ge(S["o_mean"], n + 1)
                    if n:
                        pool.wait_ge(S["o_mixed"], n)
                    tt(rs[:, 12:16], rs[:, 8:12], pw[:, 0:4], ALU.pow).then_inc(S["o_rstd"], 1)
                elif k == "ssd_l":
                    g, c = s[2:]
                    m = NT * (SG * p + g) + c
                    heads = slice(GH + HG * g, GH + HG * (g + 1))
                    if m:
                        wait_filled(pool, ("ssd_l", *ssd_before(s)[1:], 1))
                    if g == 0 and c == 0:
                        wait_filled(pool, ("gdn_o", p, GH - 1, NT - 1))
                    tt(aU.rearrange("p (h n) -> p h n", h=HG), over_rows(upper, HG), over_cols(dg[:, p % 2, c, heads]),
                       ALU.mult).then_inc(S["ssd_au"], 1)
                    per_head = lambda a: a.unsqueeze(2).broadcast_to([P, HG, SP])
                    v8 = lambda a: a.rearrange("p (h n) -> p h n", h=HG)
                    pool.wait_ge(S["ssd_xdt"], m + 1)
                    if m >= 2:
                        wait_filled(pool, (*ssd_before(ssd_before(s)), "w"))
                    tt(v8(xw[m % 2]), v8(xdt[m % 2]), per_head(dec[:, p % 2, 1, c, heads]), ALU.mult).then_inc(S["ssd_xw"], 1)
                elif k == "ssd_y":
                    g, c = s[2:]
                    m = NT * (SG * p + g) + c
                    heads = slice(GH + HG * g, GH + HG * (g + 1))
                    per_head = lambda a: a.unsqueeze(2).broadcast_to([P, HG, SP])
                    v8 = lambda a: a.rearrange("p (h n) -> p h n", h=HG)
                    if m:
                        pool.wait_ge(S["ssd_ygated"], m)
                    tt(v8(xD), v8(xt[:, c, :]), per_head(row[:, p // 2, R_D + HG * g:R_D + HG * (g + 1)]), ALU.mult)\
                        .then_inc(S["ssd_xd"], 1)
                elif k == "ssd_norm":
                    n = SG * p + s[2]
                    pool.wait_ge(S["ssd_mean"], n + 1)
                    if n:
                        pool.wait_ge(S["ssd_mixed"], n)
                    tt(ssr[:], sss[:, NT:2 * NT], pw[:, 0:NT], ALU.pow).then_inc(S["ssd_rstd"], 1)
                elif k == "squares":
                    t = s[2]
                    n = NT * p + t
                    if t == 0:
                        if n:
                            pool.wait_ge(S["f_done"], n)
                        if n % (2 * NT) == 0:
                            pool.dma_start(post[:], post_norm[p // 2].partition_broadcast(P)).then_inc(post_in, 16)
                        pool.dma_start(xfin, x_rows(p, 0)).then_inc(xf_in[0], 16)
                    pool.wait_ge(S["f_squares"], n + 1)
                    chain(ts(fss[:, t:t + 1], fss[:, t:t + 1], 1.0 / D, EPS, ALU.mult, ALU.add))
                    if p:
                        pool.wait_ge(S["f_done"], n - NT + 1)
                    tt(frs[:, t:t + 1], fss[:, t:t + 1], pw[:, 0:1], ALU.pow).then_inc(S["f_rstd"], 1)
                elif k == "final":
                    t = s[2]
                    n = NT * p + t
                    pool.wait_ge(S["f_done"], n + 1)
                    if t + 1 < NT:
                        pool.dma_start(xfin, x_rows(p, t + 1)).then_inc(xf_in[0], 16)
                    r = (p % 2) * HALF + t * P
                    pool.dma_start((x1 if p < 2 else out)[r:r + P, :], acc[:, t, :]).then_inc(x_stored[t], 16)
            for t in range(NT):
                pool.wait_ge(x_stored[t], 16 * PARTS)


def kernel(**inputs):
    import concourse.bacc as bacc
    from concourse.bass_utils import run_bass_kernel_spmd

    f = {k: np.asarray(v) for k, v in inputs.items()}
    w, wo = f["w_in"], f["w_out"]
    at = np.cumsum([0, 512, 512, 512, 512, 4, 4, 1024, 256, 256, 1024, 16, 512, 512, 512, 512])
    gq, gk, gv, gz, gb, ga, sx, sB, sC, sz, sdt, rq, rk, rv, rg = [w[:, :, a:b] for a, b in zip(at[:-1], at[1:])]
    h128 = lambda a, h: a[:, :, h * P:(h + 1) * P]
    heads = [t for h in range(GH) for t in (h128(gq, h), h128(gk, h), h128(gv, h))]
    cols = [gz[:, :, :PC]] + heads[:8] + [gz[:, :, PC:]] + heads[8:] + [sB, sC]
    for g in range(SG):
        cols += [sx[:, :, g * 512:(g + 1) * 512], sz[:, :, g * 512:(g + 1) * 512]]
    cols += [t for h in range(RH) for t in (h128(rq, h), h128(rk, h), h128(rv, h), h128(rg, h))]
    wl = np.concatenate(cols, axis=2)
    n_pc = len(PIECES)
    wl = wl.reshape(DEPTH, KD, P, n_pc, PC).transpose(0, 3, 2, 1, 4).reshape(DEPTH, n_pc, P, KD * PC)
    ws = np.concatenate([gb, ga, sdt], axis=2).reshape(DEPTH, KD, P, NSM).transpose(0, 2, 1, 3)
    wol = wo.reshape(DEPTH, GROUPS, 4, P, 2, 512).transpose(0, 1, 4, 3, 2, 5).reshape(DEPTH, GROUPS, 2, P, 2048)
    pars = np.zeros((DEPTH, P, Q_END), np.float32)
    gc, scv = f["gdn_conv"], f["ssd_conv"]
    tiles = [gc[:, :, j * 512 + h * P:j * 512 + (h + 1) * P] for h in range(GH) for j in range(3)]
    tiles += [scv[:, :, 1024 + j * P:1024 + (j + 1) * P] for j in range(4)] + [scv[:, :, j * P:(j + 1) * P] for j in range(8)]
    bias = f["ssd_conv_b"]
    bts = [bias[:, 1024 + j * P:1024 + (j + 1) * P] for j in range(4)] + [bias[:, j * P:(j + 1) * P] for j in range(8)]
    for m, t in enumerate(tiles):
        pars[:, :, Q_CONV + TAPS * m:Q_CONV + TAPS * (m + 1)] = t.transpose(0, 2, 1)
    for m, t in enumerate(bts):
        pars[:, :, Q_BIAS + m] = t
    pars[:, :, Q_PRE:Q_PRE + KD] = f["pre_norm"].reshape(DEPTH, KD, P).transpose(0, 2, 1)
    pars[:, :, Q_MIX:Q_MIX + 4] = f["gdn_norm"][:, :, None]
    pars[:, :, Q_MIX + 4:Q_MIX + 12] = f["ssd_norm"].reshape(DEPTH, 8, P).transpose(0, 2, 1)
    pars[:, :, Q_MIX + 12:Q_MIX + 16] = f["ret_norm"][:, :, None]
    rows = np.concatenate([f["gdn_A_log"], f["ssd_A_log"], f["gdn_dt_bias"], f["ssd_dt_bias"], f["ssd_D"]], axis=1)
    cons, rope = constants()

    nc = bacc.Bacc("TRN2", target_bir_lowering=False, num_devices=1)
    arrays = {"x": f["x"].reshape(SEQ, D), "w_in": wl, "w_small": ws, "w_out": wol, "cons": cons, "rope": rope, "pars": pars, "rows": rows,
              "post": f["post_norm"]}
    arrays = {f"in_{k}": np.ascontiguousarray(v) for k, v in arrays.items()}
    args = [nc.dram_tensor(k, v.shape, mybir.dt.from_np(v.dtype), kind="ExternalInput").ap() for k, v in arrays.items()]
    out = nc.dram_tensor("out_0", (SEQ, D), F32, kind="ExternalOutput").ap()
    hybrid_kernel(nc, *args, out)
    r = run_bass_kernel_spmd(nc, [arrays], core_ids=[0])
    return r.results[0]["out_0"].reshape(1, SEQ, D)
```

```python
from contextlib import ExitStack

import numpy as np

import concourse.bass as bass
from concourse import mybir

ALU = mybir.AluOpType
ACT = mybir.ActivationFunctionType
F32 = mybir.dt.float32
F32R = mybir.dt.float32r

P = 128
D, SEQ, DEPTH = 1024, 1024, 2
HALF = 512
NT = HALF // P
KD = D // P
PARTS = DEPTH * SEQ // HALF
EPS = 1e-6
GH, SH, RH = 4, 16, 4
SG, SP = 2, 64
HG = SH // SG
DK = 128
NDEC = GH + SH
NSM = GH + NDEC
LEVELS = 7
TAPS = 4
GROUPS = 4

PC = 256
N_GDN_PC, N_GZ, N_BC, N_SZ, N_SX, N_RET = 6, 2, 2, 2, 2, 8
PIECES = ([("gz", 0)] + [("gdn", i) for i in range(4)] + [("gz", 1)] + [("gdn", i) for i in range(4, N_GDN_PC)]
          + [("bc", i) for i in range(N_BC)]
          + [(k, g, i) for g in range(SG) for k, n in (("sx", N_SX), ("sz", N_SZ)) for i in range(n)]
          + [("ret", i) for i in range(N_RET)])
AT = {piece: i for i, piece in enumerate(PIECES)}
W_RING = 2
Q = KD
SBUF = 224 * 1024 - 1
UNITS = D // PC
SLOTS = 2
MIX_BANKS = (2, 3, 4, 5, 6)
LAM = [1.0 - 2.0 ** (-5.0 - h) for h in range(RH)]

C_ID, C_UP, C_LOW, C_ONE, C_LEV = 0, 128, 256, 384, 512
C_DM = C_LEV + LEVELS * 128
C_QD = C_DM + RH * 128
C_KD = C_QD + RH * 128
C_PW = C_KD + RH
C_ZERO = C_PW + 8
C_END = C_ZERO + 4
ROPE = NT * (DK // 2 + DK)

Q_CONV, Q_BIAS, Q_PRE, Q_MIX = 0, 96, 108, 116
Q_END = Q_MIX + 16
R_A, R_DT, R_D, R_END = 0, NDEC, 2 * NDEC, 2 * NDEC + SH


def constants():
    c = np.zeros((P, C_END), np.float32)
    r = np.arange(P)
    c[:, C_ID:C_ID + P] = np.eye(P)
    c[:, C_UP:C_UP + P] = r[:, None] <= r[None, :]
    c[:, C_LOW:C_LOW + P] = r[:, None] > r[None, :]
    c[:, C_ONE:C_ONE + P] = 1.0
    for k in range(LEVELS):
        b = 1 << k
        same = (r[:, None] // (2 * b)) == (r[None, :] // (2 * b))
        c[:, C_LEV + k * P:C_LEV + (k + 1) * P] = same & (r[:, None] // b % 2 == 0) & (r[None, :] // b % 2 == 1)
    for h, lam in enumerate(LAM):
        rel = (r[None, :] - r[:, None]).astype(np.float64)
        c[:, C_DM + h * P:C_DM + (h + 1) * P] = np.where(rel >= 0, lam ** np.maximum(rel, 0), 0.0) * DK ** -0.5
        c[:, C_QD + h * P:C_QD + (h + 1) * P] = (lam ** (r + 1.0))[None, :]
        c[:, C_KD + h] = lam ** (P - 1.0 - r) * DK ** -0.5
    c[:, C_PW:C_PW + 8] = -0.5
    half = DK // 2
    inv = (np.float32(10000.0) ** (-np.arange(half, dtype=np.float32) / half)).astype(np.float32)
    ang = (np.arange(SEQ, dtype=np.float32)[:, None] * inv[None, :]).astype(np.float32).astype(np.float64)
    ang = ang.reshape(SEQ // P, P, half).transpose(1, 0, 2)
    rope = np.zeros((SEQ // HALF, P, ROPE), np.float32)
    for i in range(SEQ // HALF):
        a = ang[:, i * NT:(i + 1) * NT]
        rope[i, :, :NT * half] = np.cos(a).reshape(P, -1)
        rope[i, :, NT * half:] = np.concatenate([-np.sin(a), np.sin(a)], axis=-1).reshape(P, -1)
    return c, rope


def mixing_steps(p):
    out = [("gdn_decay", p, h) for h in range(GH)]
    for h in range(GH):
        out += [("gdn_turn", p, h), ("gdn_back", p, h), ("gdn_gram", p, h), ("gdn_x0", p, h)]
        for k in range(1, LEVELS):
            out += [("gdn_p", p, h, k), ("gdn_xx", p, h, k)]
        out.append(("gdn_w", p, h))
        for c in range(NT):
            out += [("gdn_v", p, h, c), ("gdn_o", p, h, c)]
        out.append(("gdn_fin", p, h))
    for g in range(SG):
        out.append(("bc_turn", p, g))
        out.append(("mix_turn", p, g))
        out.append(("x_turn", p, g))
        out.append(("ssd_l", p, g, 0))
        for c in range(NT):
            out += [("ssd_l", p, g, c + 1)] * (c + 1 < NT) + [("ssd_y", p, g, c)]
        out.append(("ssd_norm", p, g))
    out.append(("mix_turn", p, SG))
    for h in range(RH):
        out += [("ret_turn", p, h), ("ret_s", p, h)] + [("ret_o", p, h, c) for c in range(NT)] + [("ret_fin", p, h)]
    out.append(("mix_turn", p, 3))
    return out


def make_plan():
    mix = [s for p in range(PARTS) for s in mixing_steps(p)]
    plan, done, at, rest = [], set(), [0], [0]
    pause = {"gdn_turn": 10, "gdn_back": 6, "ssd_y": 3, "gdn_gram": 5, "gdn_fin": 3, "ret_turn": 3, "ret_fin": 4, "ssd_norm": 7, "x_turn": 3,
             "gdn_decay": 3, "gdn_v": 0, "gdn_o": 0, "ret_o": 1}
    outs = []

    def emit(s):
        plan.append(s)
        done.add(s)

    def ready(s):
        kind, p = s[0], s[1]
        after = lambda i, half: ("proj", p, i + half, 1 - half, Q - 1)
        need = {"gdn_turn": lambda: after(AT["gdn", (3 * s[2] + 2) // 2], (3 * s[2] + 2) % 2),
                "gdn_decay": lambda: ("small2", p), "gdn_fin": lambda: ("proj", p, AT["gz", s[2] // 2], 1, Q - 1),
                "bc_turn": lambda: after(AT["bc", N_BC - 1], 1),
                "x_turn": lambda: ("proj", p, AT["sz", s[2], N_SZ - 1], 1, Q - 1),
                "ret_turn": lambda: ("proj", p, AT["ret", 2 * s[2] + 1], 1, Q - 1)}.get(kind)
        return need is None or need() in done

    def mix_one(forced=False):
        s = mix[at[0]]
        if not ready(s):
            return False
        if rest[0] > 0 and not forced:
            rest[0] -= 1
            return False
        if s[0] == "mix_turn" and outs:
            flush_outs(len(outs))
        at[0] += 1
        emit(s)
        rest[0] = 4 if s[0] == "ssd_l" and s[3] == 0 else pause.get(s[0], 1)
        if s[0] == "mix_turn":
            outs.extend(("out", s[1], s[2], u, tp) for u in range(UNITS) for tp in range(NT // 2))
            if s[2] == GROUPS - 1:
                q = s[1]
                outs[-1:] = [("squares", q, 0), ("squares", q, 1), outs[-1], ("final", q, 0), ("squares", q, 2),
                             ("final", q, 1), ("squares", q, 3), ("final", q, 2), ("final", q, 3)]
        return True

    def mix_until(s):
        while s not in done:
            assert mix_one(True), (s, mix[at[0]])
            if rest[0] > 1:
                flush_outs(1)

    def flush_outs(n):
        while outs and n:
            emit(outs.pop(0))
            n -= 1

    for p in range(PARTS):
        if p >= 2:
            while ("final", p - 2, NT - 1) not in done:
                mix_until(("mix_turn", p - 2, 3))
                flush_outs(99)
        if p == 0:
            emit(("scale", 0, 0))
            emit(("scale", 0, 1))
            for j in range(4):
                emit(("split", 0, 0, j))
            for t in range(NT):
                emit(("norm", 0, t))
                if t < 2:
                    emit(("scale", 0, t + 2))
        for i, piece in enumerate(PIECES):
            for half in range(2):
                if p + 1 < PARTS and (i, half) == (len(PIECES) - 1, 1):
                    for t in range(2):
                        emit(("norm", p + 1, t))
                        mix_one()
                if p and (i, half) == (0, 0):
                    emit(("norm", p, 2))
                    mix_one()
                if piece[0] == "bc" and p:
                    while ("final", p - 1, NT - 1) not in done:
                        mix_until(("mix_turn", p - 1, 3))
                        flush_outs(99)
                for s in frees(p, i, half):
                    mix_until(s)
                flush_outs(1)
                if i == len(PIECES) - 2 and p + 1 < PARTS:
                    if p >= 1:
                        while ("final", p - 1, NT - 1) not in done:
                            mix_until(("mix_turn", p - 1, 3))
                            flush_outs(99)
                    emit(("scale", p + 1, half))
                for q in range(Q):
                    j, odd = divmod(Q * half + q - 6, 2)
                    if 0 <= j < 4 and not odd and (p, i) != (PARTS - 1, len(PIECES) - 1):
                        emit(("split", *((p, i + 1) if i + 1 < len(PIECES) else (p + 1, 0)), j))
                    emit(("proj", p, i, half, q))
                    if p + 1 < PARTS and (i, half) == (len(PIECES) - 1, 1) and q in (3, Q - 1):
                        emit(("scale", p + 1, 2 + (q > 3)))
                    if p and (i, half, q) == (0, 0, 1):
                        emit(("norm", p, 3))
                    if (i, half, q) == (0, 1, 3):
                        emit(("split_small", p))
                    if (i, half, q) == (1, 0, 1):
                        emit(("small_turn", p))
                    if (i, half, q) == (2, 0, 3):
                        emit(("small2", p))
                    if mix_one() and rest[0] > 2 and outs:
                        flush_outs(1)
                        rest[0] -= 4
                if (i, half) == (0, 1):
                    emit(("small", p))
    while at[0] < len(mix):
        assert mix_one(True)
        flush_outs(1)
    flush_outs(99)
    return plan


def slot_of(p, i, half):
    kind = PIECES[i][0]
    if kind == "gdn":
        return 10 * p + (2 * PIECES[i][1] + half) // 3
    if kind == "sx":
        return 10 * p + 4 + PIECES[i][1]
    if kind == "ret":
        return 10 * p + 6 + PIECES[i][1] // 2
    return None


def slot_reader(n):
    p, j = divmod(n, 10)
    if j < 4:
        return ("gdn_turn", p, j)
    if j < 6:
        return ("x_turn", p, j - 4)
    return ("ret_o", p, j - 6, NT - 1)


def gate_of(p, i):
    kind = PIECES[i][0]
    return {"gz": 4 * p, "sz": 4 * p + 1 + (PIECES[i][1] if kind == "sz" else 0), "ret": 4 * p + 3}.get(kind)


def frees(p, i, half):
    need = []
    n = slot_of(p, i, half)
    if n is not None and n >= SLOTS:
        need.append(slot_reader(n - SLOTS))
    g = gate_of(p, i)
    if g is not None and g >= 2:
        need.append(("mix_turn", (g - 2) // 4, (g - 2) % 4))
    if PIECES[i][0] == "bc" and p:
        need.append(("ssd_y", p - 1, SG - 1, NT - 1))
    return need


def bank_uses(step):
    k = step[0]
    if k == "norm":
        return [("mix", (*step, j)) for j in range(2)]
    if k in ("small", "small_turn", "small2", "gdn_decay", "gdn_x0", "gdn_p", "gdn_w", "gdn_v"):
        return [("mix", step)]
    if k == "proj":
        return [("proj", step[:4])] if step[4] == 0 else []
    if k == "out":
        return [("mix", step)]
    if k == "gdn_turn":
        return [("mix", (*step, j)) for j in "qkv"]
    if k == "gdn_back":
        return [("mix", (*step, j)) for j in range(4)]
    if k == "gdn_gram":
        return [("mix", (*step, j)) for j in range(2)]
    if k == "gdn_xx":
        return [("mix", (*step, j)) for j in range(2 if step[3] < LEVELS - 1 else 1)]
    if k == "gdn_o":
        return ([("o", ("gdn_oo", *step[1:3]))] if step[3] == 0 else []) + [("mix", step)]
    if k == "mix_turn":
        return [("mix", (*step, t)) for t in range(NT)]
    if k == "bc_turn":
        return [("mix", (*step, j)) for j in range(2)]
    if k == "x_turn":
        return [("mix", (*step, c)) for c in range(NT)]
    if k == "ssd_l":
        return [("mix", (*step, j)) for j in range(2)]
    if k == "ssd_y":
        return [("mix", (*step, j)) for j in "zyw"]
    if k == "ret_turn":
        return [("mix", (*step, j)) for j in "qk"]
    if k == "ret_s":
        return [("mix", step)]
    if k == "ret_o":
        return ([("o", ("ret_oo", *step[1:3]))] if step[3] == 0 else []) + [("mix", step)]
    return []


def hybrid_kernel(nc, x, w_in, w_small, w_out, cons, rope, pars, rows, post_norm, out):
    plan = make_plan()
    pools = {"proj": (0, 1), "mix": MIX_BANKS, "o": (7,)}
    counts, bank_of, use_of = {k: 0 for k in pools}, {}, {}
    for s in plan:
        for pool, tag in bank_uses(s):
            banks = pools[pool]
            bank_of[tag] = banks[counts[pool] % len(banks)]
            use_of[tag] = counts[pool] // len(banks)
            counts[pool] += 1

    x1 = nc.dram_tensor("x_mid", (SEQ, D), F32, kind="Internal").ap()

    with ExitStack() as ctx:
        def sb(name, *shape, dtype=F32):
            return ctx.enter_context(nc.sbuf_tensor(name, [P, *shape], dtype))

        def sem(name):
            return ctx.enter_context(nc.semaphore(name))

        ps = ctx.enter_context(nc.psum_tensor("ps", [P, 8, 512], F32))
        at = -(-(SBUF - nc.sbuf_bytes_remaining) // 32) * 32
        sb("weights", W_RING * KD * PC + 2 * 4 * PC)
        wr = nc.alloc_sbuf_tensor_at("w_loaded", [P, W_RING, KD * PC], F32, offset=at)
        w_lo = nc.alloc_sbuf_tensor_at("w_low", [P, W_RING, KD * PC], F32R, offset=at)
        at += 4 * W_RING * KD * PC
        wo = nc.alloc_sbuf_tensor_at("wo_loaded", [P, 2, 4 * PC], F32, offset=at)
        wo_parts = nc.alloc_sbuf_tensor_at("wo_parts", [P, 2, 4 * PC], F32R, offset=at)
        con = sb("con", C_END)
        par = sb("par", DEPTH, Q_END)
        row = sb("row", DEPTH, R_END)
        nega = sb("nega", DEPTH, NDEC)
        rp = sb("rp", ROPE)
        hT_hi, hT_lo = sb("hT_hi", KD, HALF, dtype=F32R), sb("hT_lo", KD, HALF, dtype=F32R)
        w_hi = sb("w_hi", W_RING, KD * PC, dtype=F32R)
        raw = sb("raw", 2, 3 + HALF)
        halo = sb("halo", 24, 3)
        slot = sb("slot", SLOTS, 4 * HALF)
        bc = sb("bc", 4, HALF)
        xfin, post = (bc[:, 2 * i:2 * i + 2, :].rearrange("p a b -> p (a b)") for i in range(2))
        gate = sb("gate", 2, NT, 512)
        mixT = sb("mixT", 4, HALF)
        acc = sb("acc", NT, D)
        st_g = sb("st_g", GH, P)
        st_s = sb("st_s", SG, 512)
        st_r = sb("st_r", RH, P)
        beta = sb("beta", NT, GH)
        dt = sb("dt", NT, NDEC)
        dg = sb("dg", NT, NDEC)
        dec = sb("dec", 3, NT, NDEC)
        ss = sb("ss", 16)
        fss = sb("fss", NT)
        rs = sb("rs", 16)
        sc = sb("sc", 6, NT)
        gss = sb("gss", 8)
        xss = sb("xss", 4)
        xrs, ssr, frs, sss = sb("xrs", 2), sb("ssr", NT), sb("frs", NT), sb("sss", 2 * NT)
        wk = sb("wk", 12, NT, P)
        et = sb("et", GH, NT, P)
        vnew = sb("vnew", 2, P)
        junk = sb("junk", 2, 512)
        kh, kb, qh, qe, kbe, kdc, vb, kT, kbT, qT, qeT = (wk[:, i] for i in range(11))
        X, XT, PP, wT, bT0, bT1, aT, att = kh, kb, qh, qh, qe, kT, kbT, qT
        xdt1, xw1 = sb("xdt1", 512), sb("xw1", 512)
        flat = wk[:, :, :, :].rearrange("p a c n -> p (a c n)")
        bt = flat[:, 0:512].rearrange("p (c n) -> p c n", c=NT)
        gT = flat[:, 512:1024].rearrange("p (c n) -> p c n", c=NT)
        xt = flat[:, 1024:3072].rearrange("p (c n) -> p c n", c=NT)
        aU = flat[:, 3072:4096]
        LGs = (flat[:, 4096:5120], flat[:, 5120:6144])
        xdt0, xw0, xD, yy = (et[:, i].rearrange("p c n -> p (c n)") for i in range(4))
        xdt, xw = (xdt0, xdt1[:]), (xw0, xw1[:])
        rqT, rkT, rqd, rS, rkd = (flat[:, i * 512:(i + 1) * 512].rearrange("p (c n) -> p c n", c=NT) for i in range(5))
        xin = flat[:, 3584:3584 + 2 * D].rearrange("p (a b) -> p a b", a=2)
        sm_t = flat[:, 3584 + 2 * D:3584 + 2 * D + 6 * NT * NDEC].rearrange("p (a b) -> p a b", a=6)
        gu = (flat[:, 2560:3072], flat[:, 3072:3584])
        smT = flat[0:NSM, 2560:3072]
        small = flat[:, 3072:3072 + NT * NSM].rearrange("p (t n) -> p t n", t=NT)
        rot = sb("rot", 512)

        filled = [sem(f"filled{b}") for b in range(8)]
        emptied = [sem(f"emptied{b}") for b in range(8)]
        loaded = sem("consts_loaded")
        w_in_sem = [sem(f"piece_loaded{i}") for i in range(W_RING)]
        wo_in = [sem(f"unit_loaded{i}") for i in range(2)]
        x_in = [sem(f"x_loaded{i}") for i in range(2)]
        xf_in = sem("xf_loaded")
        x_stored = [sem(f"x_stored{t}") for t in range(NT)]
        rope_in, post_in = sem("rope_loaded"), sem("post_loaded")
        act_step, dve_step, pool_step = sem("act_step"), sem("dve_step"), sem("pool_step")
        names = ["nega_ready", "x_squares", "x_rstd", "x_normed", "sm_abs", "sm_exp", "sm_beta_exp", "sm_decays",
                 "conv_begun", "conv_done", "gdn_k_scaled", "silu_done", "gdn_squares", "gdn_sums", "gdn_rstd", "gdn_gu", "gdn_masks", "gdn_xt", "gdn_attn",
                 "gdn_used", "o_squares", "o_mean", "o_rstd", "o_mixed", "ssd_au", "ssd_lg", "ssd_xdt", "ssd_xw", "ssd_xd",
                 "ssd_state", "ssd_ygated", "ssd_squares", "ssd_chunk_squares", "ssd_mean", "ssd_rstd", "ssd_mixed", "ret_rot", "ret_sum", "ret_kd",
                 "gdn_state", "ret_state", "f_squares", "f_rstd", "f_done",
                
                 "states_clear", "w_hi_ready", "w_lo_ready", "wsm_hi_ready", "wsm_lo_ready"]
        S = {n: sem(n) for n in names}

        ident = con[:, C_ID:C_ID + P]
        upper = con[:, C_UP:C_UP + P]
        lower = con[:, C_LOW:C_LOW + P]
        ones = con[:, C_ONE:C_ONE + P]
        pw = con[:, C_PW:C_PW + 8]

        def bank(tag):
            return ps[:, bank_of[tag], :]

        def bank4(tag, n=NT):
            return bank(tag).rearrange("p (c n) -> p c n", c=n)

        def wait_filled(eng, tag):
            eng.wait_ge(filled[bank_of[tag]], use_of[tag] + 1)

        def wait_emptied(eng, tag):
            eng.wait_ge(emptied[bank_of[tag]], use_of[tag] + 1)

        def empty(ins, tag):
            ins.then_inc(emptied[bank_of[tag]], 1)

        def over_rows(a, n=NT):
            return a.unsqueeze(1).broadcast_to([P, n, a.shape[1]])

        def over_cols(a, m=P):
            return a.unsqueeze(2).broadcast_to([P, a.shape[1], m])

        def mtile(p, i, half):
            kind = PIECES[i][0]
            if kind == "gdn":
                m = 2 * PIECES[i][1] + half
                n = slot_of(p, i, half)
                return 24 * p + m, m, slot[:, n % SLOTS, (m % 3) * HALF:(m % 3 + 1) * HALF]
            if kind == "bc":
                j = 2 * PIECES[i][1] + half
                return 24 * p + 12 + j, 12 + j, bc[:, j, :]
            if kind == "sx":
                g, j = PIECES[i][1], 2 * PIECES[i][2] + half
                n = slot_of(p, i, half)
                return 24 * p + 16 + 4 * g + j, 16 + 4 * g + j, slot[:, n % SLOTS, j * HALF:(j + 1) * HALF]
            return None

        where = {s: i for i, s in enumerate(plan)}
        units, loads = [], []
        for s in plan:
            if s[0] == "split_small":
                units.append(("small", s[1]))
            if s[0] == "out" and s[4] == 0:
                units.append(s[:4])
        unit_no = {u: i for i, u in enumerate(units)}
        unit_use = lambda u: u if u[0] == "small" else (*u, NT // 2 - 1)
        for n, u in enumerate(units):
            loads.append((where[unit_use(units[n - 2])] if n >= 2 else -1, n, u))
        for n in range(PARTS * len(PIECES)):
            p, i = divmod(n, len(PIECES))
            release = ("proj", *divmod(n - W_RING, len(PIECES)), 1, Q - 1)
            loads.append((where[release] if n >= W_RING else -2, n, ("in", p, i)))
        for n in range(PARTS * NT):
            p, t = divmod(n, NT)
            release = [where["norm", (n - 2) // NT, (n - 2) % NT]] if n >= 2 else [-3]
            if p and t < 2:
                release.append(where["ssd_y", p - 1, SG - 1, NT - 1])
            if p >= 2:
                release.append(where["final", p - 2, t])
            loads.append((max(release), n, ("x", p, t)))
            loads.append((where["final", p, t - 1] if t else where["squares", p, 0], n, ("rest", p, t)))
            loads.append((where["final", p, t], -1, ("store", p, t)))
        for p in range(PARTS):
            loads.append((where["squares", p, 0], p, ("post", p)))
            loads.append((where["gdn_decay", p, 0], p, ("rope", p)))
        loads.sort()
        block = ctx.enter_context(nc.Block())

        def ssd_before(s):
            m = NT * (SG * s[1] + s[2]) + s[3] - 1
            return ("ssd_y", m // (NT * SG), m // NT % SG, m % NT)

        def slot_wait(eng, n):
            if n is None or n < SLOTS:
                return
            r = slot_reader(n - SLOTS)
            if r[0] == "gdn_turn":
                wait_filled(eng, (*r, "v"))
            elif r[0] == "x_turn":
                wait_filled(eng, (*r, NT - 1))
            else:
                wait_filled(eng, r)

        def gate_wait(eng, G):
            if G >= 2:
                wait_filled(eng, ("mix_turn", (G - 2) // 4, (G - 2) % 4, NT - 1))

        def x_rows(p, t):
            r = (p % 2) * HALF + t * P
            return (x if p < 2 else x1)[r:r + P, :]

        @block.sync
        def _(sp):
            for _, n, key in loads:
                kind, p = key[:2]
                if kind == "x":
                    if n >= 2:
                        wait_filled(sp, ("norm", (n - 2) // NT, (n - 2) % NT, 1))
                    if p and key[2] < 2:
                        wait_filled(sp, ("ssd_y", p - 1, SG - 1, NT - 1, "w"))
                    if p >= 2:
                        sp.wait_ge(x_stored[key[2]], 16 * (p - 1))
                    sp.dma_start(xin[:, n % 2, :], x_rows(p, key[2])).then_inc(x_in[n % 2], 16)
                elif kind == "rest":
                    if key[2]:
                        sp.wait_ge(S["f_done"], n)
                    else:
                        wait_filled(sp, ("ssd_y", p, SG - 1, NT - 1, "w"))
                    sp.dma_start(xfin, x_rows(p, key[2])).then_inc(xf_in, 16)
                elif kind == "post":
                    wait_filled(sp, ("ssd_y", p, SG - 1, NT - 1, "w"))
                    sp.dma_start(post, post_norm[p // 2].partition_broadcast(P)).then_inc(post_in, 16)
                elif kind == "rope":
                    if p:
                        sp.wait_ge(S["ret_sum"], 2 * RH * p)
                    sp.dma_start(rp[:], rope[p % 2]).then_inc(rope_in, 16)
                elif kind == "store":
                    t = key[2]
                    sp.wait_ge(S["f_done"], NT * p + t + 1)
                    r = (p % 2) * HALF + t * P
                    sp.dma_start((x1 if p < 2 else out)[r:r + P, :], acc[:, t, :]).then_inc(x_stored[t], 16)
                elif kind == "in":
                    if n >= W_RING:
                        wait_filled(sp, ("proj", *divmod(n - W_RING, len(PIECES)), 1))
                    sp.dma_start(wr[:, n % W_RING, :], w_in[p // 2, key[2]]).then_inc(w_in_sem[n % W_RING], 16)
                else:
                    if n >= 2:
                        wait_filled(sp, unit_use(units[n - 2]))
                    if kind == "small":
                        sp.dma_start(wo[:, n % 2, 0:KD * NSM], w_small[p // 2].rearrange("p k n -> p (k n)")).then_inc(wo_in[n % 2], 16)
                    else:
                        sp.dma_start(wo[:, n % 2, :], w_out[p // 2, key[2], key[3]]).then_inc(wo_in[n % 2], 16)

            for t in range(NT):
                sp.wait_ge(x_stored[t], 16 * PARTS)

        def loaded_unit(eng, u):
            n = unit_no[u]
            eng.wait_ge(wo_in[n % 2], 16 * (n // 2 + 1))

        def wsm_parts(p):
            r, n = unit_no["small", p] % 2, KD * NSM
            return wo[:, r, 0:n], wo_parts[:, r, 0:n], wo_parts[:, r, n:2 * n]

        @block.tensor
        def _(pe):
            last_use = {}

            def opened(tag):
                if use_of[tag]:
                    pe.wait_ge(emptied[bank_of[tag]], use_of[tag])
                return bank(tag)

            def close(ins, tag):
                ins.then_inc(filled[bank_of[tag]], 1)

            def mm(o, a, b, start=True, stop=True):
                return nc.tensor.matmul(o, a, b, start=start, stop=stop)

            def turn(o, a):
                return nc.tensor.transpose(o, a, ident)

            pe.wait_ge(loaded, 16 * (1 + 2 * DEPTH))
            for s in plan:
                k, p = s[0], s[1]
                if k == "norm":
                    t = s[2]
                    pe.wait_ge(S["x_normed"], NT * p + t + 1)
                    for j in range(2):
                        tag = (*s, j)
                        b = opened(tag)
                        for c in range(4):
                            i = turn(b[:, c * P:(c + 1) * P], xin[:, (NT * p + t) % 2, (4 * j + c) * P:(4 * j + c + 1) * P])
                        close(i, tag)
                elif k == "small":
                    b = opened(s)[0:NSM, :]
                    lo, hi = (a.rearrange("p (k n) -> p k n", k=KD) for a in wsm_parts(p)[1:])
                    pe.wait_ge(S["wsm_lo_ready"], p + 1)
                    for kk in range(KD):
                        mm(b, hi[:, kk, :], hT_hi[:, kk, :], kk == 0, False)
                        mm(b, lo[:, kk, :], hT_hi[:, kk, :], False, False)
                        i = mm(b, hi[:, kk, :], hT_lo[:, kk, :], False, kk == KD - 1)
                    close(i, s)
                elif k == "small_turn":
                    wait_emptied(pe, ("small", p))
                    b = opened(s)
                    for t in range(NT):
                        i = nc.tensor.transpose(b[:, t * NSM:(t + 1) * NSM], smT[:, t * P:(t + 1) * P], ident[0:NSM, 0:NSM])
                    close(i, s)
                elif k == "small2":
                    pe.wait_ge(S["sm_decays"], p + 1)
                    b = opened(s)
                    n = NT * NDEC
                    for j, m in enumerate((upper, lower, ones)):
                        i = mm(b[:, j * n:(j + 1) * n], m, dg[:].rearrange("p t n -> p (t n)"))
                    close(i, s)
                elif k == "proj":
                    i_, half, q = s[2], s[3], s[4]
                    n = len(PIECES) * p + i_
                    hi = w_hi[:, n % W_RING, :].rearrange("p (k n) -> p k n", k=KD)
                    lo = w_lo[:, n % W_RING, :].rearrange("p (k n) -> p k n", k=KD)
                    tag = s[:4]
                    if q == 0:
                        opened(tag)
                        if i_ == 0:
                            wait_emptied(pe, ("norm", p, 2 * half + 1, 1))
                    b = bank(tag)
                    wide = PIECES[i_][0] in ("gdn", "bc", "sx")
                    v, k0 = divmod(2 * q, KD)
                    t = 2 * half + v
                    for kk in ((q,) if wide else (k0, k0 + 1)):
                        if half == 0 and kk % 2 == 0 and (wide or v == 0):
                            pe.wait_ge(S["w_lo_ready"], 4 * n + kk // 2 + 1)
                        for hw, hh in ((0, 0), (1, 0), (0, 1)):
                            wp, hp = (lo if hw else hi), (hT_lo if hh else hT_hi)
                            st, sp_ = kk == 0 and not (hw or hh), kk == KD - 1 and hh == 1
                            if wide:
                                i = mm(b, wp[:, kk, half * P:(half + 1) * P], hp[:, kk, :], st, sp_)
                            else:
                                i = mm(b[:, v * PC:(v + 1) * PC], hp[:, kk, t * P:(t + 1) * P], wp[:, kk, :], st, sp_)
                    if q == Q - 1:
                        close(i, tag)
                elif k == "out":
                    G, u, tp = s[2:]
                    w = wo[:, unit_no[s[:4]] % 2, :].rearrange("p (k n) -> p k n", k=4)
                    b = opened(s)
                    if tp == 0:
                        loaded_unit(pe, s[:4])
                    for v in range(2):
                        t = 2 * tp + v
                        wait_emptied(pe, ("mix_turn", p, G, t))
                        for kk in range(4):
                            i = mm(b[:, v * PC:(v + 1) * PC], mixT[:, kk, t * P:(t + 1) * P], w[:, kk, :], kk == 0, kk == 3)
                    close(i, s)
                elif k == "gdn_decay":
                    h = s[2]
                    pe.wait_ge(S["gdn_gu"], GH * p + h + 1)
                    b = opened(s)
                    close(mm(b, lower, gu[h % 2]), s)
                elif k == "gdn_turn":
                    h = s[2]
                    n = 10 * p + h
                    pe.wait_ge(S["silu_done"], 24 * p + 3 * h + 3)
                    for j, name in enumerate("qkv"):
                        tag = (*s, name)
                        b = opened(tag)
                        for c in range(NT):
                            i = turn(b[:, c * P:(c + 1) * P], slot[:, n % SLOTS, j * HALF + c * P:j * HALF + (c + 1) * P])
                        close(i, tag)
                elif k == "gdn_back":
                    h = s[2]
                    pe.wait_ge(S["gdn_k_scaled"], GH * p + h + 1)
                    for j, src in enumerate((kh, kb, qh, qe)):
                        if j == 2:
                            wait_emptied(pe, ("gdn_turn", p, h, "q"))
                        tag = (*s, j)
                        b = opened(tag)
                        for c in range(NT):
                            i = turn(b[:, c * P:(c + 1) * P], src[:, c, :])
                        close(i, tag)
                elif k == "gdn_gram":
                    h = s[2]
                    for j, src in enumerate((kbT, qT)):
                        wait_emptied(pe, ("gdn_back", p, h, j + 1))
                        tag = (*s, j)
                        b = opened(tag)
                        for c in range(NT):
                            i = mm(b[:, c * P:(c + 1) * P], kT[:, c, :], src[:, c, :])
                        close(i, tag)
                elif k == "gdn_x0":
                    h = s[2]
                    pe.wait_ge(S["gdn_xt"], GH * p + h + 1)
                    b = opened(s)
                    for c in range(NT):
                        i = turn(b[:, c * P:(c + 1) * P], XT[:, c, :])
                    close(i, s)
                elif k == "gdn_p":
                    h, lv = s[2], s[3]
                    wait_emptied(pe, ("gdn_x0", p, h) if lv == 1 else ("gdn_xx", p, h, lv - 1, 1))
                    pe.wait_ge(S["gdn_masks"], (LEVELS - 1) * (GH * p + h) + lv)
                    b = opened(s)
                    for c in range(NT):
                        i = mm(b[:, c * P:(c + 1) * P], (bT0, bT1)[lv % 2][:, c, :], X[:, c, :])
                    close(i, s)
                elif k == "gdn_xx":
                    h, lv = s[2], s[3]
                    wait_emptied(pe, ("gdn_p", p, h, lv))
                    if lv < LEVELS - 1:
                        tag = (*s, 0)
                        b = opened(tag)
                        for c in range(NT):
                            i = mm(b[:, c * P:(c + 1) * P], XT[:, c, :], PP[:, c, :])
                        close(i, tag)
                    tag = (*s, 1 if lv < LEVELS - 1 else 0)
                    b = opened(tag)
                    for c in range(NT):
                        i = mm(b[:, c * P:(c + 1) * P], PP[:, c, :], XT[:, c, :])
                    close(i, tag)
                elif k == "gdn_w":
                    h = s[2]
                    wait_emptied(pe, ("gdn_xx", p, h, LEVELS - 1, 0))
                    wait_emptied(pe, ("gdn_turn", p, h, "k"))
                    b = opened(s)
                    for c in range(NT):
                        i = mm(b[:, c * P:(c + 1) * P], kbe[:, c, :], XT[:, c, :])
                    close(i, s)
                elif k == "gdn_v":
                    h, c = s[2:]
                    first = p % 2 == 0 and c == 0
                    if c == 0:
                        wait_emptied(pe, ("gdn_w", p, h))
                    else:
                        wait_emptied(pe, ("gdn_o", p, h, c - 1))
                    b = opened(s)[:, 0:P]
                    i = mm(b, XT[:, c, :], vb[:, c, :], True, first)
                    if not first:
                        i = mm(b, wT[:, c, :], st_g[:, h, :], False, True)
                    close(i, s)
                elif k == "gdn_o":
                    h, c = s[2:]
                    first = p % 2 == 0 and c == 0
                    oo = ("gdn_oo", p, h)
                    if c == 0:
                        opened(oo)
                        wait_emptied(pe, ("gdn_back", p, h, 3))
                        pe.wait_ge(S["gdn_attn"], GH * p + h + 1)
                    o = bank(oo)[:, c * P:(c + 1) * P]
                    if not first:
                        mm(o, qeT[:, c, :], st_g[:, h, :], True, False)
                    wait_emptied(pe, ("gdn_v", p, h, c))
                    i = mm(o, att[:, c, :], vnew[:, c % 2, :], first, True)
                    if c == NT - 1:
                        close(i, oo)
                    b = opened(s)[:, 0:P]
                    close(mm(b, kdc[:, c, :], vnew[:, c % 2, :]), s)
                elif k == "mix_turn":
                    G = 4 * p + s[2]
                    if s[2] in (0, 3):
                        pe.wait_ge(S["o_mixed"], 8 * p + (4 if s[2] == 0 else 8))
                    else:
                        pe.wait_ge(S["ssd_mixed"], SG * p + s[2])
                    for t in range(NT):
                        tag = (*s, t)
                        b = opened(tag)
                        for j in range(4):
                            i = turn(b[:, j * P:(j + 1) * P], gate[:, G % 2, t, j * P:(j + 1) * P])
                        close(i, tag)
                elif k == "bc_turn":
                    pe.wait_ge(S["silu_done"], 24 * p + 16)
                    g = s[2]
                    tag = (*s, 0)
                    b = opened(tag)
                    for c in range(NT):
                        i = turn(b[:, c * P:(c + 1) * P], bc[:, g, c * P:(c + 1) * P])
                    close(i, tag)
                    tag = (*s, 1)
                    b = opened(tag)
                    for c in range(NT):
                        i = mm(b[:, c * P:(c + 1) * P], bc[:, g, c * P:(c + 1) * P], bc[:, 2 + g, c * P:(c + 1) * P])
                    close(i, tag)
                elif k == "x_turn":
                    g = s[2]
                    n = 10 * p + 4 + g
                    pe.wait_ge(S["silu_done"], 24 * p + 20 + 4 * g)
                    for c in range(NT):
                        tag = (*s, c)
                        b = opened(tag)
                        for j in range(4):
                            i = turn(b[:, j * P:(j + 1) * P], slot[:, n % SLOTS, j * HALF + c * P:j * HALF + (c + 1) * P])
                        close(i, tag)
                elif k == "ssd_l":
                    g, c = s[2:]
                    m = NT * (SG * p + g) + c
                    pe.wait_ge(S["ssd_au"], m + 1)
                    for j in range(2):
                        tag = (*s, j)
                        close(mm(opened(tag), lower, aU[:, j * 512:(j + 1) * 512]), tag)
                elif k == "ssd_y":
                    g, c = s[2:]
                    m = NT * (SG * p + g) + c
                    first = p % 2 == 0 and c == 0
                    tag = (*s, "z")
                    b = opened(tag)
                    if first:
                        pe.wait_ge(S["states_clear"], p // 2 + 1)
                    elif c or p % 2:
                        pe.wait_ge(S["ssd_state"], m if c else m - NT)
                    close(mm(b, bc[:, 2 + g, c * P:(c + 1) * P], st_s[:, g, :]), tag)
                    pe.wait_ge(S["ssd_lg"], m + 1)
                    pe.wait_ge(S["ssd_xdt"], m + 1)
                    LG = LGs[m % 2]
                    tag = (*s, "y")
                    b = opened(tag)
                    for j in range(HG):
                        i = mm(b[:, j * SP:(j + 1) * SP], LG[:, j * P:(j + 1) * P], xdt[m % 2][:, j * SP:(j + 1) * SP])
                    close(i, tag)
                    tag = (*s, "w")
                    b = opened(tag)
                    pe.wait_ge(S["ssd_xw"], m + 1)
                    close(mm(b, bt[:, c, :], xw[m % 2]), tag)
                elif k == "ret_turn":
                    h = s[2]
                    pe.wait_ge(S["ret_rot"], 2 * (RH * p + h) + 2)
                    v = slot[:, (10 * p + 6 + h) % SLOTS, 0:1024].rearrange("p (t q n) -> p t q n", t=NT, q=2)
                    for j, name in enumerate("qk"):
                        tag = (*s, name)
                        b = opened(tag)
                        for c in range(NT):
                            i = turn(b[:, c * P:(c + 1) * P], v[:, c, j, :])
                        close(i, tag)
                elif k == "ret_s":
                    h = s[2]
                    wait_emptied(pe, ("ret_turn", p, h, "q"))
                    wait_emptied(pe, ("ret_turn", p, h, "k"))
                    b = opened(s)
                    for c in range(NT):
                        i = mm(b[:, c * P:(c + 1) * P], rkT[:, c, :], rqT[:, c, :])
                    close(i, s)
                elif k == "ret_o":
                    h, c = s[2:]
                    first = p % 2 == 0 and c == 0
                    oo = ("ret_oo", p, h)
                    vv = slot[:, (10 * p + 6 + h) % SLOTS, 1024:1536].rearrange("p (t n) -> p t n", t=NT)
                    if c == 0:
                        opened(oo)
                        wait_emptied(pe, ("ret_s", p, h))
                        wait_emptied(pe, ("proj", p, AT["ret", 2 * h + 1], 1))
                    else:
                        wait_emptied(pe, ("ret_o", p, h, c - 1))
                    o = bank(oo)[:, c * P:(c + 1) * P]
                    if not first:
                        mm(o, rqd[:, c, :], st_r[:, h, :], True, False)
                    i = mm(o, rS[:, c, :], vv[:, c, :], first, True)
                    if c == NT - 1:
                        close(i, oo)
                    if c == 0:
                        pe.wait_ge(S["ret_kd"], RH * p + h + 1)
                    b = opened(s)[:, 0:P]
                    close(mm(b, rkd[:, c, :], vv[:, c, :]), s)

        @block.vector
        def _(dve):
            n_step = [0]

            def chain(ins):
                n_step[0] += 1
                ins.then_inc(dve_step, 1)
                dve.wait_ge(dve_step, n_step[0])

            tt, ts, stt = nc.vector.tensor_tensor, nc.vector.tensor_scalar, nc.vector.scalar_tensor_tensor

            def clear_states():
                nc.vector.memset(st_s[:].rearrange("p a b -> p (a b)"), 0.0).then_inc(S["states_clear"], 1)

            def mean_eps(src, dst, width, name):
                ts(dst, src, 1.0 / width, EPS, ALU.mult, ALU.add).then_inc(S[name], 1)

            conv_at = None
            dve.wait_ge(loaded, 16 * (1 + 2 * DEPTH))
            chain(nc.vector.memset(sm_t[:].rearrange("p a b -> p (a b)"), 0.0))
            clear_states()
            dve.wait_ge(S["nega_ready"], 1)
            chain(ts(nega[:], nega[:], -1.0, None, ALU.mult))
            for s in plan:
                k, p = s[0], s[1]
                l, first_half = p // 2, p % 2 == 0
                if k == "norm":
                    t = s[2]
                    for j in range(2):
                        tag = (*s, j)
                        wait_filled(dve, tag)
                        cols = slice(t * P, (t + 1) * P)
                        chain(tt(hT_hi[:, 4 * j:4 * j + 4, cols], bank4(tag),
                                 over_cols(par[:, l, Q_PRE + 4 * j:Q_PRE + 4 * j + 4]), ALU.mult))
                        for kk in range(4 * j, 4 * j + 4):
                            ins = stt(hT_lo[:, kk, cols], bank4(tag)[:, kk - 4 * j, :], par[:, l, Q_PRE + kk:Q_PRE + kk + 1],
                                      hT_hi[:, kk, cols], ALU.mult, ALU.subtract)
                        empty(ins, tag)
                elif k == "small_turn":
                    wait_filled(dve, s)
                    sm = small
                    empty(nc.vector.tensor_copy(sm, bank(s)[:, 0:NT * NSM].rearrange("p (t n) -> p t n", t=NT)), s)
                    wait_emptied(dve, s)
                    v = [sm_t[:, i, :].rearrange("p (t n) -> p t n", t=NT) for i in range(6)]
                    a, e, z, q, r, m = v
                    chain(tt(a, sm[:, :, GH:NSM], over_rows(row[:, l, R_DT:R_DT + NDEC]), ALU.add))
                    chain(ts(m, a, -1.0, None, ALU.mult))
                    tt(m, m, a, ALU.max).then_inc(S["sm_abs"], 1)
                    dve.wait_ge(S["sm_exp"], p + 1)
                    chain(ts(q, e, 2.0, None, ALU.add))
                    chain(nc.vector.reciprocal(q, q))
                    chain(tt(q, q, e, ALU.mult))
                    chain(tt(z, q, q, ALU.mult))
                    chain(ts(r, z, 1.0 / 17, None, ALU.mult))
                    for o in (15, 13, 11, 9, 7, 5, 3):
                        chain(stt(r, r, 1.0 / o, z, ALU.add, ALU.mult))
                    chain(stt(r, r, 1.0, q, ALU.add, ALU.mult))
                    chain(ts(a, a, 0.0, None, ALU.max))
                    chain(stt(dt[:], r, 2.0, a, ALU.mult, ALU.add))
                    dve.wait_ge(S["sm_beta_exp"], p + 1)
                    chain(ts(beta[:], beta[:], 1.0, None, ALU.add))
                    chain(nc.vector.reciprocal(beta[:], beta[:]))
                    tt(dg[:], dt[:], over_rows(nega[:, l, :]), ALU.mult).then_inc(S["sm_decays"], 1)
                elif k == "proj":
                    i, half, q = s[2], s[3], s[4]
                    tag = s[:4]
                    if conv_at is not None:
                        cp, ci, ch = conv_at
                        n, m, dst = mtile(cp, ci, ch)
                        w = par[:, cp // 2, Q_CONV + TAPS * m:Q_CONV + TAPS * (m + 1)]
                        r, o = raw[:, n % 2, :], dst
                        j, odd = divmod(q - 1, 2)
                        if j == 1 and not odd:
                            dve.wait_ge(S["conv_begun"], n + 1)
                        elif j > 1 and not odd:
                            dve.wait_ge(S["conv_done"], (TAPS - 1) * n + j - 1)
                        if j >= 1 and not odd:
                            stt(o, r[:, j:j + HALF], w[:, j:j + 1], o, ALU.mult, ALU.add).then_inc(S["conv_done"], 1)
                        if q == Q - 1:
                            conv_at = None
                    if q < Q - 1:
                        continue
                    if mtile(p, i, half):
                        conv_at = (p, i, half)
                    elif PIECES[i][0] == "ret" and PIECES[i][1] % 2 == 0:
                        h = PIECES[i][1] // 2
                        m = 2 * (RH * p + h) + half
                        wait_filled(dve, tag)
                        dve.wait_ge(rope_in, 16 * (p + 1))
                        slot_wait(dve, 10 * p + 6 + h)
                        if m:
                            dve.wait_ge(S["ret_sum"], m)
                        own = slot[:, (10 * p + 6 + h) % SLOTS, half * 512:half * 512 + 512]
                        b = bank(tag).rearrange("p (t q e n) -> p t q e n", t=2, q=2, e=2)
                        ns = slot[:, (10 * p + 6 + h) % SLOTS, 0:1024].rearrange("p (t q e n) -> p t q e n", t=NT, q=2, e=2)
                        r0 = own.rearrange("p (t q e n) -> p t q e n", t=2, q=2, e=2)
                        r1 = rot[:].rearrange("p (t q e n) -> p t q e n", t=2, q=2, e=2)
                        for u in range(2):
                            tile = 2 * half + u
                            co = rp[:, tile * 64:(tile + 1) * 64]
                            si = rp[:, NT * 64 + tile * 128:NT * 64 + (tile + 1) * 128].rearrange("p (e n) -> p e n", e=2)
                            tt(r0[:, u].rearrange("p q e n -> p (q e) n"), b[:, u].rearrange("p q e n -> p (q e) n"),
                               over_rows(co), ALU.mult)
                            ins = tt(r1[:, u], b[:, u, :, ::-1, :],
                                     si.unsqueeze(1).broadcast_to([P, 2, 2, 64]), ALU.mult)
                        empty(ins, tag)
                        wait_emptied(dve, tag)
                        tt(own, own, rot[:], ALU.add).then_inc(S["ret_sum"], 1)
                        dve.wait_ge(S["ret_sum"], m + 1)
                        dve.sem_inc(S["ret_rot"], 1)
                elif k == "gdn_turn":
                    h = s[2]
                    n = GH * p + h
                    be = beta[:, :, h]
                    de = dec[:]
                    dve.wait_ge(S["gdn_squares"], n + 1)
                    if n:
                        dve.wait_ge(S["gdn_rstd"], n)
                    chain(nc.vector.tensor_reduce(gss[:], junk[:].rearrange("p q (c n) -> p (q c) n", c=NT), mybir.AxisListType.X,
                                                  ALU.add))
                    ts(gss[:], gss[:], EPS, None, ALU.add).then_inc(S["gdn_sums"], 1)
                    dve.wait_ge(S["gdn_rstd"], n + 1)
                    wait_emptied(dve, ("small2", p))
                    rq, rk = rs[:, 0:4], rs[:, 4:8]
                    nc.vector.tensor_copy(sc[:, 0, :], rk)
                    tt(sc[:, 1, :], rk, be, ALU.mult)
                    tt(sc[:, 3, :], rk, de[:, 1, :, h], ALU.mult)
                    chain(ts(sc[:, 4, :], rq, DK ** -0.5, None, ALU.mult))
                    tt(sc[:, 2, :], sc[:, 1, :], de[:, 0, :, h], ALU.mult)
                    chain(tt(sc[:, 5, :], sc[:, 4, :], de[:, 0, :, h], ALU.mult))
                    for name, outs in (("k", ((kh, 0), (kb, 1))), ("q", ((qh, 4), (qe, 5)))):
                        tag = (*s, name)
                        wait_filled(dve, tag)
                        for o, j in outs:
                            ins = tt(o, bank4(tag), over_cols(sc[:, j, :]), ALU.mult)
                        if outs[0][1]:
                            empty(ins, tag)
                        else:
                            ins.then_inc(S["gdn_k_scaled"], 1)
                elif k == "gdn_back":
                    h = s[2]
                    tag = ("gdn_turn", p, h, "k")
                    tt(kbe, bank4(tag), over_cols(sc[:, 2, :]), ALU.mult)
                    empty(tt(kdc, bank4(tag), over_cols(sc[:, 3, :]), ALU.mult), tag)
                    tag = ("gdn_turn", p, h, "v")
                    wait_filled(dve, tag)
                    empty(tt(vb, bank4(tag), over_cols(beta[:, :, h]), ALU.mult), tag)
                elif k == "gdn_gram":
                    h = s[2]
                    n = GH * p + h
                    wait_emptied(dve, ("gdn_decay", p, h))
                    tag = (*s, 0)
                    wait_filled(dve, tag)
                    if n:
                        dve.wait_ge(S["gdn_masks"], (LEVELS - 1) * n)
                    empty(tt(aT, bank4(tag), et[:, h], ALU.mult), tag)
                    tag = (*s, 1)
                    wait_filled(dve, tag)
                    empty(tt(att, bank4(tag), et[:, h], ALU.mult), tag)
                    wait_emptied(dve, (*s, 0))
                    chain(tt(bT0, aT, over_rows(con[:, C_LEV:C_LEV + P]), ALU.mult))
                    stt(XT, bT0, -1.0, over_rows(ident), ALU.mult, ALU.add).then_inc(S["gdn_xt"], 1)
                elif k == "gdn_xx":
                    h, lv = s[2], s[3]
                    if lv < LEVELS - 1:
                        tag = (*s, 0)
                        wait_filled(dve, tag)
                        wait_emptied(dve, ("gdn_x0", p, h) if lv == 1 else ("gdn_xx", p, h, lv - 1, 1))
                        empty(tt(X, X, bank4(tag), ALU.subtract), tag)
                    tag = (*s, 1 if lv < LEVELS - 1 else 0)
                    wait_filled(dve, tag)
                    if lv == 1:
                        dve.wait_ge(S["gdn_xt"], GH * p + h + 1)
                    empty(tt(XT, XT, bank4(tag), ALU.subtract), tag)
                elif k == "gdn_v":
                    wait_filled(dve, s)
                    empty(nc.vector.tensor_copy(vnew[:, s[3] % 2, :], bank(s)[:, 0:P]), s)
                elif k == "gdn_o":
                    h, c = s[2:]
                    wait_filled(dve, s)
                    if first_half and c == 0:
                        empty(nc.vector.tensor_copy(st_g[:, h, :], bank(s)[:, 0:P]), s)
                    else:
                        if c:
                            wait_emptied(dve, ("gdn_o", p, h, c - 1))
                        empty(stt(st_g[:, h, :], st_g[:, h, :], dec[:, 2, c, h:h + 1], bank(s)[:, 0:P],
                                  ALU.mult, ALU.add), s)
                elif k in ("gdn_fin", "ret_fin"):
                    h = s[2]
                    r = k == "ret_fin"
                    n = 8 * p + 4 * r + h
                    G = 4 * p + 3 * r
                    oo = ("ret_oo" if r else "gdn_oo", p, h)
                    dve.wait_ge(S["o_squares"], n + 1)
                    chain(nc.vector.tensor_reduce(ss[:, 2:6], junk[:, 0, :].rearrange("p (c n) -> p c n", c=NT),
                                                  mybir.AxisListType.X, ALU.add))
                    mean_eps(ss[:, 2:6], rs[:, 8:12], P, "o_mean")
                    dve.wait_ge(S["o_rstd"], n + 1)
                    g = gate[:, G % 2, :, h * P:(h + 1) * P]
                    if r:
                        wait_emptied(dve, ("proj", p, AT["ret", 2 * h + 1], 1))
                    else:
                        wait_emptied(dve, ("proj", p, AT["gz", h // 2], 1))
                    chain(tt(g, g, over_cols(rs[:, 12:16]), ALU.mult))
                    empty(tt(g, g, bank4(oo), ALU.mult), oo)
                    wait_emptied(dve, oo)
                    dve.sem_inc(S["o_mixed"], 1)
                elif k == "mix_turn":
                    for t in range(NT):
                        tag = (*s, t)
                        wait_filled(dve, tag)
                        empty(tt(mixT[:, :, t * P:(t + 1) * P], bank4(tag), over_cols(par[:, l, Q_MIX + 4 * s[2]:Q_MIX + 4 * s[2] + 4]),
                                 ALU.mult), tag)
                elif k == "out":
                    G, u, tp = s[2:]
                    wait_filled(dve, s)
                    o = acc[:, 2 * tp:2 * tp + 2, u * PC:(u + 1) * PC]
                    b = bank(s).rearrange("p (t n) -> p t n", t=2)
                    if G == 0:
                        if p and u == 0:
                            for v in range(2):
                                dve.wait_ge(x_stored[2 * tp + v], 16 * p)
                        empty(nc.vector.tensor_copy(o, b), s)
                    else:
                        wait_emptied(dve, ("out", p, G - 1, u, tp))
                        empty(tt(o, o, b, ALU.add), s)
                elif k == "bc_turn":
                    tag = (*s, 1)
                    wait_filled(dve, tag)
                    empty(tt(gT, bank4(tag), over_rows(upper), ALU.mult), tag)
                elif k == "ssd_y":
                    g, c = s[2:]
                    m = NT * (SG * p + g) + c
                    G = 4 * p + 1 + g
                    heads = slice(GH + HG * g, GH + HG * (g + 1))
                    per_head = lambda a: a.unsqueeze(2).broadcast_to([P, HG, SP])
                    v8 = lambda a: a.rearrange("p (h n) -> p h n", h=HG)
                    tag = (*s, "z")
                    wait_filled(dve, tag)
                    if m:
                        dve.wait_ge(S["ssd_ygated"], m)
                    empty(tt(v8(yy), v8(bank(tag)), per_head(dec[:, 0, c, heads]), ALU.mult), tag)
                    st = st_s[:, g, :]
                    chain(tt(v8(st), v8(st), per_head(dec[:, 2, c, heads]), ALU.mult))
                    wait_emptied(dve, tag)
                    tag = (*s, "y")
                    wait_filled(dve, tag)
                    empty(tt(yy, yy, bank(tag), ALU.add), tag)
                    tag = (*s, "w")
                    wait_filled(dve, tag)
                    empty(tt(st, st, bank(tag), ALU.add), tag)
                    wait_emptied(dve, tag)
                    if first_half is False and c == NT - 1 and g == SG - 1 and l + 1 < DEPTH:
                        clear_states()
                    dve.sem_inc(S["ssd_state"], 1)
                    dve.wait_ge(S["ssd_xd"], m + 1)
                    chain(tt(yy, yy, xD, ALU.add))
                    wait_emptied(dve, ("proj", p, AT["sz", g, N_SZ - 1], 1))
                    tt(gate[:, G % 2, c, :], yy, gate[:, G % 2, c, :], ALU.mult).then_inc(S["ssd_ygated"], 1)
                elif k == "ssd_norm":
                    dve.wait_ge(S["ssd_squares"], SG * p + s[2] + 1)
                    mean_eps(sss[:, 0:NT], sss[:, NT:2 * NT], 512, "ssd_mean")
                elif k == "ssd_l":
                    g, c = s[2:]
                    m = NT * (SG * p + g) + c
                    heads = slice(GH + HG * g, GH + HG * (g + 1))
                    per_head = lambda a: a.unsqueeze(2).broadcast_to([P, HG, SP])
                    v8 = lambda a: a.rearrange("p (h n) -> p h n", h=HG)
                    wait_emptied(dve, ("x_turn", p, g, c))
                    if m >= 2:
                        dve.wait_ge(S["ssd_xw"], m - 1)
                        wait_filled(dve, (*ssd_before(ssd_before(s)), "y"))
                    tt(v8(xdt[m % 2]), v8(xt[:, c, :]), per_head(dt[:, c, heads]), ALU.mult).then_inc(S["ssd_xdt"], 1)
                    wait_emptied(dve, ("ssd_l", p, g, c, 1))
                    if c == 0:
                        wait_emptied(dve, ("bc_turn", p, g, 1))
                    L3 = LGs[m % 2].rearrange("p (h n) -> p h n", h=HG)
                    tt(L3, L3, over_rows(gT[:, c, :], HG), ALU.mult).then_inc(S["ssd_lg"], 1)
                elif k == "ret_turn":
                    h = s[2]
                    tag = (*s, "q")
                    wait_filled(dve, tag)
                    nc.vector.tensor_copy(rqT, bank4(tag))
                    empty(tt(rqd, bank4(tag), over_rows(con[:, C_QD + h * P:C_QD + (h + 1) * P]), ALU.mult), tag)
                elif k == "ret_s":
                    h = s[2]
                    wait_filled(dve, s)
                    empty(tt(rS, bank4(s), over_rows(con[:, C_DM + h * P:C_DM + (h + 1) * P]), ALU.mult), s)
                elif k == "ret_o":
                    h, c = s[2:]
                    wait_filled(dve, s)
                    if first_half and c == 0:
                        empty(nc.vector.tensor_copy(st_r[:, h, :], bank(s)[:, 0:P]), s)
                    else:
                        if c:
                            wait_emptied(dve, ("ret_o", p, h, c - 1))
                        empty(stt(st_r[:, h, :], st_r[:, h, :], LAM[h] ** P, bank(s)[:, 0:P], ALU.mult, ALU.add), s)
                elif k == "final":
                    t = s[2]
                    n = NT * p + t
                    dve.wait_ge(S["f_rstd"], n + 1)
                    dve.wait_ge(post_in, 16 * (p + 1))
                    chain(stt(acc[:, t, :], acc[:, t, :], frs[:, t:t + 1], post, ALU.mult, ALU.mult))
                    dve.wait_ge(xf_in, 16 * (n + 1))
                    tt(acc[:, t, :], acc[:, t, :], xfin, ALU.add).then_inc(S["f_done"], 1)

        @block.scalar
        def _(act):
            A = nc.scalar.activation
            n_step = [0]

            def chain(ins):
                n_step[0] += 1
                ins.then_inc(act_step, 1)
                act.wait_ge(act_step, n_step[0])

            silu_at = None
            junk_read = []

            def square_into_junk(read_by):
                if junk_read:
                    act.wait_ge(*junk_read.pop())
                junk_read.append(read_by)

            act.wait_ge(loaded, 16 * (1 + 2 * DEPTH))
            A(nega[:], row[:, :, R_A:R_A + NDEC], ACT.Exp).then_inc(S["nega_ready"], 1)
            for s in plan:
                k, p = s[0], s[1]
                l, first_half = p // 2, p % 2 == 0
                if k == "scale":
                    t = s[2]
                    n = NT * p + t
                    act.wait_ge(x_in[n % 2], 16 * (n // 2 + 1))
                    square_into_junk((S["x_squares"], n + 1))
                    A(junk[:].rearrange("p a b -> p (a b)"), xin[:, n % 2, :], ACT.Square, accum_out=xss[:, 0:1]).then_inc(S["x_squares"], 1)
                    act.wait_ge(S["x_rstd"], n + 1)
                    A(xin[:, n % 2, :], xin[:, n % 2, :], ACT.Copy, scale=xrs[:, 0:1]).then_inc(S["x_normed"], 1)
                elif k == "small":
                    wait_filled(act, s)
                    empty(A(smT, bank(s)[0:NSM, :], ACT.Copy), s)
                elif k == "small_turn":
                    act.wait_ge(S["sm_abs"], p + 1)
                    A(sm_t[:, 1, :], sm_t[:, 5, :], ACT.Exp, scale=-1.0).then_inc(S["sm_exp"], 1)
                    A(beta[:], small[:, :, 0:GH], ACT.Exp, scale=-1.0).then_inc(S["sm_beta_exp"], 1)
                elif k == "split":
                    n, j = len(PIECES) * p + s[2], s[3]
                    if j == 0:
                        act.wait_ge(w_in_sem[n % W_RING], 16 * (n // W_RING + 1))
                        if n >= W_RING:
                            wait_filled(act, ("proj", *divmod(n - W_RING, len(PIECES)), 1))
                    A(w_hi[:, n % W_RING, j * 512:(j + 1) * 512], wr[:, n % W_RING, j * 512:(j + 1) * 512], ACT.Copy)\
                        .then_inc(S["w_hi_ready"], 1)
                elif k == "split_small":
                    loaded_unit(act, ("small", p))
                    w, _, hi = wsm_parts(p)
                    A(hi, w, ACT.Copy).then_inc(S["wsm_hi_ready"], 1)
                elif k == "small2":
                    wait_filled(act, s)
                    empty(A(dec[:].rearrange("p j t n -> p (j t n)"), bank(s)[:, 0:3 * NT * NDEC], ACT.Exp), s)
                elif k == "proj" and s[4] == Q - 1:
                    i, half = s[2], s[3]
                    tag = s[:4]
                    mt = mtile(p, i, half)
                    kind = PIECES[i][0]
                    silu_of, silu_at = silu_at, None
                    if kind != "ret" or PIECES[i][1] % 2:
                        wait_filled(act, tag)
                    if mt:
                        n, m, dst = mt
                        if n >= 2:
                            act.wait_ge(S["conv_done"], (TAPS - 1) * (n - 1))
                        A(raw[:, n % 2, 0:3], halo[:, m, :] if not first_half else con[:, C_ZERO:C_ZERO + 3], ACT.Copy)
                        if first_half:
                            act.wait_ge(act_step, n_step[0]) if n_step[0] else None
                            A(halo[:, m, :], bank(tag)[:, HALF - 3:HALF], ACT.Copy)
                        empty(A(raw[:, n % 2, 3:3 + HALF], bank(tag), ACT.Copy), tag)
                        wait_emptied(act, tag)
                        slot_wait(act, slot_of(p, i, half))
                        w0 = par[:, l, Q_CONV + TAPS * m:Q_CONV + TAPS * m + 1]
                        if m >= 12:
                            ins = A(dst, raw[:, n % 2, 0:HALF], ACT.Identity, bias=par[:, l, Q_BIAS + m - 12:Q_BIAS + m - 11], scale=w0)
                        else:
                            ins = A(dst, raw[:, n % 2, 0:HALF], ACT.Copy, scale=w0)
                        ins.then_inc(S["conv_begun"], 1)
                        silu_at = (n, dst)
                    elif kind in ("gz", "sz"):
                        j = PIECES[i][-1]
                        G = gate_of(p, i)
                        gate_wait(act, G)
                        empty(A(gate[:, G % 2, 2 * half:2 * half + 2, j * PC:(j + 1) * PC],
                                bank(tag).rearrange("p (t n) -> p t n", t=2), ACT.Silu), tag)
                    elif PIECES[i][1] % 2:
                        h = PIECES[i][1] // 2
                        G = gate_of(p, i)
                        gate_wait(act, G)
                        b = bank(tag).rearrange("p (t n) -> p t n", t=2)
                        v = slot[:, (10 * p + 6 + h) % SLOTS, 1024:1536].rearrange("p (t n) -> p t n", t=NT)
                        slot_wait(act, 10 * p + 6 + h)
                        A(v[:, 2 * half:2 * half + 2, :], b[:, :, 0:P], ACT.Copy)
                        empty(A(gate[:, G % 2, 2 * half:2 * half + 2, h * P:(h + 1) * P], b[:, :, P:2 * P], ACT.Silu), tag)
                    if silu_of is not None:
                        n, was = silu_of
                        act.wait_ge(S["conv_done"], (TAPS - 1) * (n + 1))
                        A(was, was, ACT.Silu).then_inc(S["silu_done"], 1)
                elif k == "gdn_decay":
                    wait_filled(act, s)
                    empty(A(et[:, s[2]].rearrange("p c n -> p (c n)"), bank(s), ACT.Exp), s)
                elif k == "gdn_turn":
                    h = s[2]
                    n = GH * p + h
                    square_into_junk((S["gdn_sums"], n + 1))
                    for j, name in enumerate("qk"):
                        tag = (*s, name)
                        wait_filled(act, tag)
                        ins = A(junk[:, j, :], bank(tag), ACT.Square)
                    ins.then_inc(S["gdn_squares"], 1)
                elif k == "gdn_back":
                    for j, o in enumerate((kT, kbT, qT, qeT)):
                        tag = (*s, j)
                        wait_filled(act, tag)
                        empty(A(o, bank4(tag), ACT.Copy), tag)
                elif k == "gdn_x0":
                    wait_filled(act, s)
                    empty(A(X, bank4(s), ACT.Copy), s)
                elif k == "gdn_p":
                    wait_filled(act, s)
                    empty(A(PP, bank4(s), ACT.Copy), s)
                elif k == "gdn_w":
                    wait_filled(act, s)
                    empty(A(wT, bank4(s), ACT.Copy, scale=-1.0), s)
                elif k in ("gdn_fin", "ret_fin"):
                    r = k == "ret_fin"
                    n = 8 * p + 4 * r + s[2]
                    oo = ("ret_oo" if r else "gdn_oo", p, s[2])
                    wait_filled(act, oo)
                    square_into_junk((S["o_mean"], n + 1))
                    A(junk[:, 0, :], bank(oo), ACT.Square).then_inc(S["o_squares"], 1)
                elif k == "bc_turn":
                    tag = (*s, 0)
                    wait_filled(act, tag)
                    wait_filled(act, ("ssd_y", p, 0, NT - 1, "w") if s[2] else ("gdn_o", p, GH - 1, NT - 1))
                    empty(A(bt, bank4(tag), ACT.Copy), tag)
                elif k == "x_turn":
                    g = s[2]
                    if SG * p + g:
                        act.wait_ge(S["ssd_xd"], NT * (SG * p + g))
                        act.wait_ge(S["ssd_xdt"], NT * (SG * p + g))
                    for c in range(NT):
                        tag = (*s, c)
                        wait_filled(act, tag)
                        empty(A(xt[:, c, :], bank(tag), ACT.Copy), tag)
                elif k == "ssd_l":
                    g, c = s[2:]
                    m = NT * (SG * p + g) + c
                    LG = LGs[m % 2]
                    if m >= 2:
                        wait_filled(act, (*ssd_before(ssd_before(s)), "y"))
                    for j in range(2):
                        tag = (*s, j)
                        wait_filled(act, tag)
                        empty(A(LG[:, j * 512:(j + 1) * 512], bank(tag), ACT.Exp), tag)
                elif k == "ssd_norm":
                    n = SG * p + s[2]
                    G = 4 * p + 1 + s[2]
                    if n:
                        act.wait_ge(S["ssd_mean"], n)
                    for c in range(NT):
                        act.wait_ge(S["ssd_ygated"], NT * n + c + 1)
                        square_into_junk((S["ssd_chunk_squares"], (NT - 1) * n + c + 1) if c < NT - 1 else (S["ssd_squares"], n + 1))
                        A(junk[:, 0, :], gate[:, G % 2, c, :], ACT.Square, accum_out=sss[:, c:c + 1])\
                            .then_inc(S["ssd_chunk_squares" if c < NT - 1 else "ssd_squares"], 1)
                    act.wait_ge(S["ssd_rstd"], n + 1)
                    for c in range(NT):
                        ins = A(gate[:, G % 2, c, :], gate[:, G % 2, c, :], ACT.Copy, scale=ssr[:, c:c + 1])
                    ins.then_inc(S["ssd_mixed"], 1)
                elif k == "ret_turn":
                    h = s[2]
                    tag = (*s, "k")
                    wait_filled(act, tag)
                    empty(A(rkT, bank4(tag), ACT.Copy), tag)
                    v = slot[:, (10 * p + 6 + h) % SLOTS, 0:1024].rearrange("p (t q n) -> p t q n", t=NT, q=2)
                    if h:
                        wait_filled(act, ("ret_o", p, h - 1, NT - 1))
                    else:
                        act.wait_ge(S["ssd_mixed"], SG * (p + 1))
                    A(rkd, v[:, :, 1, :], ACT.Copy, scale=con[:, C_KD + h:C_KD + h + 1]).then_inc(S["ret_kd"], 1)
                elif k == "squares":
                    t = s[2]
                    n = NT * p + t
                    wait_emptied(act, ("out", p, GROUPS - 1, UNITS - 1, t // 2))
                    if p:
                        act.wait_ge(S["f_rstd"], n - NT + 1)
                    square_into_junk((S["f_squares"], n + 1))
                    A(junk[:].rearrange("p a b -> p (a b)"), acc[:, t, :], ACT.Square, accum_out=fss[:, t:t + 1]).then_inc(S["f_squares"], 1)

        @block.gpsimd
        def _(pool):
            tt, ts = nc.gpsimd.tensor_tensor, nc.gpsimd.tensor_scalar
            n_step = [0]

            def chain(ins):
                n_step[0] += 1
                ins.then_inc(pool_step, 1)
                pool.wait_ge(pool_step, n_step[0])

            def mask_level(lv):
                m = con[:, C_LEV + lv * P:C_LEV + (lv + 1) * P]
                tt((bT0, bT1)[lv % 2], aT, over_rows(m), ALU.mult).then_inc(S["gdn_masks"], 1)

            pool.dma_start(con[:], cons).then_inc(loaded, 16)
            for l in range(DEPTH):
                pool.dma_start(par[:, l, :], pars[l]).then_inc(loaded, 16)
                pool.dma_start(row[:, l, :], rows[l].partition_broadcast(P)).then_inc(loaded, 16)
            pool.wait_ge(loaded, 16 * (1 + 2 * DEPTH))
            for s in plan:
                k, p = s[0], s[1]
                if k == "scale":
                    n = NT * p + s[2]
                    pool.wait_ge(S["x_squares"], n + 1)
                    chain(ts(xss[:, 1:2], xss[:, 0:1], 1.0 / D, EPS, ALU.mult, ALU.add))
                    if n:
                        pool.wait_ge(S["x_normed"], n)
                    tt(xrs[:, 0:1], xss[:, 1:2], pw[:, 0:1], ALU.pow).then_inc(S["x_rstd"], 1)
                elif k == "gdn_decay":
                    h = s[2]
                    if h == 0:
                        pool.wait_ge(S["sm_decays"], p + 1)
                    if h >= 2:
                        wait_filled(pool, ("gdn_decay", p, h - 2))
                    tt(gu[h % 2].rearrange("p (c n) -> p c n", c=NT), over_rows(upper), over_cols(dg[:, :, h]),
                       ALU.mult).then_inc(S["gdn_gu"], 1)
                elif k == "gdn_turn":
                    n = GH * p + s[2]
                    pool.wait_ge(S["gdn_sums"], n + 1)
                    if n:
                        wait_emptied(pool, ("gdn_turn", (n - 1) // GH, (n - 1) % GH, "q"))
                    tt(rs[:, 0:8], gss[:, :], pw, ALU.pow).then_inc(S["gdn_rstd"], 1)
                elif k == "gdn_gram":
                    h = s[2]
                    for lv in (1, 2):
                        if lv == 2:
                            pool.wait_ge(S["gdn_xt"], GH * p + h + 1)
                        if lv == 1:
                            wait_emptied(pool, (*s, 1))
                            tt(att, att, over_rows(upper), ALU.mult).then_inc(S["gdn_attn"], 1)
                        mask_level(lv)
                elif k == "gdn_p" and s[3] + 2 < LEVELS:
                    wait_filled(pool, s)
                    mask_level(s[3] + 2)
                elif k in ("gdn_fin", "ret_fin"):
                    n = 8 * p + 4 * (k == "ret_fin") + s[2]
                    pool.wait_ge(S["o_mean"], n + 1)
                    if n:
                        pool.wait_ge(S["o_mixed"], n)
                    tt(rs[:, 12:16], rs[:, 8:12], pw[:, 0:4], ALU.pow).then_inc(S["o_rstd"], 1)
                elif k == "ssd_l":
                    g, c = s[2:]
                    m = NT * (SG * p + g) + c
                    heads = slice(GH + HG * g, GH + HG * (g + 1))
                    if m:
                        wait_filled(pool, ("ssd_l", *ssd_before(s)[1:], 1))
                    if g == 0 and c == 0:
                        wait_filled(pool, ("gdn_o", p, GH - 1, NT - 1))
                    tt(aU.rearrange("p (h n) -> p h n", h=HG), over_rows(upper, HG), over_cols(dg[:, c, heads]),
                       ALU.mult).then_inc(S["ssd_au"], 1)
                    per_head = lambda a: a.unsqueeze(2).broadcast_to([P, HG, SP])
                    v8 = lambda a: a.rearrange("p (h n) -> p h n", h=HG)
                    pool.wait_ge(S["ssd_xdt"], m + 1)
                    if m >= 2:
                        wait_filled(pool, (*ssd_before(ssd_before(s)), "w"))
                    tt(v8(xw[m % 2]), v8(xdt[m % 2]), per_head(dec[:, 1, c, heads]), ALU.mult).then_inc(S["ssd_xw"], 1)
                elif k == "ssd_y":
                    g, c = s[2:]
                    m = NT * (SG * p + g) + c
                    heads = slice(GH + HG * g, GH + HG * (g + 1))
                    per_head = lambda a: a.unsqueeze(2).broadcast_to([P, HG, SP])
                    v8 = lambda a: a.rearrange("p (h n) -> p h n", h=HG)
                    if m:
                        pool.wait_ge(S["ssd_ygated"], m)
                    tt(v8(xD), v8(xt[:, c, :]), per_head(row[:, p // 2, R_D + HG * g:R_D + HG * (g + 1)]), ALU.mult)\
                        .then_inc(S["ssd_xd"], 1)
                elif k == "ssd_norm":
                    n = SG * p + s[2]
                    pool.wait_ge(S["ssd_mean"], n + 1)
                    if n:
                        pool.wait_ge(S["ssd_mixed"], n)
                    tt(ssr[:], sss[:, NT:2 * NT], pw[:, 0:NT], ALU.pow).then_inc(S["ssd_rstd"], 1)
                elif k == "squares":
                    t = s[2]
                    n = NT * p + t
                    pool.wait_ge(S["f_squares"], n + 1)
                    chain(ts(fss[:, t:t + 1], fss[:, t:t + 1], 1.0 / D, EPS, ALU.mult, ALU.add))
                    if p:
                        pool.wait_ge(S["f_done"], n - NT + 1)
                    tt(frs[:, t:t + 1], fss[:, t:t + 1], pw[:, 0:1], ALU.pow).then_inc(S["f_rstd"], 1)
                elif k == "split":
                    n, j = len(PIECES) * p + s[2], s[3]
                    pool.wait_ge(S["w_hi_ready"], 4 * n + j + 1)
                    at = (slice(None), n % W_RING, slice(j * 512, (j + 1) * 512))
                    tt(w_lo[at], wr[at], w_hi[at], ALU.subtract)\
                        .then_inc(S["w_lo_ready"], 1)
                elif k == "split_small":
                    pool.wait_ge(S["wsm_hi_ready"], p + 1)
                    w, lo, hi = wsm_parts(p)
                    tt(lo, w, hi, ALU.subtract).then_inc(S["wsm_lo_ready"], 1)


def kernel(**inputs):
    import concourse.bacc as bacc
    from concourse.bass_utils import run_bass_kernel_spmd

    f = {k: np.asarray(v) for k, v in inputs.items()}
    w, wo = f["w_in"], f["w_out"]
    at = np.cumsum([0, 512, 512, 512, 512, 4, 4, 1024, 256, 256, 1024, 16, 512, 512, 512, 512])
    gq, gk, gv, gz, gb, ga, sx, sB, sC, sz, sdt, rq, rk, rv, rg = [w[:, :, a:b] for a, b in zip(at[:-1], at[1:])]
    h128 = lambda a, h: a[:, :, h * P:(h + 1) * P]
    heads = [t for h in range(GH) for t in (h128(gq, h), h128(gk, h), h128(gv, h))]
    cols = [gz[:, :, :PC]] + heads[:8] + [gz[:, :, PC:]] + heads[8:] + [sB, sC]
    for g in range(SG):
        cols += [sx[:, :, g * 512:(g + 1) * 512], sz[:, :, g * 512:(g + 1) * 512]]
    cols += [t for h in range(RH) for t in (h128(rq, h), h128(rk, h), h128(rv, h), h128(rg, h))]
    wl = np.concatenate(cols, axis=2)
    n_pc = len(PIECES)
    wl = wl.reshape(DEPTH, KD, P, n_pc, PC).transpose(0, 3, 2, 1, 4).reshape(DEPTH, n_pc, P, KD * PC)
    ws = np.concatenate([gb, ga, sdt], axis=2).reshape(DEPTH, KD, P, NSM).transpose(0, 2, 1, 3)
    wol = wo.reshape(DEPTH, GROUPS, 4, P, UNITS, PC).transpose(0, 1, 4, 3, 2, 5).reshape(DEPTH, GROUPS, UNITS, P, 4 * PC)
    pars = np.zeros((DEPTH, P, Q_END), np.float32)
    gc, scv = f["gdn_conv"], f["ssd_conv"]
    tiles = [gc[:, :, j * 512 + h * P:j * 512 + (h + 1) * P] for h in range(GH) for j in range(3)]
    tiles += [scv[:, :, 1024 + j * P:1024 + (j + 1) * P] for j in range(4)] + [scv[:, :, j * P:(j + 1) * P] for j in range(8)]
    bias = f["ssd_conv_b"]
    bts = [bias[:, 1024 + j * P:1024 + (j + 1) * P] for j in range(4)] + [bias[:, j * P:(j + 1) * P] for j in range(8)]
    for m, t in enumerate(tiles):
        pars[:, :, Q_CONV + TAPS * m:Q_CONV + TAPS * (m + 1)] = t.transpose(0, 2, 1)
    for m, t in enumerate(bts):
        pars[:, :, Q_BIAS + m] = t
    pars[:, :, Q_PRE:Q_PRE + KD] = f["pre_norm"].reshape(DEPTH, KD, P).transpose(0, 2, 1)
    pars[:, :, Q_MIX:Q_MIX + 4] = f["gdn_norm"][:, :, None]
    pars[:, :, Q_MIX + 4:Q_MIX + 12] = f["ssd_norm"].reshape(DEPTH, 8, P).transpose(0, 2, 1)
    pars[:, :, Q_MIX + 12:Q_MIX + 16] = f["ret_norm"][:, :, None]
    rows = np.concatenate([f["gdn_A_log"], f["ssd_A_log"], f["gdn_dt_bias"], f["ssd_dt_bias"], f["ssd_D"]], axis=1)
    cons, rope = constants()

    nc = bacc.Bacc("TRN2", target_bir_lowering=False, num_devices=1)
    arrays = {"x": f["x"].reshape(SEQ, D), "w_in": wl, "w_small": ws, "w_out": wol, "cons": cons, "rope": rope, "pars": pars, "rows": rows,
              "post": f["post_norm"]}
    arrays = {f"in_{k}": np.ascontiguousarray(v) for k, v in arrays.items()}
    args = [nc.dram_tensor(k, v.shape, mybir.dt.from_np(v.dtype), kind="ExternalInput").ap() for k, v in arrays.items()]
    out = nc.dram_tensor("out_0", (SEQ, D), F32, kind="ExternalOutput").ap()
    hybrid_kernel(nc, *args, out)
    r = run_bass_kernel_spmd(nc, [arrays], core_ids=[0])
    return r.results[0]["out_0"].reshape(1, SEQ, D)
```
